# Optimizing a Trainium2 kernel written in Bass

```python
import jax, jax.numpy as jnp
from jax import lax
import numpy as np
import math

D_MODEL = 1024
BATCH = 1
SEQ = 256
DEPTH = 2

D_FF = 2816
GDN_HEADS = 8
GDN_DK = 128
GDN_DV = 128
GDN_CONV = 4
CHUNK = 64
CNV_CH = 1024
CNV_K = 31
W_Q = GDN_HEADS * GDN_DK
W_K = GDN_HEADS * GDN_DK
W_V = GDN_HEADS * GDN_DV
W_Z = GDN_HEADS * GDN_DV
W_BETA = GDN_HEADS
W_A = GDN_HEADS
W_GLU = 2 * CNV_CH
W_GATE = 2 * D_MODEL
SPLITS = [int(s) for s in np.cumsum([W_Q + W_K + W_V, W_Z, W_BETA, W_A, W_GLU])]
P_IN = W_Q + W_K + W_V + W_Z + W_BETA + W_A + W_GLU + W_GATE
RMS_EPS = 1e-6
LN_EPS = 1e-5


def rmsnorm(x, w):
    xf = x.astype(jnp.float32)
    y = xf * lax.rsqrt(jnp.mean(xf * xf, axis=-1, keepdims=True) + RMS_EPS)
    return (y * w.astype(jnp.float32)).astype(x.dtype)

def layernorm(x, g, b):
    xf = x.astype(jnp.float32)
    mu = jnp.mean(xf, axis=-1, keepdims=True)
    var = jnp.mean(jnp.square(xf - mu), axis=-1, keepdims=True)
    y = (xf - mu) * lax.rsqrt(var + LN_EPS)
    return (y * g.astype(jnp.float32) + b.astype(jnp.float32)).astype(x.dtype)

def l2norm(x):
    return x * lax.rsqrt(jnp.sum(x * x, axis=-1, keepdims=True) + 1e-6)

def causal_dwconv(x, w):
    k, c = w.shape
    return lax.conv_general_dilated(
        x, w[:, None, :].astype(x.dtype), window_strides=(1,), padding=[(k - 1, 0)],
        dimension_numbers=("NWC", "WIO", "NWC"), feature_group_count=c)

def swiglu_ffn(h, w_in, w_out):
    gate, up = jnp.split(h @ w_in, 2, axis=-1)
    return (jax.nn.silu(gate) * up) @ w_out

def chunk_gated_delta_rule(q, k, v, g, beta):
    b, l, h, dk = q.shape
    dv = v.shape[-1]
    n = l // CHUNK

    def to_chunks(t):
        return t.reshape(b, n, CHUNK, h, -1).transpose(0, 3, 1, 2, 4)

    q, k, v = to_chunks(q), to_chunks(k), to_chunks(v)
    g = g.reshape(b, n, CHUNK, h).transpose(0, 3, 1, 2)
    beta = beta.reshape(b, n, CHUNK, h).transpose(0, 3, 1, 2)
    G = jnp.cumsum(g, axis=-1)
    causal = jnp.tril(jnp.ones((CHUNK, CHUNK), dtype=bool))
    strict = jnp.tril(jnp.ones((CHUNK, CHUNK), dtype=bool), k=-1)
    diff = G[..., :, None] - G[..., None, :]
    decay = jnp.where(causal, jnp.exp(jnp.where(causal, diff, 0.0)), 0.0)
    kk = jnp.einsum("bhncd,bhnsd->bhncs", k, k)
    a_mat = jnp.where(strict, kk * decay * beta[..., :, None], 0.0)
    lhs = jnp.eye(CHUNK, dtype=jnp.float32) + a_mat
    rhs = jnp.concatenate([v * beta[..., None], k * (beta * jnp.exp(G))[..., None]], axis=-1)
    sol = lax.linalg.triangular_solve(lhs, rhs, left_side=True, lower=True, unit_diagonal=True)
    u, w = sol[..., :dv], sol[..., dv:]
    qk = jnp.einsum("bhncd,bhnsd->bhncs", q, k) * decay
    q_dec = q * jnp.exp(G)[..., None]
    k_dec = k * jnp.exp(G[..., -1:] - G)[..., None]
    chunk_decay = jnp.exp(G[..., -1])

    xs = tuple(jnp.moveaxis(t, 2, 0) for t in (q_dec, k_dec, u, w, qk, chunk_decay))

    def step(state, inp):
        q_c, k_c, u_c, w_c, qk_c, d_c = inp
        v_new = u_c - jnp.einsum("bhck,bhkv->bhcv", w_c, state)
        o_c = jnp.einsum("bhck,bhkv->bhcv", q_c, state) + jnp.einsum("bhcs,bhsv->bhcv", qk_c, v_new)
        state = state * d_c[..., None, None] + jnp.einsum("bhck,bhcv->bhkv", k_c, v_new)
        return state, o_c

    s0 = jnp.zeros((b, h, dk, dv), jnp.float32)
    _, o = lax.scan(step, s0, xs)
    return o.transpose(1, 0, 3, 2, 4).reshape(b, l, h, dv)

def gated_deltanet(qkv, z, beta_logit, a_logit, conv_w, a_log, dt_bias, norm_w, w_o):
    b, l, _ = qkv.shape
    qkv = jax.nn.silu(causal_dwconv(qkv, conv_w))
    q, k, v = jnp.split(qkv.astype(jnp.float32), [W_Q, W_Q + W_K], axis=-1)
    q = l2norm(q.reshape(b, l, GDN_HEADS, GDN_DK)) * (GDN_DK ** -0.5)
    k = l2norm(k.reshape(b, l, GDN_HEADS, GDN_DK))
    v = v.reshape(b, l, GDN_HEADS, GDN_DV)
    beta = jax.nn.sigmoid(beta_logit.astype(jnp.float32))
    g = -jnp.exp(a_log.astype(jnp.float32)) * jax.nn.softplus(
        a_logit.astype(jnp.float32) + dt_bias.astype(jnp.float32))
    o = chunk_gated_delta_rule(q, k, v, g, beta)
    zf = z.astype(jnp.float32).reshape(b, l, GDN_HEADS, GDN_DV)
    o = rmsnorm(o, norm_w) * jax.nn.silu(zf)
    return o.reshape(b, l, GDN_HEADS * GDN_DV).astype(qkv.dtype) @ w_o

def conformer_conv(glu_in, pw1_b, dw_w, dw_b, ln_g, ln_b, w_o, b_o):
    a, gate = jnp.split(glu_in + pw1_b, 2, axis=-1)
    h = a * jax.nn.sigmoid(gate)
    h = causal_dwconv(h, dw_w) + dw_b
    h = jax.nn.silu(layernorm(h, ln_g, ln_b))
    return h @ w_o + b_o

def first_inputs(seed: int = 0) -> dict:
    key = jax.random.key(seed)
    ks = iter(jax.random.split(key, 40))

    def nrm(shape, scale):
        return jax.random.normal(next(ks), shape, jnp.float32) * scale

    def gain(shape):
        return 1.0 + 0.02 * jax.random.normal(next(ks), shape, jnp.float32)

    L = DEPTH
    inp = {}
    inp["x"] = nrm((BATCH, SEQ, D_MODEL), 1.0)
    inp["ffn1_norm_pre"] = gain((L, D_MODEL))
    inp["ffn1_norm_post"] = gain((L, D_MODEL))
    inp["ffn1_w_in"] = nrm((L, D_MODEL, 2 * D_FF), D_MODEL ** -0.5)
    inp["ffn1_w_out"] = nrm((L, D_FF, D_MODEL), D_FF ** -0.5)
    inp["mix_norm_pre"] = gain((L, D_MODEL))
    inp["mix_norm_post"] = gain((L, D_MODEL))
    inp["mix_w_in"] = nrm((L, D_MODEL, P_IN), D_MODEL ** -0.5)
    inp["gdn_conv_w"] = nrm((L, GDN_CONV, W_Q + W_K + W_V), GDN_CONV ** -0.5)
    inp["gdn_a_log"] = jnp.log(jax.random.uniform(next(ks), (L, GDN_HEADS), jnp.float32, 1.0, 16.0))
    dt = jnp.exp(jax.random.uniform(next(ks), (L, GDN_HEADS), jnp.float32, np.log(1e-3), np.log(1e-1)))
    inp["gdn_dt_bias"] = dt + jnp.log(-jnp.expm1(-dt))
    inp["gdn_norm_w"] = gain((L, GDN_DV))
    inp["gdn_w_o"] = nrm((L, GDN_HEADS * GDN_DV, D_MODEL), (GDN_HEADS * GDN_DV) ** -0.5)
    inp["cnv_pw1_b"] = nrm((L, W_GLU), 0.02)
    inp["cnv_dw_w"] = nrm((L, CNV_K, CNV_CH), CNV_K ** -0.5)
    inp["cnv_dw_b"] = nrm((L, CNV_CH), 0.02)
    inp["cnv_ln_g"] = gain((L, CNV_CH))
    inp["cnv_ln_b"] = nrm((L, CNV_CH), 0.02)
    inp["cnv_w_o"] = nrm((L, CNV_CH, D_MODEL), CNV_CH ** -0.5)
    inp["cnv_b_o"] = nrm((L, D_MODEL), 0.02)
    inp["mix_w_out"] = nrm((L, D_MODEL, D_MODEL), D_MODEL ** -0.5)
    inp["ffn2_norm_pre"] = gain((L, D_MODEL))
    inp["ffn2_norm_post"] = gain((L, D_MODEL))
    inp["ffn2_w_in"] = nrm((L, D_MODEL, 2 * D_FF), D_MODEL ** -0.5)
    inp["ffn2_w_out"] = nrm((L, D_FF, D_MODEL), D_FF ** -0.5)
    return inp

def first_block(x, ffn1_norm_pre, ffn1_norm_post, ffn1_w_in, ffn1_w_out,
              mix_norm_pre, mix_norm_post, mix_w_in,
              gdn_conv_w, gdn_a_log, gdn_dt_bias, gdn_norm_w, gdn_w_o,
              cnv_pw1_b, cnv_dw_w, cnv_dw_b, cnv_ln_g, cnv_ln_b, cnv_w_o, cnv_b_o,
              mix_w_out,
              ffn2_norm_pre, ffn2_norm_post, ffn2_w_in, ffn2_w_out):
    for i in range(DEPTH):
        f = swiglu_ffn(rmsnorm(x, ffn1_norm_pre[i]), ffn1_w_in[i], ffn1_w_out[i])
        x = x + 0.5 * rmsnorm(f, ffn1_norm_post[i])

        h = rmsnorm(x, mix_norm_pre[i])
        p = h @ mix_w_in[i]
        qkv, z, beta_logit, a_logit, glu_in, gates = jnp.split(p, SPLITS, axis=-1)
        y_a = gated_deltanet(qkv, z, beta_logit, a_logit, gdn_conv_w[i], gdn_a_log[i],
                             gdn_dt_bias[i], gdn_norm_w[i], gdn_w_o[i])
        y_b = conformer_conv(glu_in, cnv_pw1_b[i], cnv_dw_w[i], cnv_dw_b[i],
                             cnv_ln_g[i], cnv_ln_b[i], cnv_w_o[i], cnv_b_o[i])
        g_a, g_b = jnp.split(jax.nn.sigmoid(gates), 2, axis=-1)
        y = (g_a * y_a + g_b * y_b) @ mix_w_out[i]
        x = x + rmsnorm(y, mix_norm_post[i])

        f = swiglu_ffn(rmsnorm(x, ffn2_norm_pre[i]), ffn2_w_in[i], ffn2_w_out[i])
        x = x + 0.5 * rmsnorm(f, ffn2_norm_post[i])
    return x


DEPTH_2 = 1

MLSTM_HEADS = 4
MLSTM_HEAD_DIM = 256
MLSTM_WIDTH = MLSTM_HEADS * MLSTM_HEAD_DIM
MLSTM_CHUNK = 128
N_GATE_COLS = 4 * MLSTM_HEADS
LRU_WIDTH = D_MODEL
LRU_BLOCKS = 8
LRU_BLOCK_DIM = LRU_WIDTH // LRU_BLOCKS
LRU_C = 8.0
CONV_WIDTH = 4
CONV_PAD = (2, 1)
PEER_HEADS = 8
PEER_N_KEYS = 128
PEER_N_EXPERTS = PEER_N_KEYS * PEER_N_KEYS
PEER_QUERY_DIM = 256
PEER_HALF = PEER_QUERY_DIM // 2
PEER_TOPK = 16
PEER_TOKEN_BLOCK = 128
EPS = 1e-6

IN_SPLIT_SIZES = (MLSTM_WIDTH, MLSTM_WIDTH, N_GATE_COLS, LRU_WIDTH, LRU_WIDTH, 2 * D_MODEL)
D_IN = MLSTM_WIDTH * 2 + N_GATE_COLS + LRU_WIDTH * 2 + 2 * D_MODEL


def rms_norm(x, g):
    x32 = x.astype(jnp.float32)
    y = x32 * lax.rsqrt(jnp.mean(x32 * x32, axis=-1, keepdims=True) + EPS)
    return (y * g.astype(jnp.float32)).astype(x.dtype)

def dwconv_centred(x, w, b):
    y = lax.conv_general_dilated(
        x, w[:, None, :].astype(x.dtype), window_strides=(1,), padding=[CONV_PAD],
        dimension_numbers=("NWC", "WIO", "NWC"), feature_group_count=x.shape[-1])
    return y + b.astype(x.dtype)

def mlstm_scan(q, k, v, log_i, log_f):
    B, H, S, d = q.shape
    nc = S // MLSTM_CHUNK

    def to_chunks(t):
        return jnp.moveaxis(t.reshape((B, H, nc, MLSTM_CHUNK) + t.shape[3:]), 2, 0)

    tril = jnp.tril(jnp.ones((MLSTM_CHUNK, MLSTM_CHUNK), dtype=bool))

    def body(carry, xs):
        C, n, m = carry
        qc, kc, vc, ic, fc = xs
        b = jnp.cumsum(fc, axis=-1)
        d_log = jnp.where(tril, b[..., :, None] - b[..., None, :] + ic[..., None, :], -jnp.inf)
        inter = b + m[..., None]
        m_t = jnp.maximum(inter, jnp.max(d_log, axis=-1))
        w_intra = jnp.exp(d_log - m_t[..., None])
        w_inter = jnp.exp(inter - m_t)
        s = jnp.einsum("bhtd,bhsd->bhts", qc, kc) * w_intra
        num = w_inter[..., None] * jnp.einsum("bhtd,bhde->bhte", qc, C) + jnp.einsum("bhts,bhse->bhte", s, vc)
        den = w_inter * jnp.einsum("bhtd,bhd->bht", qc, n) + jnp.sum(s, axis=-1)
        h = num / jnp.maximum(jnp.abs(den), jnp.exp(-m_t))[..., None]
        g = b[..., -1]
        w_log = g[..., None] - b + ic
        m_new = jnp.maximum(g + m, jnp.max(w_log, axis=-1))
        decay = jnp.exp(g + m - m_new)
        w_state = jnp.exp(w_log - m_new[..., None])
        kw = kc * w_state[..., None]
        C_new = decay[..., None, None] * C + jnp.einsum("bhsd,bhse->bhde", kw, vc)
        n_new = decay[..., None] * n + jnp.sum(kw, axis=2)
        return (C_new, n_new, m_new), h

    init = (jnp.zeros((B, H, d, d), jnp.float32), jnp.zeros((B, H, d), jnp.float32),
            jnp.zeros((B, H), jnp.float32))
    _, h = lax.scan(body, init, (to_chunks(q), to_chunks(k), to_chunks(v), to_chunks(log_i), to_chunks(log_f)))
    return jnp.moveaxis(h, 0, 2).reshape(B, H, S, d)

def mlstm_branch(xm, o_pre, gate_pre, conv_w, conv_b, w_q, w_k, w_v, norm_g):
    B, S, _ = xm.shape
    H, d = MLSTM_HEADS, MLSTM_HEAD_DIM
    xc = jax.nn.silu(dwconv_centred(xm, conv_w, conv_b)).reshape(B, S, H, d)
    xv = xm.reshape(B, S, H, d)
    q = jnp.einsum("bshd,hde->bhse", xc, w_q).astype(jnp.float32)
    k = (jnp.einsum("bshd,hde->bhse", xc, w_k) / math.sqrt(d)).astype(jnp.float32)
    v = jnp.einsum("bshd,hde->bhse", xv, w_v).astype(jnp.float32)
    gates = gate_pre.astype(jnp.float32).reshape(B, S, 4, H).transpose(2, 0, 3, 1)
    i_f, f_f, i_b, f_b = gates[0], gates[1], gates[2], gates[3]
    flip = lambda t: jnp.flip(t, axis=2)
    h_fwd = mlstm_scan(q, k, v, i_f, jax.nn.log_sigmoid(f_f))
    h_bwd = flip(mlstm_scan(flip(q), flip(k), flip(v), flip(i_b), flip(jax.nn.log_sigmoid(f_b))))
    h = jnp.transpose(h_fwd + h_bwd, (0, 2, 1, 3))
    h = rms_norm(h, norm_g.reshape(H, d)).reshape(B, S, MLSTM_WIDTH)
    return (jax.nn.sigmoid(o_pre.astype(jnp.float32)) * h.astype(jnp.float32)).astype(xm.dtype)

def rglru_dir(x, w_r, b_r, w_i, b_i, lam):
    B, S, C = x.shape
    xb = x.reshape(B, S, LRU_BLOCKS, LRU_BLOCK_DIM)
    r = jax.nn.sigmoid(jnp.einsum("bsnc,ncd->bsnd", xb, w_r).reshape(B, S, C) + b_r)
    i = jax.nn.sigmoid(jnp.einsum("bsnc,ncd->bsnd", xb, w_i).reshape(B, S, C) + b_i)
    log_a = -LRU_C * r * jax.nn.softplus(-lam)
    a = jnp.exp(log_a)
    u = jnp.sqrt(-jnp.expm1(2.0 * log_a)) * (i * x)

    def combine(left, right):
        a1, b1 = left
        a2, b2 = right
        return a1 * a2, a2 * b1 + b2

    _, h = lax.associative_scan(combine, (a, u), axis=1)
    return h

def lru_branch(xl, gate_pre, conv_w, conv_b, w_r, b_r, w_i, b_i, lam):
    xc = dwconv_centred(xl, conv_w, conv_b).astype(jnp.float32)
    w_r, b_r, w_i, b_i, lam = (t.astype(jnp.float32) for t in (w_r, b_r, w_i, b_i, lam))
    h_fwd = rglru_dir(xc, w_r[0], b_r[0], w_i[0], b_i[0], lam[0])
    h_bwd = jnp.flip(rglru_dir(jnp.flip(xc, axis=1), w_r[1], b_r[1], w_i[1], b_i[1], lam[1]), axis=1)
    y = (h_fwd + h_bwd) * jax.nn.gelu(gate_pre.astype(jnp.float32), approximate=False)
    return y.astype(xl.dtype)

def peer(h, w_q, sub_keys, expert_u, expert_v):
    B, S, D = h.shape
    nb = (B * S) // PEER_TOKEN_BLOCK
    keys32 = sub_keys.astype(jnp.float32)

    def block_fn(hb):
        tb = hb.shape[0]
        q = jnp.einsum("td,de->te", hb, w_q).astype(jnp.float32).reshape(tb, PEER_HEADS, 2, PEER_HALF)
        scores = jnp.einsum("thpc,hpnc->thpn", q, keys32)
        s_top, i_top = lax.top_k(scores, PEER_TOPK)
        cand = (s_top[:, :, 0, :, None] + s_top[:, :, 1, None, :]).reshape(tb, PEER_HEADS, PEER_TOPK * PEER_TOPK)
        cand_idx = (i_top[:, :, 0, :, None] * PEER_N_KEYS + i_top[:, :, 1, None, :]).reshape(tb, PEER_HEADS, PEER_TOPK * PEER_TOPK)
        best, pos = lax.top_k(cand, PEER_TOPK)
        idx = jnp.take_along_axis(cand_idx, pos, axis=-1).reshape(tb, PEER_HEADS * PEER_TOPK)
        gate = jax.nn.softmax(best, axis=-1).reshape(tb, PEER_HEADS * PEER_TOPK)
        u = jnp.take(expert_u, idx, axis=0)
        act = jax.nn.gelu(jnp.einsum("tkd,td->tk", u, hb).astype(jnp.float32), approximate=False)
        vv = jnp.take(expert_v, idx, axis=0)
        return jnp.einsum("tk,tkd->td", (gate * act).astype(hb.dtype), vv)

    out = lax.map(block_fn, h.reshape(nb, PEER_TOKEN_BLOCK, D))
    return out.reshape(B, S, D)

def second_inputs(seed: int = 0) -> dict:
    key = jax.random.key(seed)
    ks = jax.random.split(key, 32)
    nrm = lambda k, shape, scale: jax.random.normal(k, shape, jnp.float32) * scale
    L = DEPTH_2
    f_base = jnp.linspace(3.0, 6.0, MLSTM_HEADS)
    z = jnp.zeros((MLSTM_HEADS,), jnp.float32)
    gate_base = jnp.stack([z, f_base, z, f_base])
    b_gates = (gate_base[None] + nrm(ks[3], (L, 4, MLSTM_HEADS), 0.1)).reshape(L, N_GATE_COLS)
    a0 = jax.random.uniform(ks[16], (L, 2, LRU_WIDTH), jnp.float32, 0.9, 0.999) ** (1.0 / LRU_C)
    lru_lambda = jnp.log(a0) - jnp.log1p(-a0)
    return {
        "x": nrm(ks[0], (BATCH, SEQ, D_MODEL), 1.0),
        "norm1_g": 1.0 + nrm(ks[1], (L, D_MODEL), 0.02),
        "w_in": nrm(ks[2], (L, D_MODEL, D_IN), D_MODEL ** -0.5),
        "b_gates": b_gates,
        "mlstm_conv_w": nrm(ks[4], (L, CONV_WIDTH, MLSTM_WIDTH), CONV_WIDTH ** -0.5),
        "mlstm_conv_b": nrm(ks[5], (L, MLSTM_WIDTH), 0.02),
        "mlstm_w_q": nrm(ks[6], (L, MLSTM_HEADS, MLSTM_HEAD_DIM, MLSTM_HEAD_DIM), MLSTM_HEAD_DIM ** -0.5),
        "mlstm_w_k": nrm(ks[7], (L, MLSTM_HEADS, MLSTM_HEAD_DIM, MLSTM_HEAD_DIM), MLSTM_HEAD_DIM ** -0.5),
        "mlstm_w_v": nrm(ks[8], (L, MLSTM_HEADS, MLSTM_HEAD_DIM, MLSTM_HEAD_DIM), MLSTM_HEAD_DIM ** -0.5),
        "mlstm_norm_g": 1.0 + nrm(ks[9], (L, MLSTM_WIDTH), 0.02),
        "lru_conv_w": nrm(ks[10], (L, CONV_WIDTH, LRU_WIDTH), CONV_WIDTH ** -0.5),
        "lru_conv_b": nrm(ks[11], (L, LRU_WIDTH), 0.02),
        "lru_w_r": nrm(ks[12], (L, 2, LRU_BLOCKS, LRU_BLOCK_DIM, LRU_BLOCK_DIM), LRU_BLOCK_DIM ** -0.5),
        "lru_b_r": nrm(ks[13], (L, 2, LRU_WIDTH), 0.02),
        "lru_w_i": nrm(ks[14], (L, 2, LRU_BLOCKS, LRU_BLOCK_DIM, LRU_BLOCK_DIM), LRU_BLOCK_DIM ** -0.5),
        "lru_b_i": nrm(ks[15], (L, 2, LRU_WIDTH), 0.02),
        "lru_lambda": lru_lambda,
        "w_branch_mlstm": nrm(ks[17], (L, MLSTM_WIDTH, D_MODEL), MLSTM_WIDTH ** -0.5),
        "w_branch_lru": nrm(ks[18], (L, LRU_WIDTH, D_MODEL), LRU_WIDTH ** -0.5),
        "w_out": nrm(ks[19], (L, D_MODEL, D_MODEL), D_MODEL ** -0.5),
        "norm2_g": 1.0 + nrm(ks[20], (L, D_MODEL), 0.02),
        "peer_w_q": nrm(ks[21], (L, D_MODEL, PEER_HEADS * PEER_QUERY_DIM), D_MODEL ** -0.5),
        "peer_sub_keys": nrm(ks[22], (L, PEER_HEADS, 2, PEER_N_KEYS, PEER_HALF), PEER_HALF ** -0.5),
        "peer_u": nrm(ks[23], (L, PEER_N_EXPERTS, D_MODEL), D_MODEL ** -0.5),
        "peer_v": nrm(ks[24], (L, PEER_N_EXPERTS, D_MODEL), PEER_HEADS ** -0.5),
        "final_norm_g": 1.0 + nrm(ks[25], (D_MODEL,), 0.02),
    }

def second_block(x, norm1_g, w_in, b_gates, mlstm_conv_w, mlstm_conv_b, mlstm_w_q, mlstm_w_k, mlstm_w_v,
              mlstm_norm_g, lru_conv_w, lru_conv_b, lru_w_r, lru_b_r, lru_w_i, lru_b_i, lru_lambda,
              w_branch_mlstm, w_branch_lru, w_out, norm2_g, peer_w_q, peer_sub_keys, peer_u, peer_v,
              final_norm_g):
    split_points = np.cumsum(IN_SPLIT_SIZES)[:-1].tolist()
    for l in range(DEPTH_2):
        h = rms_norm(x, norm1_g[l])
        proj = jnp.einsum("bsd,de->bse", h, w_in[l])
        xm, o_pre, gate_pre, xl, lru_gate, merge_pre = jnp.split(proj, split_points, axis=-1)
        gate_pre = gate_pre + b_gates[l].astype(gate_pre.dtype)
        y_m = mlstm_branch(xm, o_pre, gate_pre, mlstm_conv_w[l], mlstm_conv_b[l], mlstm_w_q[l],
                           mlstm_w_k[l], mlstm_w_v[l], mlstm_norm_g[l])
        y_l = lru_branch(xl, lru_gate, lru_conv_w[l], lru_conv_b[l], lru_w_r[l], lru_b_r[l],
                         lru_w_i[l], lru_b_i[l], lru_lambda[l])
        g_m, g_l = jnp.split(jax.nn.sigmoid(merge_pre), 2, axis=-1)
        merged = (g_m * jnp.einsum("bsc,cd->bsd", y_m, w_branch_mlstm[l])
                  + g_l * jnp.einsum("bsc,cd->bsd", y_l, w_branch_lru[l]))
        x = x + jnp.einsum("bsd,de->bse", merged, w_out[l])
        h2 = rms_norm(x, norm2_g[l])
        x = x + peer(h2, peer_w_q[l], peer_sub_keys[l], peer_u[l], peer_v[l])
    return rms_norm(x, final_norm_g)


def setup_inputs(seed=0):
    out = dict(first_inputs(seed))
    for name, value in second_inputs(seed + 1).items():
        if name != "x":
            out[name + "_2"] = value
    return out


def reference(
    x, ffn1_norm_pre, ffn1_norm_post, ffn1_w_in, ffn1_w_out, mix_norm_pre, mix_norm_post,
    mix_w_in, gdn_conv_w, gdn_a_log, gdn_dt_bias, gdn_norm_w, gdn_w_o, cnv_pw1_b, cnv_dw_w,
    cnv_dw_b, cnv_ln_g, cnv_ln_b, cnv_w_o, cnv_b_o, mix_w_out, ffn2_norm_pre, ffn2_norm_post,
    ffn2_w_in, ffn2_w_out, norm1_g_2, w_in_2, b_gates_2, mlstm_conv_w_2, mlstm_conv_b_2,
    mlstm_w_q_2, mlstm_w_k_2, mlstm_w_v_2, mlstm_norm_g_2, lru_conv_w_2, lru_conv_b_2,
    lru_w_r_2, lru_b_r_2, lru_w_i_2, lru_b_i_2, lru_lambda_2, w_branch_mlstm_2, w_branch_lru_2,
    w_out_2, norm2_g_2, peer_w_q_2, peer_sub_keys_2, peer_u_2, peer_v_2, final_norm_g_2,
):
    x = first_block(
        x, ffn1_norm_pre, ffn1_norm_post, ffn1_w_in, ffn1_w_out, mix_norm_pre, mix_norm_post,
        mix_w_in, gdn_conv_w, gdn_a_log, gdn_dt_bias, gdn_norm_w, gdn_w_o, cnv_pw1_b, cnv_dw_w,
        cnv_dw_b, cnv_ln_g, cnv_ln_b, cnv_w_o, cnv_b_o, mix_w_out, ffn2_norm_pre,
        ffn2_norm_post, ffn2_w_in, ffn2_w_out,
    )
    return second_block(
        x, norm1_g_2, w_in_2, b_gates_2, mlstm_conv_w_2, mlstm_conv_b_2, mlstm_w_q_2,
        mlstm_w_k_2, mlstm_w_v_2, mlstm_norm_g_2, lru_conv_w_2, lru_conv_b_2, lru_w_r_2,
        lru_b_r_2, lru_w_i_2, lru_b_i_2, lru_lambda_2, w_branch_mlstm_2, w_branch_lru_2,
        w_out_2, norm2_g_2, peer_w_q_2, peer_sub_keys_2, peer_u_2, peer_v_2, final_norm_g_2,
    )


_drawn_inputs = setup_inputs


def setup_inputs(seed=0):
    import zlib

    import numpy as np

    out = dict(_drawn_inputs(seed))
    spreads = {}
    factors = {'ffn1_norm_post': 2.688,
     'gdn_norm_w': 2.934,
     'ffn2_norm_pre': 3.137,
     'ffn2_norm_post': 4.137,
     'norm1_g_2': 3.819,
     'mlstm_conv_b_2': 5.119,
     'mlstm_norm_g_2': 50.59,
     'lru_b_r_2': 22.921,
     'lru_b_i_2': 8.0,
     'norm2_g_2': 22.379,
     'final_norm_g_2': 7.942}
    for name, (base, spread) in spreads.items():
        noise = np.random.default_rng([zlib.crc32(name.encode()), seed]).standard_normal(out[name].shape)
        drawn = base * np.exp(spread * noise) if base else spread * noise
        out[name] = __import__('jax').numpy.asarray(drawn.astype(out[name].dtype))
    for name, factor in factors.items():
        out[name] = (out[name] * factor).astype(out[name].dtype)
    return out
```

```python
from contextlib import ExitStack, contextmanager

import numpy as np

import concourse.bass as bass
from concourse import mybir

F32 = mybir.dt.float32
I32 = mybir.dt.int32
U32 = mybir.dt.uint32
ALU = mybir.AluOpType
ACT = mybir.ActivationFunctionType
AX = mybir.AxisListType
P = 128
NT = 256
KT = 8
RMS_EPS, LN_EPS = 1e-6, 1e-5
LOWEST = -3.0e38


class Done:

    def __init__(self, sem, value):
        self.sem, self.value = sem, value


class Queue:

    def __init__(self, nc, eng, name):
        self.eng, self.sem, self.n, self.waited = eng, nc.alloc_semaphore(f"{name}_done"), 0, {}

    def wait(self, *dones):
        for d in dones:
            if d is None:
                continue
            if isinstance(d, (list, tuple)):
                self.wait(*d)
            elif self.waited.get(d.sem.num, 0) < d.value:
                self.eng.wait_ge(d.sem, d.value)
                self.waited[d.sem.num] = d.value

    def __call__(self, ins, *args, after=(), **kw):
        self.wait(*after)
        ins(*args, **kw).then_inc(self.sem, 1)
        self.n += 1
        return Done(self.sem, self.n)

    def reset(self):
        self.n, self.waited = 0, {}


class Count:

    def __init__(self, nc, name, unit=1):
        self.sem, self.unit, self.n, self.loop = nc.alloc_semaphore(name), unit, 0, None

    def by(self, ins):
        ins.then_inc(self.sem, self.unit)
        self.n += 1

    def wait(self, q, but=0):
        value = (self.n - but) * self.unit
        assert value > 0
        if self.loop is not None:
            reg, per = self.loop
            value = reg * (per * self.unit) + value
        q.eng.wait_ge(self.sem, value)

    def done(self):
        assert self.loop is None
        return Done(self.sem, self.n * self.unit)


@contextmanager
def rounds(nc, n, counts):
    start = {c: c.n for c in counts}
    with nc.Fori(0, n) as reg:
        for c, per in counts.items():
            c.loop = (reg, per)
        yield reg
        for c, per in counts.items():
            assert c.n == start[c] + per, (c.sem, c.n - start[c], per)
            c.loop = None
            c.n = start[c] + n * per


class Machine:

    SLOTS = 4

    def __init__(self, nc):
        self.nc = nc
        self.pe = Queue(nc, nc.tensor, "pe")
        self.act = Queue(nc, nc.scalar, "act")
        self.dve = Queue(nc, nc.vector, "dve")
        self.pool = Queue(nc, nc.gpsimd, "pool")
        self.sp = Queue(nc, nc.sync, "sp")
        self.queues = [self.pe, self.act, self.dve, self.pool, self.sp]
        S = self.SLOTS
        self.loaded = [Count(nc, f"weights_loaded{s}", 16) for s in range(S)]
        self.computed = [Count(nc, f"weights_used{s}") for s in range(S)]
        self.evicted = [Count(nc, f"bank_evicted{s}") for s in range(S)]
        self.params_in = Count(nc, "params_in", 16)
        self.misc_in = Count(nc, "misc_in", 16)
        self.counts = [*self.loaded, *self.computed, *self.evicted, self.params_in, self.misc_in]
        self.bank = [nc.alloc_psum_tensor(f"bank{b}", [P, 512], F32) for b in range(8)]
        self.read = [[] for _ in range(8)]
        self.slot = [nc.alloc_sbuf_tensor(f"wslot{s}", [P, KT, 256], F32) for s in range(S)]
        self.next_slot = 0

    def sb(self, name, shape, dt=F32):
        return self.nc.alloc_sbuf_tensor(name, shape, dt)

    def start_phase(self):
        for q in self.queues:
            q.reset()
        self.read = [[] for _ in range(8)]
        self.next_slot = 0
        for c in self.counts:
            c.n = 0
        for s in range(self.SLOTS):
            self.computed[s].by(self.prime(self.nc.tensor))
            self.evicted[s].by(self.prime(self.nc.scalar))

    @staticmethod
    def prime(eng):
        return eng.nop()

    def end_phase(self):
        sems = [q.sem.num for q in self.queues] + [c.sem.num for c in self.counts]
        assert sorted(sems) == list(range(min(sems), max(sems) + 1)), sems
        self.nc.all_engine_barrier(sems_to_clear=range(min(sems), max(sems) + 1))

    def matmuls(self, steps, after=(), bank=None):
        self.pe.wait(*after)
        if bank is not None:
            self.pe.wait(*self.read[bank])
        for out, lhsT, rhs, start, stop in steps[:-1]:
            self.nc.tensor.matmul(out, lhsT, rhs, start=start, stop=stop)
        out, lhsT, rhs, start, stop = steps[-1]
        return self.pe(self.nc.tensor.matmul, out, lhsT, rhs, start=start, stop=stop)

    def load_block(self, src, dst=None):
        s = self.next_slot
        self.next_slot = (s + 1) % self.SLOTS
        self.computed[s].wait(self.sp)
        self.loaded[s].by(self.nc.sync.dma_start(self.slot[s][:, :, :] if dst is None else dst(s), src))
        return s

    def block_products(self, s, x, after=()):
        self.loaded[s].wait(self.pe)
        self.evicted[s].wait(self.pe)
        self.pe.wait(*after)
        for m in range(2):
            for k in range(KT):
                ins = self.nc.tensor.matmul(self.bank[s][:, m * NT:(m + 1) * NT],
                                            self.slot[s][:, k, m * P:(m + 1) * P], x[:, k, :],
                                            start=(k == 0), stop=(k == KT - 1))
        self.computed[s].by(ins)

    def release(self, s, last):
        self.pe.wait(last)
        self.computed[s].by(self.prime(self.nc.tensor))

    def settle_banks(self):
        for s in range(self.SLOTS):
            self.pe.wait(*self.read[s])
            self.read[s] = []

    def streamed(self):
        for s in range(self.SLOTS):
            self.read[s] = [self.evicted[s].done()]

    def project(self, x, block_src, n_blocks, dst, tile0, after=()):
        S = self.SLOTS
        self.settle_banks()
        self.pe.wait(*after)
        assert self.next_slot == 0 and n_blocks % S == 0

        def one_round(j):
            for b in range(S):
                s = self.load_block(block_src(j * S + b))
                self.block_products(s, x)
                self.computed[s].wait(self.act)
                at = tile0 + (j * S + b) * 2
                self.evicted[s].by(self.nc.scalar.copy(
                    dst[:, at:at + 2, :] if isinstance(at, int) else dst[:, bass.ds(at, 2), :],
                    self.bank[s][:, :].rearrange("p (a n) -> p a n", a=2)))

        n = n_blocks // S
        if n == 1:
            one_round(0)
        else:
            with rounds(self.nc, n, {c: 1 for c in [*self.loaded, *self.computed, *self.evicted]}) as j:
                one_round(j)
        self.streamed()
        return [self.evicted[s].done() for s in range(S)]

    def project_with(self, x, block_src, evict, after=()):
        self.settle_banks()
        self.pe.wait(*after)
        for b in range(4):
            s = self.load_block(block_src(b))
            self.block_products(s, x)
            evict(b, s)
        self.streamed()


def columns(w, layer, col):
    if not isinstance(col, int):
        cols = bass.ds(col, 256)
    else:
        cols = slice(col, col + 256)
    return w[bass.ds(layer, 1), :, cols].rearrange("o (k p) c -> p (o k) c", p=P)


def rms_norm(m, x, gain, out, tmp, stat, bank, eps=RMS_EPS, after=()):
    nc = m.nc
    squares = []
    for i in range(4):
        two = slice(2 * i, 2 * i + 2)
        squares.append(m.act(nc.scalar.square, tmp[:, two, :], x[:, two, :], after=after))
    for k in range(KT):
        m.pe.wait(squares[k // 2])
        if k == 0:
            m.pe.wait(*m.read[bank])
        ins = nc.tensor.matmul(m.bank[bank][:, 0:NT], m.ones[:, :], tmp[:, k, :], start=(k == 0), stop=(k == KT - 1))
    ins.then_inc(m.pe.sem, 1)
    m.pe.n += 1
    summed = Done(m.pe.sem, m.pe.n)
    mean = m.dve(nc.vector.tensor_scalar, stat, m.bank[bank][:, 0:NT], 1.0 / (KT * P), eps, ALU.mult, ALU.add, after=(summed,))
    m.read[bank] = [mean]
    inv = m.dve(nc.vector.reciprocal, stat, stat, after=(mean,))
    root = m.act(nc.scalar.activation, stat, stat, ACT.Sqrt, after=(inv,))
    dones = []
    for k in range(KT):
        dones.append(m.dve(nc.vector.scalar_tensor_tensor, out=out[:, k, :], in0=x[:, k, :], scalar=gain[:, k:k + 1],
                           in1=stat, op0=ALU.mult, op1=ALU.mult, after=(root,)))
    return dones


def add_normed(m, x, y, gain, tmp, stat, bank, after=()):
    nc = m.nc
    normed = rms_norm(m, y, gain, y, tmp, stat, bank, after=after)
    return m.dve(nc.vector.tensor_tensor, x[:, :, :], x[:, :, :], y[:, :, :], ALU.add, after=(normed[-1],))


def ffn(m, h, w_in, w_out, layer, d_ff, gated, silu, y, after=()):
    nc = m.nc
    n = d_ff // 256
    m.settle_banks()
    for b in range(4, 8):
        m.pe.wait(*m.read[b])
    m.pe.wait(*after)
    gate_s, up_s, out_s = 0, 1, 2
    bank2 = [m.bank[s][:, :].rearrange("p (a n) -> p a n", a=2) for s in range(2)]

    def gate(j):
        m.next_slot = gate_s
        m.load_block(columns(w_in, layer, j * 256))
        m.block_products(gate_s, h)
        m.computed[gate_s].wait(m.act)
        m.evicted[up_s].wait(m.act)
        m.evicted[gate_s].by(nc.scalar.activation(silu[:, :, :], bank2[gate_s], ACT.Silu))

    def up(j):
        m.next_slot = up_s
        m.load_block(columns(w_in, layer, j * 256 + d_ff))
        m.block_products(up_s, h)
        m.evicted[gate_s].wait(m.dve)
        m.computed[up_s].wait(m.dve)
        m.computed[out_s].wait(m.dve)
        m.evicted[up_s].by(nc.vector.tensor_tensor(gated[:, :, :], silu[:, :, :], bank2[up_s], ALU.mult))

    def out(j, first=False, last=False):
        m.next_slot = out_s
        rows = w_out[bass.ds(layer, 1), bass.ds(j * 256, 256), :].rearrange("o (k p) c -> p (o k) c", p=P)
        m.load_block(rows, lambda s: m.slot[s][:, :, :].rearrange("p (k q) c -> p k (q c)", k=2))
        w = m.slot[out_s][:, :, :].rearrange("p (k q) c -> p k (q c)", k=2)
        m.loaded[out_s].wait(m.pe)
        m.evicted[up_s].wait(m.pe)
        for k in range(2):
            for t in range(KT):
                ins = nc.tensor.matmul(m.bank[4 + t // 2][:, t % 2 * NT:(t % 2 + 1) * NT], w[:, k, t * P:(t + 1) * P],
                                       gated[:, k, :], start=(first and k == 0 and t % 2 == 0),
                                       stop=(last and k == 1), skip_group_check=True)
        m.computed[out_s].by(ins)

    gate(0)
    up(0)
    gate(1)
    out(0, first=True)
    up(1)
    with rounds(nc, n - 2, {m.loaded[0]: 1, m.loaded[1]: 1, m.loaded[2]: 1, m.computed[0]: 1, m.computed[1]: 1,
                            m.computed[2]: 1, m.evicted[0]: 1, m.evicted[1]: 1}) as j:
        gate(j + 2)
        out(j + 1)
        up(j + 2)
    out(n - 1, last=True)
    m.next_slot = 0
    m.streamed()
    dones = []
    for b in range(4):
        d = m.act(nc.scalar.copy, y[:, 2 * b:2 * b + 2, :], m.bank[4 + b][:, :].rearrange("p (a n) -> p a n", a=2),
                  after=(m.computed[out_s].done(),))
        m.read[4 + b] = [d]
        dones.append(d)
    return dones


def to_columns(m, rows, n_rows, cols, bank, after=()):
    nc = m.nc
    t = m.pe(nc.tensor.transpose, m.bank[bank][:, 0:n_rows], rows[0:n_rows, :], m.ident[0:n_rows, 0:n_rows],
             after=(*after, *m.read[bank]))
    d = m.dve(nc.vector.tensor_copy, cols, m.bank[bank][:, 0:n_rows], after=(t,))
    m.read[bank] = [d]
    return d


def softplus(m, x, out, a, b, after=()):
    nc = m.nc
    d = m.dve(nc.vector.scalar_tensor_tensor, out=a, in0=x, scalar=-1.0, in1=x, op0=ALU.mult, op1=ALU.max, after=after)
    e = m.act(nc.scalar.activation, a, a, ACT.Exp, scale=-1.0, after=(d,))
    d = m.dve(nc.vector.tensor_scalar, b, a, 2.0, None, ALU.add, after=(e,))
    d = m.dve(nc.vector.reciprocal, b, b, after=(d,))
    z = m.dve(nc.vector.tensor_tensor, a, a, b, ALU.mult, after=(d,))
    d = m.dve(nc.vector.tensor_tensor, b, a, a, ALU.mult, after=(z,))
    d = m.dve(nc.vector.tensor_scalar, out, b, 2.0 / 17, None, ALU.mult, after=(d,))
    for k in range(7, 0, -1):
        d = m.dve(nc.vector.scalar_tensor_tensor, out=out, in0=out, scalar=2.0 / (2 * k + 1), in1=b,
                  op0=ALU.add, op1=ALU.mult, after=(d,))
    d = m.dve(nc.vector.scalar_tensor_tensor, out=out, in0=out, scalar=2.0, in1=a, op0=ALU.add, op1=ALU.mult, after=(d,))
    return m.dve(nc.vector.scalar_tensor_tensor, out=out, in0=x, scalar=0.0, in1=out, op0=ALU.max, op1=ALU.add, after=(d,))


def make_constants(m):
    nc = m.nc
    m.ones = m.sb("ones", [P, P])
    m.ident = m.sb("ident", [P, P])
    m.upto = m.sb("mask_s_le_t", [P, P])
    m.from_ = m.sb("mask_s_ge_t", [P, P])
    m.level = m.sb("level_masks", [P, 7, P])
    m.onehot = m.sb("onehot_columns", [P, 16, 16])
    m.pick = m.sb("row_pickers", [16, 16, P])
    xor = m.slot[0][:, 0, 0:P].bitcast(I32)
    srow = m.slot[0][:, 0, P:2 * P].bitcast(I32)
    tmp = m.slot[0][:, 1, 0:P].bitcast(I32)
    ones = m.pool(nc.gpsimd.memset, m.ones[:, :], 1.0)
    big = m.pool(nc.gpsimd.memset, m.onehot[:, :, :], 1.0)
    big2 = m.pool(nc.gpsimd.memset, m.pick[:, :, :], 1.0)
    out = [
        m.pool(nc.gpsimd.affine_select, out=m.ident[:, :], in_=m.ones[:, :], compare_op=ALU.is_equal, fill=0.0,
               base=0, pattern=[[-1, P]], channel_multiplier=1, after=(ones,)),
        m.pool(nc.gpsimd.affine_select, out=m.upto[:, :], in_=m.ones[:, :], compare_op=ALU.is_ge, fill=0.0,
               base=0, pattern=[[1, P]], channel_multiplier=-1),
        m.pool(nc.gpsimd.affine_select, out=m.from_[:, :], in_=m.ones[:, :], compare_op=ALU.is_ge, fill=0.0,
               base=0, pattern=[[-1, P]], channel_multiplier=1),
        m.pool(nc.gpsimd.affine_select, out=m.onehot[:, :, :], in_=m.onehot[:, :, :], compare_op=ALU.is_equal, fill=0.0,
               base=0, pattern=[[1, 16], [-1, 16]], channel_multiplier=0, after=(big,)),
        m.pool(nc.gpsimd.affine_select, out=m.pick[:, :, :], in_=m.pick[:, :, :], compare_op=ALU.is_equal, fill=0.0,
               base=0, pattern=[[-1, 16], [0, P]], channel_multiplier=1, after=(big2,)),
    ]
    s = m.pool(nc.gpsimd.iota, xor, pattern=[[1, P]], base=0, channel_multiplier=0)
    t = m.pool(nc.gpsimd.iota, srow, pattern=[[0, P]], base=0, channel_multiplier=1)
    x = m.dve(nc.vector.tensor_tensor, xor, xor, srow, ALU.bitwise_xor, after=(s, t))
    d = None
    for l in range(7):
        d = m.dve(nc.vector.tensor_scalar, tmp, xor, l, None, ALU.logical_shift_right, after=(x, d))
        d = m.dve(nc.vector.tensor_scalar, m.level[:, l, :], tmp, 1.0, None, ALU.is_equal, after=(d,))
        d = m.dve(nc.vector.tensor_tensor, m.level[:, l, :], m.level[:, l, :], m.upto[:, :], ALU.mult, after=(d, out[1]))
    return out + [d]


class Layer:

    GLU_A, GLU_G, QKV, Z, GATES, TILES = 0, 8, 16, 40, 48, 64
    NORMS = ["ffn1_norm_pre", "ffn1_norm_post", "mix_norm_pre", "mix_norm_post", "ffn2_norm_pre", "ffn2_norm_post",
             "cnv_dw_b", "cnv_ln_g", "cnv_ln_b", "cnv_b_o"]

    def __init__(self, m):
        sb = m.sb
        self.x, self.h, self.y = (sb(n, [P, KT, NT]) for n in ("residual", "normed", "branch"))
        self.stat = sb("stat", [P, NT])
        self.proj = sb("proj", [P, self.TILES, NT])
        self.conv = sb("gdn_conv", [P, 24, NT])
        self.glu = sb("glu_conv", [P, KT, NT])
        self.silu = sb("ffn_silu", [P, 2, NT])
        self.gated = sb("ffn_gated", [P, 2, NT])
        self.rows = sb("param_rows", [P, 4, P])
        self.cols = sb("param_cols", [P, 97])
        self.gdn_w = sb("gdn_conv_cols", [P, 4 * 24])
        self.dw_w = sb("cnv_dw_cols", [P, 31 * KT])
        self.w_ab = sb("w_beta_a", [P, KT, 16])
        self.head = sb("head_params", [8, 4])
        self.hrow = sb("head_rows", [8, 6, NT])
        self.tok = sb("token_cols", [P, 2, 4, 8])
        self.q2 = [sb(f"q_decayed{g}", [P, 4, P]) for g in range(2)]
        self.norm16 = sb("row_norms", [16, NT])
        eight = lambda t, a: t[:, a:a + 4, :].rearrange("p a (b n) -> p (a b) n", b=2)
        self.spare_tiles = spare = sb("delta_spare", [P, 8, NT])
        names = ["D", "A", "KB", "T", "TT", "QK", "VB", "KX"]
        homes = [[(self.proj, 4 * i) for i in range(8)],
                 [(self.proj, 32), (self.proj, 36), (self.h, 0), (self.h, 4), (self.y, 0), (self.y, 4), (spare, 0), (spare, 4)]]
        self.spare = eight(spare, 0)

        self.delta = [{n: eight(*at) for n, at in zip(names, home)} for home in homes]


def load_layer_params(m, L, io, l):
    nc = m.nc
    one = lambda a: a[bass.ds(l, 1), :].rearrange("o (k c) -> (o k) c", c=P)
    sp = nc.sync
    m.params_in.by(sp.dma_start(L.w_ab[:, :, :], io["mix_w_in"][bass.ds(l, 1), :, 4096:4112].rearrange(
        "o (k p) c -> p (o k) c", p=P)))
    for i, name in enumerate(L.NORMS):
        m.params_in.by(sp.dma_start(L.rows[8 * i:8 * i + 8, 0, :], one(io[name])))
    m.params_in.by(sp.dma_start(L.rows[80:96, 0, :], one(io["cnv_pw1_b"])))
    m.params_in.by(sp.dma_start(L.rows[96:97, 0, :], one(io["gdn_norm_w"])))
    m.params_in.by(sp.dma_start(L.rows[0:96, 1, :], io["gdn_conv_w"][bass.ds(l, 1), :, :].rearrange(
        "o t (k c) -> (o t k) c", c=P)))
    for i, (a, b) in enumerate(((0, 16), (16, 31))):
        m.params_in.by(sp.dma_start(L.rows[0:(b - a) * KT, 2 + i, :], io["cnv_dw_w"][bass.ds(l, 1), a:b, :].rearrange(
            "o t (k c) -> (o t k) c", c=P)))
    m.params_in.by(sp.dma_start(L.head[:, 0:1], io["gdn_a_log"][bass.ds(l, 1), :].rearrange("o h -> h o")))
    m.params_in.by(sp.dma_start(L.head[:, 1:2], io["gdn_dt_bias"][bass.ds(l, 1), :].rearrange("o h -> h o")))
    there = m.params_in.done()
    d = [to_columns(m, L.rows[:, 0, :], 97, L.cols[:, :], 4, after=(there,)),
         to_columns(m, L.rows[:, 1, :], 96, L.gdn_w[:, :], 5, after=(there,)),
         to_columns(m, L.rows[:, 2, :], 128, L.dw_w[:, 0:128], 6, after=(there,)),
         to_columns(m, L.rows[:, 3, :], 120, L.dw_w[:, 128:248], 7, after=(there,))]
    d.append(m.dve(nc.vector.tensor_scalar, L.cols[:, 8:16], L.cols[:, 8:16], 0.5, None, ALU.mult, after=(d[0],)))
    d.append(m.dve(nc.vector.tensor_scalar, L.cols[:, 40:48], L.cols[:, 40:48], 0.5, None, ALU.mult, after=(d[0],)))
    return d[-1]


def depthwise(m, src, dst, weight, taps, centre, tiles, bias=None, after=()):
    nc = m.nc
    last = {}
    order = [centre] + [k for k in range(taps) if k != centre]
    for k in order:
        s = k - centre
        for c in tiles:
            w = weight(k, c)
            if k == centre:
                if bias is None:
                    last[c] = m.dve(nc.vector.tensor_scalar, dst(c), src(c), w, None, ALU.mult, after=after)
                else:
                    last[c] = m.dve(nc.vector.tensor_scalar, dst(c), src(c), w, bias(c), ALU.mult, ALU.add, after=after)
                continue
            to, frm = (slice(-s, NT), slice(0, NT + s)) if s < 0 else (slice(0, NT - s), slice(s, NT))
            last[c] = m.dve(nc.vector.scalar_tensor_tensor, out=dst(c)[:, to], in0=src(c)[:, frm], scalar=w,
                            in1=dst(c)[:, to], op0=ALU.mult, op1=ALU.add, after=(last[c],))
    return last


def head_sums(m, squares, n_rows, out, bank, eps, scale=1.0, per_row=1, after=()):
    nc = m.nc
    steps = []
    n = n_rows * per_row
    for i in range(n):
        steps.append((m.bank[bank][0:n_rows, 0:NT], m.onehot[:, i // per_row, 0:n_rows], squares(i), i == 0, i == n - 1))
    s = m.matmuls(steps, after=after, bank=bank)
    d = m.dve(nc.vector.tensor_scalar, out, m.bank[bank][0:n_rows, 0:NT], scale, eps, ALU.mult, ALU.add, after=(s,))
    m.read[bank] = [d]
    d = m.dve(nc.vector.reciprocal, out, out, after=(d,))
    return m.act(nc.scalar.activation, out, out, ACT.Sqrt, after=(d,))


def spread_row(m, bank, half, rows, n_rows, j, after=()):
    return m.matmuls([(m.bank[bank][:, half * NT:(half + 1) * NT], m.pick[0:n_rows, j, :], rows, True, True)],
                     after=after, bank=bank)


def conformer(m, L, glu_in, tap_cols):
    nc = m.nc
    proj = L.proj
    for k in range(KT):
        s = m.act(nc.scalar.activation, proj[:, L.GLU_G + k, :], proj[:, L.GLU_G + k, :], ACT.Sigmoid,
                  bias=L.cols[:, 88 + k:89 + k], after=glu_in)
        d = m.dve(nc.vector.scalar_tensor_tensor, out=proj[:, L.GLU_G + k, :], in0=proj[:, L.GLU_A + k, :],
                  scalar=L.cols[:, 80 + k:81 + k], in1=proj[:, L.GLU_G + k, :], op0=ALU.add, op1=ALU.mult, after=(s,))
    return depthwise(m, lambda c: proj[:, L.GLU_G + c, :], lambda c: L.glu[:, c, :],
                     lambda k, c: L.dw_w[:, 8 * k + c:8 * k + c + 1], 31, 30, range(KT),
                     bias=lambda c: L.cols[:, 48 + c:49 + c], after=(d,))


def conformer_norm(m, L, conv_done, bank):
    nc = m.nc
    last = [conv_done[c] for c in range(KT)]
    tmp, glu = L.proj, L.glu
    wide = lambda a: a.unsqueeze(1).to_broadcast([P, KT, NT])
    s = m.matmuls([(m.bank[bank][:, 0:NT], m.ones[:, :], glu[:, k, :], k == 0, k == KT - 1) for k in range(KT)],
                  after=last, bank=bank)
    mean = m.act(nc.scalar.mul, L.stat[:, :], m.bank[bank][:, 0:NT], 1.0 / (KT * P), after=(s,))
    m.read[bank] = [mean]
    c = m.dve(nc.vector.tensor_tensor, glu[:, :, :], glu[:, :, :], wide(L.stat[:, :]), ALU.subtract, after=(mean,))
    sq = m.act(nc.scalar.square, tmp[:, 0:KT, :], glu[:, :, :], after=(c,))
    s = m.matmuls([(m.bank[bank][:, 0:NT], m.ones[:, :], tmp[:, k, :], k == 0, k == KT - 1) for k in range(KT)],
                  after=(sq,), bank=bank)
    v = m.dve(nc.vector.tensor_scalar, L.stat[:, :], m.bank[bank][:, 0:NT], 1.0 / (KT * P), LN_EPS, ALU.mult, ALU.add, after=(s,))
    m.read[bank] = [v]
    v = m.dve(nc.vector.reciprocal, L.stat[:, :], L.stat[:, :], after=(v,))
    v = m.act(nc.scalar.activation, L.stat[:, :], L.stat[:, :], ACT.Sqrt, after=(v,))
    v = m.dve(nc.vector.tensor_tensor, glu[:, :, :], glu[:, :, :], wide(L.stat[:, :]), ALU.mult, after=(v,))
    return [m.act(nc.scalar.activation, glu[:, k, :], glu[:, k, :], ACT.Silu, bias=L.cols[:, 64 + k:65 + k],
                  scale=L.cols[:, 56 + k:57 + k], after=(v,)) for k in range(KT)]


def head_scalars(m, L, h, after):
    nc = m.nc
    hrow, head, b = L.hrow, L.head, 4
    s = m.matmuls([(m.bank[b][0:8, i * NT:(i + 1) * NT], L.w_ab[:, k, 8 * i:8 * i + 8], h[:, k, :], k == 0, k == KT - 1)
                   for i in range(2) for k in range(KT)], after=(*after, m.params_in.done()), bank=b)
    beta = m.act(nc.scalar.activation, hrow[:, 0, :], m.bank[b][0:8, 0:NT], ACT.Sigmoid, after=(s,))
    e = m.act(nc.scalar.activation, head[:, 2:3], head[:, 0:1], ACT.Exp, after=(m.params_in.done(),))
    a = m.dve(nc.vector.tensor_scalar, hrow[:, 3, :], m.bank[b][0:8, NT:2 * NT], head[:, 1:2], None, ALU.add, after=(beta,))
    m.read[b] = [beta, a]
    sp = softplus(m, hrow[:, 3, :], hrow[:, 1, :], hrow[:, 4, :], hrow[:, 5, :], after=(a,))
    g = m.dve(nc.vector.tensor_scalar, hrow[:, 1, :], hrow[:, 1, :], head[:, 2:3], -1.0, ALU.mult, ALU.mult, after=(sp, e))
    one = m.dve(nc.vector.memset, hrow[:, 4, :], 1.0, after=(sp,))
    for c in range(2):
        at = slice(c * P, (c + 1) * P)
        G = m.dve(nc.vector.tensor_tensor_scan, hrow[:, 2, at], hrow[:, 4, at], hrow[:, 1, at], 0.0, ALU.mult, ALU.add,
                  after=(g, one))
    b = 5
    m.pe.wait(*m.read[b])
    for c in range(2):
        for i, r in enumerate((0, 2)):
            t = m.pe(nc.tensor.transpose, m.bank[b][:, (2 * c + i) * 8:(2 * c + i) * 8 + 8],
                     hrow[:, r, c * P:(c + 1) * P], m.ident[0:8, 0:8], after=(G, beta))
    cp = m.dve(nc.vector.tensor_copy, L.tok[:, :, 0:2, :],
               m.bank[b][:, 0:32].rearrange("p (c i h) -> p c i h", c=2, i=2), after=(t,))
    m.read[b] = [cp]
    x = m.act(nc.scalar.activation, L.tok[:, 1, 3, :], L.tok[:, 1, 1, :], ACT.Exp, after=(cp,))
    d = m.dve(nc.vector.tensor_tensor, L.tok[:, 1, 2, :], L.tok[:, 1, 0, :], L.tok[:, 1, 3, :], ALU.mult, after=(x,))
    return G, d


def delta_rule(m, L, taps_done, row_G, tok_cols, projected):
    nc = m.nc
    conv, proj, tok = L.conv, L.proj, L.tok
    silu = {}
    for i in range(6):
        four = slice(4 * i, 4 * i + 4)
        silu[i] = m.act(nc.scalar.activation, conv[:, four, :], conv[:, four, :], ACT.Silu,
                        after=[taps_done[c] for c in range(4 * i, 4 * i + 4)])
    sq = [m.act(nc.scalar.square, proj[:, L.QKV + 4 * i:L.QKV + 4 * i + 4, :], conv[:, 4 * i:4 * i + 4, :],
                after=(silu[i], taps_done[23])) for i in range(4)]
    n = head_sums(m, lambda i: proj[:, L.QKV + i, :], 16, L.norm16[:, :], 6, 1e-6, after=sq)
    kv = {}
    for i in range(8):
        b = i % 4
        for half in range(2):
            s = spread_row(m, b, half, L.norm16[:, :], 16, 2 * i + half, after=(n,) if half == 0 else ())
        two = slice(2 * i, 2 * i + 2)
        kv[i] = m.dve(nc.vector.scalar_tensor_tensor, out=conv[:, two, :], in0=conv[:, two, :],
                      scalar=P ** -0.5 if i < 4 else 1.0,
                      in1=m.bank[b][:, :].rearrange("p (a n) -> p a n", a=2), op0=ALU.mult, op1=ALU.mult, after=(s,))
        m.read[b] = [kv[i]]
    qk_ready = [kv[7], silu[5], *sq, *projected]

    buf = L.delta
    m4 = lambda b: m.bank[b][:, :].rearrange("p (h n) -> p h n", h=4)
    ch = lambda t, c: t[:, 4 * c:4 * c + 4, :]
    head = lambda i, g: slice(8 * i + 4 * g, 8 * i + 4 * g + 4)
    D = [{} for _ in range(2)]

    for g in range(2):
        B, r = buf[g], D[g]
        b0 = 4 * g
        for i in range(4):
            s = spread_row(m, b0 + i // 2, i % 2, L.hrow[:, 2, :], 8, 4 * g + i, after=(row_G, *qk_ready))
            s2 = spread_row(m, b0 + 2 + i // 2, i % 2, L.hrow[:, 0, :], 8, 4 * g + i)
        for i in range(4):
            h = 4 * g + i
            G = m.bank[b0 + i // 2][:, (i % 2) * NT:(i % 2 + 1) * NT]
            for c in range(2):
                dd = m.dve(nc.vector.tensor_scalar, B["D"][:, 4 * c + i, :], G[:, c * P:(c + 1) * P],
                           tok[:, c, 1, h:h + 1], 0.0, ALU.subtract, ALU.min, after=(s, tok_cols))
            dl = m.dve(nc.vector.tensor_tensor, tok[:, 0, 2, h:h + 1], G[:, P - 1:P], tok[:, 0, 1, h:h + 1], ALU.subtract)
        for i in range(4):
            G = m.bank[b0 + i // 2][:, (i % 2) * NT:(i % 2 + 1) * NT]
            ge = m.act(nc.scalar.activation, L.q2[g][:, i, :], G[:, P:2 * P], ACT.Exp, after=(dl,))
        r["end"] = m.act(nc.scalar.activation, tok[:, 0, 3, 4 * g:4 * g + 4], tok[:, 0, 2, 4 * g:4 * g + 4], ACT.Exp, after=(dl,))
        r["E"] = m.act(nc.scalar.activation, B["D"], B["D"], ACT.Exp, after=(dd,))
        for i in range(2):
            kb = m.dve(nc.vector.tensor_tensor, B["KB"].rearrange("p (h c) n -> p h (c n)", c=2)[:, 2 * i:2 * i + 2, :],
                       conv[:, 8 + 4 * g + 2 * i:8 + 4 * g + 2 * i + 2, :],
                       m.bank[b0 + 2 + i][:, :].rearrange("p (a n) -> p a n", a=2), ALU.mult, after=(s2,))
        r["q2"] = m.dve(nc.vector.tensor_tensor, L.q2[g][:, :, :], L.q2[g][:, :, :], conv[:, head(0, g), P:2 * P], ALU.mult, after=(ge,))
        r["D"] = m.dve(nc.vector.tensor_tensor, B["D"], B["D"], m.upto[:, :].unsqueeze(1).to_broadcast([P, 8, P]),
                       ALU.mult, after=(r["E"],))
        r["kb"] = kb
        for i in range(4):
            m.read[b0 + i] = [dd, ge, dl, kb]

    for g in range(2):
        B, r, b0 = buf[g], D[g], 4 * g
        KB = B["KB"].rearrange("p (h c) n -> p h c n", c=2)
        for c in range(2):
            steps = [(m4(b0 + c)[:, i, :], conv[:, 8 + 4 * g + i, c * P:(c + 1) * P], KB[:, i, c, :], True, True) for i in range(4)]
            a = m.matmuls(steps, after=(r["kb"],), bank=b0 + c)
            steps = [(m4(b0 + 2 + c)[:, i, :], conv[:, 8 + 4 * g + i, c * P:(c + 1) * P],
                      conv[:, 4 * g + i, c * P:(c + 1) * P], True, True) for i in range(4)]
            q = m.matmuls(steps, bank=b0 + 2 + c)
            r["A", c] = m.dve(nc.vector.tensor_tensor, ch(B["A"], c), m4(b0 + c), ch(B["D"], c), ALU.mult, after=(a, r["D"]))
            r["QK", c] = m.dve(nc.vector.tensor_tensor, ch(B["QK"], c), m4(b0 + 2 + c), ch(B["D"], c), ALU.mult, after=(q,))
            m.read[b0 + c] = [r["A", c]]
            m.read[b0 + 2 + c] = [r["QK", c]]

    for g in range(2):
        B, r, b0 = buf[g], D[g], 4 * g
        for c in range(2):
            for i, what in ((2, 0), (1, 2)):
                b = b0 + c + what
                m.pe.wait(*m.read[b])
                for j in range(4):
                    t = m.pe(nc.tensor.transpose, m4(b)[:, j, :], conv[:, 8 * i + 4 * g + j, c * P:(c + 1) * P], m.ident[:, :])
                for j in range(4):
                    h = 4 * g + j
                    if i == 2:
                        dst, f = B["VB"], tok[:, c, 0, h:h + 1]
                    else:
                        dst, f = B["KX"], tok[:, c, 3 if c == 0 else 2, h:h + 1]
                    cp = m.act(nc.scalar.activation, dst[:, 4 * c + j, :], m4(b)[:, j, :], ACT.Copy, scale=f,
                               after=(t, r["end"], tok_cols))
                m.read[b] = [cp]
        r["tok"] = cp

    eye = m.ident[:, :].unsqueeze(1).to_broadcast([P, 4, P])
    for l in range(7):
        mask = m.level[:, l, :].unsqueeze(1).to_broadcast([P, 4, P])
        for g in range(2):
            B, r, b0 = buf[g], D[g], 4 * g
            for c in range(2):
                r["L", c] = m.dve(nc.vector.tensor_tensor, ch(B["KB"], c), ch(B["A"], c), mask, ALU.mult,
                                  after=(r["A", 1], r.get(("M", c)), r.get(("TT", c))))
        for g in range(2):
            B, r, b0 = buf[g], D[g], 4 * g
            for c in range(2):
                pr = range(4 * c, 4 * c + 4)
                mm = m.matmuls([(m4(b0 + c)[:, p % 4, :], B["KB"][:, p, :], m.ident[:, :] if l == 0 else B["T"][:, p, :],
                                 True, True) for p in pr], after=(r["L", c], r.get(("T", c))), bank=b0 + c)
                if l == 0:
                    r["T", c] = m.dve(nc.vector.tensor_tensor, ch(B["T"], c), eye, m4(b0 + c), ALU.subtract, after=(mm,))
                    r["TT", c] = m.dve(nc.vector.tensor_tensor, ch(B["TT"], c), eye, ch(B["KB"], c), ALU.subtract,
                                       after=(r["L", c],))
                    m.read[b0 + c] = [r["T", c]]
                    r["M", c] = mm
                    continue
                cp = m.act(nc.scalar.copy, ch(B["D"], c), m4(b0 + c), after=(mm, r["QK", c], r.get(("TTp", c))))
                m.read[b0 + c] = [cp]
                r["M", c], r["Mc", c] = mm, cp
        if l == 0:
            continue
        for g in range(2):
            B, r, b0 = buf[g], D[g], 4 * g
            for c in range(2):
                pr = range(4 * c, 4 * c + 4)
                if l < 6:
                    r["Tp", c] = m.matmuls([(m4(b0 + 2 + c)[:, p % 4, :], B["TT"][:, p, :], B["D"][:, p, :], True, True)
                                            for p in pr], after=(r["Mc", c], r["TT", c]), bank=b0 + 2 + c)
                r["TTp", c] = m.matmuls([(m4(b0 + c)[:, p % 4, :], B["D"][:, p, :], B["TT"][:, p, :], True, True)
                                         for p in pr], after=(r["Mc", c], r["TT", c]), bank=b0 + c)
                if l < 6:
                    r["T", c] = m.dve(nc.vector.tensor_tensor, ch(B["T"], c), ch(B["T"], c), m4(b0 + 2 + c), ALU.subtract,
                                      after=(r["Tp", c],))
                    m.read[b0 + 2 + c] = [r["T", c]]
                r["TT", c] = m.dve(nc.vector.tensor_tensor, ch(B["TT"], c), ch(B["TT"], c), m4(b0 + c), ALU.subtract,
                                   after=(r["TTp", c],))
                m.read[b0 + c] = [r["TT", c]]

    done = []
    for g in range(2):
        B, r, b0 = buf[g], D[g], 4 * g
        W, S, V = B["T"][:, 0:4, :], B["T"][:, 4:8, :], B["A"]
        r["v0p"] = m.matmuls([(m4(b0)[:, i, :], B["TT"][:, i, :], B["VB"][:, i, :], True, True) for i in range(4)],
                             after=(r["TT", 0], r["tok"]), bank=b0)
        wp = m.matmuls([(m4(b0 + 1)[:, i, :], B["KX"][:, 4 + i, :], B["TT"][:, 4 + i, :], True, True) for i in range(4)],
                       after=(r["TT", 1],), bank=b0 + 1)
        r["v0"] = m.act(nc.scalar.copy, V[:, 0:4, :], m4(b0), after=(r["v0p"],))
        r["w"] = m.act(nc.scalar.mul, W, m4(b0 + 1), -1.0, after=(wp,))
        m.read[b0], m.read[b0 + 1] = [r["v0"]], [r["w"]]
    for g in range(2):
        B, r, b0 = buf[g], D[g], 4 * g
        W, S, V = B["T"][:, 0:4, :], B["T"][:, 4:8, :], B["A"]
        s = m.matmuls([(m4(b0 + 2)[:, i, :], B["KX"][:, i, :], V[:, i, :], True, True) for i in range(4)],
                      after=(r["v0"],), bank=b0 + 2)
        r["S"] = m.act(nc.scalar.copy, S, m4(b0 + 2), after=(s,))
        m.read[b0 + 2] = [r["S"]]
    for g in range(2):
        B, r, b0 = buf[g], D[g], 4 * g
        W, S, V = B["T"][:, 0:4, :], B["T"][:, 4:8, :], B["A"]
        steps = []
        for i in range(4):
            steps.append((m4(b0 + 3)[:, i, :], B["TT"][:, 4 + i, :], B["VB"][:, 4 + i, :], True, False))
            steps.append((m4(b0 + 3)[:, i, :], W[:, i, :], S[:, i, :], False, True))
        v = m.matmuls(steps, after=(r["S"], r["w"]), bank=b0 + 3)
        r["v1"] = m.act(nc.scalar.copy, V[:, 4:8, :], m4(b0 + 3), after=(v,))
        m.read[b0 + 3] = [r["v1"]]
    for g in range(2):
        B, r, b0 = buf[g], D[g], 4 * g
        W, S, V = B["T"][:, 0:4, :], B["T"][:, 4:8, :], B["A"]
        o0 = m.matmuls([(m4(b0)[:, i, :], V[:, i, :], B["QK"][:, i, :], True, True) for i in range(4)], bank=b0)
        steps = []
        for i in range(4):
            steps.append((m4(b0 + 1)[:, i, :], S[:, i, :], L.q2[g][:, i, :], True, False))
            steps.append((m4(b0 + 1)[:, i, :], V[:, 4 + i, :], B["QK"][:, 4 + i, :], False, True))
        o1 = m.matmuls(steps, after=(r["v1"], r["q2"]), bank=b0 + 1)
        c0 = m.act(nc.scalar.copy, conv[:, head(0, g), 0:P], m4(b0), after=(o0,))
        c1 = m.act(nc.scalar.copy, conv[:, head(0, g), P:NT], m4(b0 + 1), after=(o1,))
        m.read[b0], m.read[b0 + 1] = [c0], [c1]
        done += [c0, c1]

    sq = m.act(nc.scalar.square, conv[:, 8:16, :], conv[:, 0:8, :], after=done)
    n = head_sums(m, lambda i: conv[:, 8 + i, :], 8, L.norm16[0:8, :], 2, RMS_EPS, scale=1.0 / P, after=(sq,))
    z = m.act(nc.scalar.activation, proj[:, L.Z:L.Z + 8, :], proj[:, L.Z:L.Z + 8, :], ACT.Silu)
    out = []
    for i in range(4):
        for half in range(2):
            s = spread_row(m, 4 + i, half, L.norm16[0:8, :], 8, 2 * i + half, after=(n,))
        two = slice(2 * i, 2 * i + 2)
        d = m.dve(nc.vector.scalar_tensor_tensor, out=conv[:, two, :], in0=conv[:, two, :], scalar=L.cols[:, 96:97],
                  in1=m.bank[4 + i][:, :].rearrange("p (a n) -> p a n", a=2), op0=ALU.mult, op1=ALU.mult, after=(s,))
        m.read[4 + i] = [d]
        out.append(m.dve(nc.vector.tensor_tensor, conv[:, two, :], conv[:, two, :], proj[:, L.Z + 2 * i:L.Z + 2 * i + 2, :],
                         ALU.mult, after=(d, z)))
    return out


def mixer(m, L, io, l, normed):
    nc = m.nc
    w = io["mix_w_in"]
    proj, conv = L.proj, L.conv
    G, tok_cols = head_scalars(m, L, L.h, normed)
    glu_in = m.project(L.h, lambda b: columns(w, l, b * 256 + 4112), 8, proj, L.GLU_A, after=normed)
    conv_done = conformer(m, L, glu_in, None)
    qkv_in = m.project(L.h, lambda b: columns(w, l, b * 256), 12, proj, L.QKV)
    taps_done = depthwise(m, lambda c: proj[:, L.QKV + c, :], lambda c: conv[:, c, :],
                          lambda k, c: L.gdn_w[:, 24 * k + c:24 * k + c + 1], 4, 3, range(24), after=qkv_in)
    m.project(L.h, lambda b: columns(w, l, b * 256 + 3072), 4, proj, L.Z)
    gates_in = m.project(L.h, lambda b: columns(w, l, b * 256 + 6160), 8, proj, L.GATES)
    conf = conformer_norm(m, L, conv_done, 7)
    gate = m.act(nc.scalar.activation, proj[:, L.GATES:L.GATES + 16, :], proj[:, L.GATES:L.GATES + 16, :], ACT.Sigmoid,
                 after=gates_in)
    o = delta_rule(m, L, taps_done, G, tok_cols, gates_in)

    two = lambda t, b: t[:, 2 * b:2 * b + 2, :]
    bank2 = lambda s: m.bank[s][:, :].rearrange("p (a n) -> p a n", a=2)
    branch = {}

    def evict_conf(b, s):
        m.computed[s].wait(m.dve)
        m.dve.wait(gate)
        for i in range(2):
            t = 2 * b + i
            ins = nc.vector.scalar_tensor_tensor(out=proj[:, t, :],
                                                 in0=m.bank[s][:, i * NT:(i + 1) * NT], scalar=L.cols[:, 72 + t:73 + t],
                                                 in1=proj[:, L.GATES + 8 + t, :], op0=ALU.add, op1=ALU.mult)
            if i == 1:
                m.evicted[s].by(ins)

    def evict_gdn(b, s):
        m.computed[s].wait(m.dve)
        ins = nc.vector.tensor_tensor(two(L.y, b), bank2(s), proj[:, L.GATES + 2 * b:L.GATES + 2 * b + 2, :], ALU.mult)
        m.evicted[s].by(ins)
        branch[b] = m.dve(nc.vector.tensor_tensor, two(L.y, b), two(L.y, b), two(proj, b), ALU.add,
                          after=(m.evicted[s].done(),))

    def evict_out(b, s):
        m.computed[s].wait(m.act)
        m.evicted[s].by(nc.scalar.copy(two(L.h, b), bank2(s)))
        branch["out", b] = m.evicted[s].done()

    m.project_with(L.glu, lambda b: columns(io["cnv_w_o"], l, b * 256), evict_conf, after=conf)
    m.project_with(conv, lambda b: columns(io["gdn_w_o"], l, b * 256), evict_gdn, after=o)
    m.project_with(L.y, lambda b: columns(io["mix_w_out"], l, b * 256), evict_out, after=[branch[b] for b in range(4)])
    return [branch["out", b] for b in range(4)]


def layer(m, L, io, l):
    d_ff = io["ffn1_w_out"].shape[1]
    g = lambda i: L.cols[:, 8 * i:8 * i + 8]
    tmp = L.y
    params = load_layer_params(m, L, io, l)
    n = rms_norm(m, L.x, g(0), L.h, L.y, L.stat[:, :], 0, after=(params,))
    y = ffn(m, L.h, io["ffn1_w_in"], io["ffn1_w_out"], l, d_ff, L.gated, L.silu, L.y, after=n)
    d = add_normed(m, L.x, L.y, g(1), L.h, L.stat[:, :], 0, after=y)
    n = rms_norm(m, L.x, g(2), L.h, L.y, L.stat[:, :], 0, after=(d,))
    y = mixer(m, L, io, l, n)
    d = add_normed(m, L.x, L.h, g(3), L.y, L.stat[:, :], 0, after=y)
    n = rms_norm(m, L.x, g(4), L.h, L.y, L.stat[:, :], 0, after=(d,))
    y = ffn(m, L.h, io["ffn2_w_in"], io["ffn2_w_out"], l, d_ff, L.gated, L.silu, L.y, after=n)
    return add_normed(m, L.x, L.y, g(5), L.h, L.stat[:, :], 0, after=y)


def turn_in(m, x, rows, bank0=0, after=()):
    nc = m.nc
    out = []
    for k in range(KT):
        b = bank0 + k % 4
        m.pe.wait(*m.read[b])
        for t in range(2):
            tr = m.pe(nc.tensor.transpose, m.bank[b][:, t * P:(t + 1) * P], rows[:, t, k * P:(k + 1) * P], m.ident[:, :],
                      after=after)
        c = m.act(nc.scalar.copy, x[:, k, :], m.bank[b][:, 0:NT], after=(tr,))
        m.read[b] = [c]
        out.append(c)
    return out


def turn_out(m, rows, x, bank0=0, after=()):
    nc = m.nc
    out = []
    for t in range(2):
        for half in range(2):
            b = bank0 + 2 * t + half
            m.pe.wait(*m.read[b])
            for k in range(4):
                tr = m.pe(nc.tensor.transpose, m.bank[b][:, k * P:(k + 1) * P], x[:, 4 * half + k, t * P:(t + 1) * P],
                          m.ident[:, :], after=after)
            c = m.act(nc.scalar.copy, rows[:, t, half * 512:half * 512 + 512], m.bank[b][:, :], after=(tr,))
            m.read[b] = [c]
            out.append(c)
    return out


class Block:

    XM, O, XL, LRU_GATE, MERGE, LRU_X, LRU_F = 0, 8, 16, 24, 32, 48, 56

    def __init__(self, m, L):
        self.L = L
        sb = m.sb
        self.bias = sb("gate_bias", [4, 4])
        self.rows = L.spare_tiles[0:4, :, :]
        self.c_cols = sb("c_by_token", [P, 2, 2, 4])
        self.lam = sb("lru_decay", [P, 2, 16])


def load_block_params(m, L, B, io):
    nc = m.nc
    sp = nc.sync
    rows = lambda a: a[0:1].rearrange("o (k c) -> (o k) c", c=P) if len(a.shape) == 2 else a[0:1].rearrange("o t (k c) -> (o t k) c", c=P)
    for i, group in enumerate((("norm1_g_2", "mlstm_conv_w_2", "mlstm_conv_b_2", "mlstm_norm_g_2", "lru_conv_w_2",
                                "lru_conv_b_2", "norm2_g_2"), ("lru_b_r_2", "lru_b_i_2", "lru_lambda_2"))):
        at = 0
        for name in group:
            r = rows(io[name])
            m.params_in.by(sp.dma_start(L.rows[at:at + r.shape[0], i, :], r))
            at += r.shape[0]
    m.params_in.by(sp.dma_start(L.w_ab[:, :, :], io["w_in_2"][0:1, :, 2048:2064].rearrange("o (k p) c -> p (o k) c", p=P)))
    for k in range(4):
        m.params_in.by(sp.dma_start(B.bias[:, k:k + 1], io["b_gates_2"][0:1, 4 * k:4 * k + 4].rearrange("o h -> h o")))
    there = m.params_in.done()
    return [to_columns(m, L.rows[:, 0, :], 104, L.dw_w[:, 0:104], 4, after=(there,)),
            to_columns(m, L.rows[:, 1, :], 48, L.dw_w[:, 104:152], 5, after=(there,))]


def mlstm_gates(m, L, B, normed):
    nc = m.nc
    R = B.rows
    h = L.h
    for d in range(2):
        s = m.matmuls([(m.bank[4 + d][0:4, i * NT:(i + 1) * NT], L.w_ab[:, k, 8 * d + 4 * i:8 * d + 4 * i + 4], h[:, k, :],
                        k == 0, k == KT - 1) for i in range(2) for k in range(KT)], after=(*normed, m.params_in.done()), bank=4 + d)
        x = m.dve(nc.vector.tensor_scalar, R[:, d, :], m.bank[4 + d][0:4, NT:2 * NT], B.bias[:, 2 * d + 1:2 * d + 2], -1.0,
                  ALU.add, ALU.mult, after=(s,))
    sp = softplus(m, R[:, 0:2, :], R[:, 2:4, :], R[:, 4:6, :], R[:, 6:8, :], after=(x,))
    one = m.dve(nc.vector.memset, R[:, 4:6, :], 1.0, after=(sp,))
    rev = lambda a, d: a if d == 0 else a[:, ::-1]
    for d in range(2):
        b = m.dve(nc.vector.tensor_tensor_scan, rev(R[:, 6 + d, :], d), rev(R[:, 4 + d, :], d), rev(R[:, 2 + d, :], d), 0.0,
                  ALU.mult, ALU.subtract, after=(one,))
        c = m.dve(nc.vector.scalar_tensor_tensor, out=R[:, d, :], in0=m.bank[4 + d][0:4, 0:NT], scalar=B.bias[:, 2 * d:2 * d + 1],
                  in1=R[:, 6 + d, :], op0=ALU.add, op1=ALU.subtract, after=(b,))
        m.read[4 + d] = [c]
        M = m.dve(nc.vector.tensor_tensor_scan, rev(R[:, 4 + d, :], d), rev(R[:, d, :], d), rev(R[:, d, :], d), 0.0,
                  ALU.max, ALU.max, after=(c,))
        s = m.dve(nc.vector.tensor_tensor, R[:, 2 + d, :], R[:, 6 + d, :], R[:, 4 + d, :], ALU.add, after=(M,))
    em = m.act(nc.scalar.activation, R[:, 2:4, :], R[:, 2:4, :], ACT.Exp, scale=-1.0, after=(s,))
    bk = 6
    m.pe.wait(*m.read[bk])
    for d in range(2):
        for t in range(2):
            tr = m.pe(nc.tensor.transpose, m.bank[bk][:, (2 * d + t) * 4:(2 * d + t) * 4 + 4], R[:, d, t * P:(t + 1) * P],
                      m.ident[0:4, 0:4], after=(s,))
    cp = m.dve(nc.vector.tensor_copy, B.c_cols[:, :, :, :], m.bank[bk][:, 0:16].rearrange("p (d t h) -> p d t h", d=2, t=2),
               after=(tr,))
    m.read[bk] = [cp]
    return [M, em, cp]


def head_block(io, name):
    return io[name][0].rearrange("h (k p) e -> p (h k) e", p=P)


def mlstm(m, L, B, io, projected, gates):
    nc = m.nc
    proj, conv = L.proj, L.conv
    taps = depthwise(m, lambda c: proj[:, B.XM + c, :], lambda c: conv[:, c, :],
                     lambda k, c: L.dw_w[:, 8 + 8 * k + c:9 + 8 * k + c], 4, 2, range(KT),
                     bias=lambda c: L.dw_w[:, 40 + c:41 + c], after=projected)
    xc = m.act(nc.scalar.activation, conv[:, 0:8, :], conv[:, 0:8, :], ACT.Silu, after=[taps[c] for c in range(8)])
    values = L.glu[:, :, :].rearrange("p a n -> p (a n)").rearrange("p (t e) -> p t e", t=2)
    bank2 = lambda b: m.bank[b][:, :].rearrange("p (a n) -> p a n", a=2)
    ready = []
    sv = m.load_block(head_block(io, "mlstm_w_v_2"))
    sq = m.load_block(head_block(io, "mlstm_w_q_2"))
    sk = m.load_block(head_block(io, "mlstm_w_k_2"))
    m.loaded[sv].wait(m.pe)
    for h in range(4):
        p = m.matmuls([(m.bank[h][:, t * NT:(t + 1) * NT], proj[:, B.XM + 2 * h + k, t * P:(t + 1) * P],
                        m.slot[sv][:, 2 * h + k, :], k == 0, k == 1) for t in range(2) for k in range(2)],
                      after=projected, bank=h)
        c = m.act(nc.scalar.copy, values[:, :, h * NT:(h + 1) * NT], bank2(h), after=(p,))
        m.read[h] = [c]
        ready.append(c)
    m.release(sv, p)
    for s, at in ((sq, 8), (sk, 16)):
        m.loaded[s].wait(m.pe)
        for h in range(4):
            b = h if at == 8 else 4 + h
            p = m.matmuls([(m.bank[b][:, e * NT:(e + 1) * NT], m.slot[s][:, 2 * h + k, e * P:(e + 1) * P], conv[:, 2 * h + k, :],
                            k == 0, k == 1) for e in range(2) for k in range(2)], after=(xc,), bank=b)
            c = m.act(nc.scalar.copy, conv[:, at + 2 * h:at + 2 * h + 2, :], bank2(b), after=(p,))
            m.read[b] = [c]
            ready.append(c)
        m.release(s, p)

    H = L.h
    E = lambda d, h: L.y[:, 4 * (h % 2) + 2 * d:4 * (h % 2) + 2 * d + 2, :]
    den = [L.silu, L.gated]
    used, wrote = {}, {}
    for h in range(4):
        sb = h % 2
        score = m.matmuls([(m.bank[sb][:, t * NT:(t + 1) * NT], conv[:, 16 + 2 * h + e, t * P:(t + 1) * P],
                            conv[:, 8 + 2 * h + e, :], e == 0, e == 1) for t in range(2) for e in range(2)],
                          after=ready, bank=sb)
        for d in range(2):
            ms = m.matmuls([(m.bank[2 + d][:, 0:NT], m.pick[0:4, h, :], B.rows[:, 4 + d, :], True, True),
                            (m.bank[2 + d][:, NT:2 * NT], m.pick[0:4, h, :], B.rows[:, 2 + d, :], True, True)],
                           after=gates, bank=2 + d)
            e = E(d, h)
            span = [slice(0, NT), slice(P, NT)] if d == 0 else [slice(0, P), slice(0, NT)]
            for t in range(2):
                w = m.dve(nc.vector.tensor_scalar, e[:, t, span[t]], m.bank[2 + d][:, span[t]], B.c_cols[:, d, t, h:h + 1], 0.0,
                          ALU.subtract, ALU.max, after=(ms, *gates, used.get((d, sb))))
            for t in range(2):
                x = m.act(nc.scalar.activation, e[:, t, span[t]], e[:, t, span[t]], ACT.Exp, scale=-1.0, after=(w,))
            for t in range(2):
                diag = slice(t * P, (t + 1) * P)
                k = m.dve(nc.vector.tensor_tensor, e[:, t, diag], e[:, t, diag], (m.upto if d == 0 else m.from_)[:, :],
                          ALU.mult, after=(x,))
            for t in range(2):
                pr = m.dve(nc.vector.scalar_tensor_tensor, out=e[:, t, span[t]], in0=m.bank[sb][:, t * NT + span[t].start:t * NT + span[t].stop],
                           scalar=NT ** -0.5, in1=e[:, t, span[t]], op0=ALU.mult, op1=ALU.mult, after=(k, score))
            m.read[sb] = [pr]
            order = (0, 1) if d == 0 else (1, 0)
            dn = m.matmuls([(m.bank[4 + d][:, span[t]], m.ones[:, :], e[:, t, span[t]], i == 0, i == 1)
                            for i, t in enumerate(order)], after=(pr,), bank=4 + d)
            nm = m.matmuls([(m.bank[6 + d][:, v * NT + span[t].start:v * NT + span[t].stop],
                             values[:, t, h * NT + v * P:h * NT + (v + 1) * P], e[:, t, span[t]], i == 0, i == 1)
                            for v in range(2) for i, t in enumerate(order)], bank=6 + d)
            used[d, sb] = nm
            r = den[d][:, 0, :]
            a = m.act(nc.scalar.activation, r, m.bank[4 + d][:, 0:NT], ACT.Abs, after=(dn, wrote.get(d)))
            m.read[4 + d] = [a]
            a = m.dve(nc.vector.tensor_tensor, r, r, m.bank[2 + d][:, NT:2 * NT], ALU.max, after=(a,))
            m.read[2 + d] = [a]
            a = m.dve(nc.vector.reciprocal, r, r, after=(a,))
            rr = r.unsqueeze(1).to_broadcast([P, 2, NT])
            Hh = H[:, 2 * h:2 * h + 2, :]
            if d == 0:
                a = m.dve(nc.vector.tensor_tensor, Hh, bank2(6), rr, ALU.mult, after=(a, nm))
                m.read[6] = [a]
                first = a
            else:
                a = m.dve(nc.vector.tensor_tensor, e, bank2(7), rr, ALU.mult, after=(a, nm))
                m.read[7] = [a]
                a = m.dve(nc.vector.tensor_tensor, Hh, Hh, e, ALU.add, after=(a, first))
                used[d, sb] = a
            wrote[d] = a
    sg = m.act(nc.scalar.activation, proj[:, B.O:B.O + 8, :], proj[:, B.O:B.O + 8, :], ACT.Sigmoid, after=projected)
    sq = m.act(nc.scalar.square, L.y[:, :, :], H[:, :, :], after=(a,))
    n = head_sums(m, lambda i: L.y[:, i, :], 4, L.norm16[0:4, :], 0, RMS_EPS, scale=1.0 / NT, per_row=2, after=(sq,))
    out = []
    for h in range(4):
        s = spread_row(m, 1 + h, 0, L.norm16[0:4, :], 4, h, after=(n,))
        for v in range(2):
            t = 2 * h + v
            a = m.dve(nc.vector.scalar_tensor_tensor, out=H[:, t, :], in0=H[:, t, :], scalar=L.dw_w[:, 48 + t:49 + t],
                      in1=m.bank[1 + h][:, 0:NT], op0=ALU.mult, op1=ALU.mult, after=(s,))
            out.append(m.dve(nc.vector.tensor_tensor, H[:, t, :], H[:, t, :], proj[:, B.O + t, :], ALU.mult, after=(a, sg)))
        m.read[1 + h] = [a]
    return out


def rg_lru(m, L, B, io, projected, conv_free):
    nc = m.nc
    proj, conv = L.proj, L.conv
    X = proj[:, B.LRU_X:B.LRU_X + 8, :]
    taps = depthwise(m, lambda c: proj[:, B.XL + c, :], lambda c: proj[:, B.LRU_X + c, :],
                     lambda k, c: L.dw_w[:, 56 + 8 * k + c:57 + 8 * k + c], 4, 2, range(KT),
                     bias=lambda c: L.dw_w[:, 88 + c:89 + c], after=projected)
    taps = [taps[c] for c in range(8)]
    ng = m.dve(nc.vector.tensor_scalar, B.lam[:, 0, :], L.dw_w[:, 104 + 32:104 + 48], -1.0, None, ALU.mult)
    sp = softplus(m, B.lam[:, 0, :], B.lam[:, 1, :], L.cols[:, 0:16], L.cols[:, 16:32], after=(ng,))
    pos = m.dve(nc.vector.tensor_scalar, B.lam[:, 1, :], B.lam[:, 1, :], 8.0, None, ALU.mult, after=(sp,))
    neg = m.dve(nc.vector.tensor_scalar, B.lam[:, 0, :], B.lam[:, 1, :], -1.0, None, ALU.mult, after=(pos,))
    pairs = lambda a: a[0].rearrange("d n c e -> c (d n) e")
    view = lambda s: m.slot[s][:, :, :].rearrange("p k c -> p (k c)").rearrange("p (j e) -> p j e", e=P)
    sr = m.load_block(pairs(io["lru_w_r_2"]), view)
    si = m.load_block(pairs(io["lru_w_i_2"]), view)
    m.loaded[sr].wait(m.pe)
    m.loaded[si].wait(m.pe)
    R, I, T, A2 = conv[:, 0:8, :], conv[:, 8:16, :], conv[:, 16:24, :], L.y
    gl = m.act(nc.scalar.activation, proj[:, B.LRU_GATE:B.LRU_GATE + 8, :], proj[:, B.LRU_GATE:B.LRU_GATE + 8, :], ACT.Gelu,
               after=projected)
    free = [*conv_free]
    results = []
    for d in range(2):
        rd, idn = [], []
        for w, dst, b0, bias, out in ((sr, R, 0, 104, rd), (si, I, 4, 120, idn)):
            for n in range(8):
                b = b0 + n // 2
                s = m.matmuls([(m.bank[b][:, n % 2 * NT:(n % 2 + 1) * NT], view(w)[:, 8 * d + n, :], X[:, n, :], True, True)],
                              after=(taps[n],), bank=b if n % 2 == 0 else None)
                if n % 2:
                    for q in range(2):
                        k = n - 1 + q
                        c = m.act(nc.scalar.activation, dst[:, k, :], m.bank[b][:, q * NT:(q + 1) * NT], ACT.Sigmoid,
                                  bias=L.dw_w[:, bias + 8 * d + k:bias + 8 * d + k + 1], after=(s, *free))
                        out.append(c)
                    m.read[b] = [c]
        th, aa, a2, v = [], [], [], []
        for n in range(8):
            th.append(m.act(nc.scalar.activation, T[:, n, :], R[:, n, :], ACT.Tanh, scale=B.lam[:, 1, 8 * d + n:8 * d + n + 1],
                            after=(rd[n], neg)))
            aa.append(m.act(nc.scalar.activation, R[:, n, :], R[:, n, :], ACT.Exp, scale=B.lam[:, 0, 8 * d + n:8 * d + n + 1],
                            after=(th[n],)))
        ix = m.dve(nc.vector.tensor_tensor, I, I, X, ALU.mult, after=(idn[-1],))
        for n in range(0, 8, 4):
            f = slice(n, n + 4)
            q = m.dve(nc.vector.tensor_tensor, A2[:, f, :], R[:, f, :], R[:, f, :], ALU.mult, after=(aa[n + 3], *free))
            q = m.dve(nc.vector.scalar_tensor_tensor, out=T[:, f, :], in0=A2[:, f, :], scalar=1.0, in1=T[:, f, :], op0=ALU.add,
                      op1=ALU.mult, after=(q,))
            q = m.act(nc.scalar.activation, T[:, f, :], T[:, f, :], ACT.Sqrt, after=(q,))
            q = m.dve(nc.vector.tensor_tensor, T[:, f, :], T[:, f, :], I[:, f, :], ALU.mult, after=(q, ix))
            v += [q] * 4
        for n in range(8):
            if d == 0:
                sc = m.dve(nc.vector.tensor_tensor_scan, proj[:, B.LRU_F + n, :], R[:, n, :], T[:, n, :], 0.0, ALU.mult, ALU.add,
                           after=(v[n],))
            else:
                sc = m.dve(nc.vector.tensor_tensor_scan, A2[:, n, ::-1], R[:, n, ::-1], T[:, n, ::-1], 0.0, ALU.mult, ALU.add,
                           after=(v[n],))
        free = [sc]
    m.release(sr, s)
    m.release(si, s)
    F = proj[:, B.LRU_F:B.LRU_F + 8, :]
    a = m.dve(nc.vector.tensor_tensor, F, F, A2[:, :, :], ALU.add, after=(sc,))
    return [m.dve(nc.vector.tensor_tensor, F, F, proj[:, B.LRU_GATE:B.LRU_GATE + 8, :], ALU.mult, after=(a, gl))]


def merge(m, L, B, io, y_m, y_l, gates):
    nc = m.nc
    two = lambda t, b: t[:, 2 * b:2 * b + 2, :]
    bank2 = lambda s: m.bank[s][:, :].rearrange("p (a n) -> p a n", a=2)
    F = L.proj[:, B.LRU_F:B.LRU_F + 8, :]
    g = m.act(nc.scalar.activation, L.proj[:, B.MERGE:B.MERGE + 16, :], L.proj[:, B.MERGE:B.MERGE + 16, :], ACT.Sigmoid, after=gates)
    done = {}

    def evict_m(b, s):
        m.computed[s].wait(m.dve)
        m.dve.wait(g)
        m.evicted[s].by(nc.vector.tensor_tensor(two(L.glu, b), bank2(s), two(L.proj[:, B.MERGE:B.MERGE + 8, :], b), ALU.mult))
        done["m", b] = m.evicted[s].done()

    def evict_l(b, s):
        m.computed[s].wait(m.dve)
        m.evicted[s].by(nc.vector.tensor_tensor(two(L.y, b), bank2(s), two(L.proj[:, B.MERGE + 8:B.MERGE + 16, :], b), ALU.mult))
        done["l", b] = m.dve(nc.vector.tensor_tensor, two(L.y, b), two(L.y, b), two(L.glu, b), ALU.add,
                             after=(m.evicted[s].done(), done["m", b]))

    def evict_out(b, s):
        m.computed[s].wait(m.dve)
        m.evicted[s].by(nc.vector.tensor_tensor(two(L.x, b), two(L.x, b), bank2(s), ALU.add))
        done["x", b] = m.evicted[s].done()

    m.project_with(L.h, lambda b: columns(io["w_branch_mlstm_2"], 0, b * 256), evict_m, after=y_m)
    m.project_with(F, lambda b: columns(io["w_branch_lru_2"], 0, b * 256), evict_l, after=y_l)
    m.project_with(L.y, lambda b: columns(io["w_out_2"], 0, b * 256), evict_out, after=[done["l", b] for b in range(4)])
    return [done["x", b] for b in range(4)]


class Peer:
    HEADS, TOP, KEYS, GROUP = 8, 16, 128, 8

    def __init__(self, m, L):
        flat = lambda t: t.rearrange("p a n -> p (a n)")
        self.u = flat(L.proj[:, 0:32, :]).rearrange("p (s d) -> p s d", s=8)
        self.v = flat(L.proj[:, 32:64, :]).rearrange("p (s d) -> p s d", s=8)
        self.h_tok = flat(L.y[:, :, :]).rearrange("p (t d) -> p t d", t=2)
        self.x_tok = flat(L.glu[:, :, :]).rearrange("p (t d) -> p t d", t=2)
        self.keys = flat(L.conv[:, 0:8, :]).rearrange("p (j n) -> p j n", n=P)
        self.scores = [flat(L.conv[:, 8 + 8 * t:16 + 8 * t, :]).rearrange("p (j n) -> p j n", n=P) for t in range(2)]
        self.pairs = flat(L.conv[:, 0:8, :]).rearrange("p (h c) -> p h c", h=8)
        self.match = flat(L.h[:, :, :]).rearrange("p (h c) -> p h c", h=8)
        self.diag = L.spare
        self.gain = flat(m.slot[0][:, 0:4, :])
        small = flat(m.slot[1][:, :, :])
        f = lambda i, n, dt=F32: (small[:, i * 128:i * 128 + n] if dt == F32 else small[:, i * 128:i * 128 + n].bitcast(dt))
        self.top = f(0, 256).rearrange("p (j k) -> p j k", j=16)
        self.top_i = f(2, 256, U32).rearrange("p (j k) -> p j k", j=16)
        self.top_f = f(4, 256).rearrange("p (j k) -> p j k", j=16)
        self.best = f(6, 128).rearrange("p (h k) -> p h k", h=8)
        self.pos = f(7, 128, U32).rearrange("p (h k) -> p h k", h=8)
        self.half = [f(8 + i, 128).rearrange("p (h k) -> p h k", h=8) for i in range(2)]
        self.half_i = [f(10 + i, 128, U32).rearrange("p (h k) -> p h k", h=8) for i in range(2)]
        self.row = [f(12 + i, 128).rearrange("p (h k) -> p h k", h=8) for i in range(2)]
        self.sum = f(14, 16)
        more = flat(m.slot[2][:, :, :])
        self.index = more[:, 0:256].bitcast(U32)
        self.gate = more[:, 256:512]
        self.counting = more[:, 512:528]
        self.counting_i = more[:, 528:544].bitcast(I32)
        self.stage = [more[:, 544 + 8 * i:552 + 8 * i].bitcast(U32) for i in range(2)]
        self.dots = more[:, 560:568]
        self.acts = more[:, 576:584]
        self.weights = more[:, 592:600]
        self.ss = more[:, 608:612]


def choose_experts(m, K, t, ready, iota):
    nc = m.nc
    sc = K.scores[t]
    v = nc.vector
    st = {}
    def best16(lists, values, top, top_i, after):
        last = {j: None for j in lists}
        for j in lists:
            last[j] = m.dve(v.max, top[:, j, 0:8], values[:, j, :], after=after)
        for j in lists:
            last[j] = m.dve(v.max_index, top_i[:, j, 0:8], top[:, j, 0:8], values[:, j, :], after=(last[j],))
        for j in lists:
            last[j] = m.dve(v.match_replace, values[:, j, :], top[:, j, 0:8], values[:, j, :], LOWEST, after=(last[j],))
        for j in lists:
            last[j] = m.dve(v.max, top[:, j, 8:16], values[:, j, :], after=(last[j],))
        for j in lists:
            last[j] = m.dve(v.max_index, top_i[:, j, 8:16], top[:, j, 8:16], values[:, j, :], after=(last[j],))
        return last[lists[-1]]
    d = best16(range(16), sc, K.top, K.top_i, ready)
    f = m.dve(v.tensor_copy, K.top_f[:, :, :], K.top_i[:, :, :], after=(d,))
    pair = lambda a: a.rearrange("p (h s) k -> p h s k", s=2)
    four = lambda a: a.rearrange("p h (a b) -> p h a b", a=16)
    rows = lambda a: a.unsqueeze(3).to_broadcast([P, 8, 16, 16])
    cols = lambda a: a.unsqueeze(2).to_broadcast([P, 8, 16, 16])
    d = m.dve(v.tensor_tensor, four(K.pairs), rows(pair(K.top)[:, :, 0, :]), cols(pair(K.top)[:, :, 1, :]), ALU.add, after=(d,))
    d = best16(range(8), K.pairs, K.best, K.pos, (d,))
    for i, (op, n) in enumerate(((ALU.logical_shift_right, 4), (ALU.bitwise_and, 15))):
        a = m.dve(v.tensor_scalar, K.half_i[i], K.pos, n, None, op, after=(d,))
        a = m.dve(v.tensor_copy, K.half[i], K.half_i[i], after=(a,))
        a = m.dve(v.tensor_tensor, four(K.match), rows(K.half[i]),
                  K.counting.unsqueeze(1).unsqueeze(1).to_broadcast([P, 8, 16, 16]), ALU.is_equal, after=(a, iota))
        a = m.dve(v.tensor_tensor, four(K.match), four(K.match), cols(pair(K.top_f)[:, :, i, :]), ALU.mult, after=(a, f))
        r = m.dve(v.tensor_reduce, K.row[i], four(K.match), AX.X, ALU.add, after=(a,))
        d = r
    a = m.dve(v.scalar_tensor_tensor, out=K.row[0], in0=K.row[0], scalar=float(K.KEYS), in1=K.row[1], op0=ALU.mult,
              op1=ALU.add, after=(r,))
    idx = m.dve(v.tensor_copy, K.index[:, t * P:(t + 1) * P].rearrange("p (h k) -> p h k", h=8), K.row[0], after=(a,))
    g = K.gate[:, t * P:(t + 1) * P].rearrange("p (h k) -> p h k", h=8)
    a = m.dve(v.tensor_tensor, g, K.best, K.best[:, :, 0:1].to_broadcast([P, 8, 16]), ALU.subtract, after=(d,))
    a = m.act(nc.scalar.activation, g, g, ACT.Exp, after=(a,))
    a = m.dve(v.tensor_reduce, K.sum[:, 0:8], g, AX.X, ALU.add, after=(a,))
    a = m.dve(v.reciprocal, K.sum[:, 8:16], K.sum[:, 0:8], after=(a,))
    a = m.dve(v.tensor_tensor, g, g, K.sum[:, 8:16].unsqueeze(2).to_broadcast([P, 8, 16]), ALU.mult, after=(a,))
    return [idx, a]


def run_experts(m, K, io, t, C, chosen):
    nc = m.nc
    G = K.GROUP
    U, V = io["peer_u_2"][0], io["peer_v_2"][0]
    for q in m.queues[:4]:
        q.wait(*chosen)
    for b in (0, 1):
        m.pe.wait(*m.read[b])
    h, x = K.h_tok[:, t, :], K.x_tok[:, t, :]

    def group(first, stage):
        C.u_used[G - 1].wait(m.pool, but=1)
        C.v_used[G - 1].wait(m.pool, but=1)
        C.staged.by(nc.gpsimd.tensor_copy(stage, K.index[:, bass.ds(first, G)]))
        C.staged.wait(m.pool)
        for table, rows, arrived, used in ((U, K.u, C.u_in, C.u_used), (V, K.v, C.v_in, C.v_used)):
            for s in range(G):
                used[s].wait(m.pool)
                nc.gpsimd.sem_inc(C.slot_free.sem, 1)
                arrived[s].by(nc.gpsimd.indirect_dma_start(
                    out=rows[:, s, :], out_offset=None, in_=table,
                    in_offset=bass.IndirectOffsetOnAxis(ap=stage[:, s:s + 1], axis=0)))
        C.gelu.wait(m.dve)
        for s in range(G):
            C.u_in[s].wait(m.dve)
            C.u_used[s].by(nc.vector.tensor_tensor_reduce(out=K.u[:, s, :], in0=K.u[:, s, :], in1=h, scale=1.0, scalar=0.0,
                                                          op0=ALU.mult, op1=ALU.add, accum_out=K.dots[:, s:s + 1]))
        C.u_used[G - 1].wait(m.act)
        C.weighed.wait(m.act)
        C.gelu.by(nc.scalar.activation(K.acts, K.dots, ACT.Gelu))
        C.gelu.wait(m.dve)
        C.diag.wait(m.dve)
        C.weighed.by(nc.vector.tensor_tensor(K.weights, K.acts, K.gate[:, bass.ds(first, G)], ALU.mult))
        C.weighed.wait(m.act)
        C.v_used[G - 1].wait(m.act)
        for s in range(G):
            ins = nc.scalar.activation(K.diag[:, s, :], m.ident[:, :], ACT.Copy, scale=K.weights[:, s:s + 1])
        C.diag.by(ins)
        C.diag.wait(m.pe)
        C.added.wait(m.pe)
        for s in range(G):
            C.v_in[s].wait(m.pe)
            for half in range(2):
                ins = nc.tensor.matmul(m.bank[half][:, :], K.diag[:, s, :], K.v[:, s, half * 512:half * 512 + 512],
                                       start=(s == 0), stop=(s == G - 1))
            C.v_used[s].by(ins)
        C.v_used[G - 1].wait(m.dve)
        C.added.wait(m.dve)
        for half in range(2):
            at = slice(half * 512, half * 512 + 512)
            ins = nc.vector.tensor_tensor(x[:, at], x[:, at], m.bank[half][:, :], ALU.add)
        C.added.by(ins)

    with rounds(nc, P // (2 * G), {c: 2 for c in C.all}) as j:
        for i in range(2):
            group(j * (2 * G) + (t * P + i * G), K.stage[i])
    return C.added.done()


class PeerCounts:
    def __init__(self, m):
        c = lambda name, unit=1: Count(m.nc, name, unit)
        G = Peer.GROUP
        self.u_in = [c(f"u_in{s}", 16) for s in range(G)]
        self.v_in = [c(f"v_in{s}", 16) for s in range(G)]
        self.u_used = [c(f"u_used{s}") for s in range(G)]
        self.v_used = [c(f"v_used{s}") for s in range(G)]
        self.staged, self.gelu, self.weighed, self.diag, self.added = (c(n) for n in ("staged", "gelu", "weighed", "diag", "added"))
        self.slot_free = c("gather_slot_free")
        self.all = [*self.u_in, *self.v_in, *self.u_used, *self.v_used, self.staged, self.gelu, self.weighed, self.diag, self.added]

    def prime(self, m):
        for c in (self.u_used + [self.gelu, self.weighed, self.added]) * 2:
            c.by(m.prime(m.nc.vector))
        for c in (self.v_used + [self.diag]) * 2:
            c.by(m.prime(m.nc.tensor))


def peer(m, L, io, C, x_done, h2):
    nc = m.nc
    K = Peer(m, L)
    xt = turn_out(m, K.x_tok, L.x, 4, after=x_done)
    ht = turn_out(m, K.h_tok, L.h, 4, after=h2)
    m.next_slot = 0
    q_in = m.project(L.h, lambda b: columns(io["peer_w_q_2"], 0, b * 256), 8, L.proj, 0, after=h2)
    view = lambda s: m.slot[s][:, :, :].rearrange("p k c -> p (k c)").rearrange("p (j e) -> p j e", e=P)
    sk = m.load_block(io["peer_sub_keys_2"][0].rearrange("h s n c -> n (h s) c"), view)
    m.loaded[sk].wait(m.pe)
    keys = []
    for i in range(4):
        m.pe.wait(*m.read[i])
        for j in range(4):
            tr = m.pe(nc.tensor.transpose, m.bank[i][:, j * P:(j + 1) * P], view(sk)[:, 4 * i + j, :], m.ident[:, :])
        c = m.act(nc.scalar.copy, K.keys[:, 4 * i:4 * i + 4, :], m.bank[i][:, :].rearrange("p (j n) -> p j n", j=4), after=(tr,))
        m.read[i] = [c]
        keys.append(c)
    m.release(sk, tr)
    scored = []
    for t in range(2):
        for i in range(4):
            b = 4 * t + i
            s = m.matmuls([(m.bank[b][:, j * P:(j + 1) * P], L.proj[:, 4 * i + j, t * P:(t + 1) * P], K.keys[:, 4 * i + j, :], True, True)
                           for j in range(4)], after=(*q_in, *keys), bank=b)
            c = m.act(nc.scalar.copy, K.scores[t][:, 4 * i:4 * i + 4, :], m.bank[b][:, :].rearrange("p (j n) -> p j n", j=4), after=(s,))
            m.read[b] = [c]
            scored.append(c)
    m.pool.wait(s)
    m.sp.wait(*keys)
    for c in m.computed:
        c.wait(m.sp)
    i = m.pool(nc.gpsimd.iota, K.counting_i, pattern=[[1, 16]], base=0, channel_multiplier=0, after=(s,))
    i = m.dve(nc.vector.tensor_copy, K.counting, K.counting_i, after=(i,))
    m.misc_in.by(nc.sync.dma_start(K.gain, io["final_norm_g_2"].unsqueeze(0).to_broadcast([P, KT * P])))
    gain = m.misc_in.done()
    C.prime(m)
    for t in range(2):
        chosen = choose_experts(m, K, t, (*scored, s, *xt, *ht), i)
        a = run_experts(m, K, io, t, C, (*chosen, *xt, *ht, s))
    for t in range(2):
        x = K.x_tok[:, t, :]
        ss, r = K.ss[:, 2 * t:2 * t + 1], K.ss[:, 2 * t + 1:2 * t + 2]
        q = m.act(nc.scalar.activation, K.h_tok[:, t, :], x, ACT.Square, accum_out=ss, after=(a,))
        q = m.dve(nc.vector.tensor_scalar, r, ss, 1.0 / (KT * P), RMS_EPS, ALU.mult, ALU.add, after=(q,))
        q = m.dve(nc.vector.reciprocal, r, r, after=(q,))
        q = m.act(nc.scalar.activation, r, r, ACT.Sqrt, after=(q,))
        q = m.dve(nc.vector.scalar_tensor_tensor, out=x, in0=x, scalar=r, in1=K.gain, op0=ALU.mult, op1=ALU.mult, after=(q, gain))
        m.sp.wait(q)
        m.misc_in.by(nc.sync.dma_start(io["out"][0, t * P:(t + 1) * P, :], x))
    m.sp.wait(m.misc_in.done())


def last_block(m, L, B, io, C):
    params = load_block_params(m, L, B, io)
    n = rms_norm(m, L.x, L.dw_w[:, 0:8], L.h, L.y, L.stat[:, :], 0, after=params)
    w = io["w_in_2"]
    gates = mlstm_gates(m, L, B, n)
    first = m.project(L.h, lambda b: columns(w, 0, b * 256), 8, L.proj, B.XM, after=n)
    rest = m.project(L.h, lambda b: columns(w, 0, b * 256 + 2064), 16, L.proj, B.XL)
    y_m = mlstm(m, L, B, io, (*first, *rest), gates)
    y_l = rg_lru(m, L, B, io, rest, y_m)
    x = merge(m, L, B, io, y_m, y_l, rest)
    h2 = rms_norm(m, L.x, L.dw_w[:, 96:104], L.h, L.y, L.stat[:, :], 0, after=x)
    peer(m, L, io, C, x, h2)


def program(nc, io):
    m = Machine(nc)
    L = Layer(m)
    B = Block(m, L)
    C = PeerCounts(m)
    m.start_phase()
    made = make_constants(m)
    rows = L.proj[:, 0:8, :].rearrange("p a b -> p (a b)").rearrange("p (t c) -> p t c", t=2)
    m.misc_in.by(nc.sync.dma_start(rows, io["x"][0].rearrange("(t p) c -> p t c", p=P)))
    turn_in(m, L.x, rows, after=(m.misc_in.done(), *made))
    m.end_phase()
    with nc.Fori(0, io["ffn1_w_in"].shape[0]) as l:
        m.start_phase()
        layer(m, L, io, l)
        m.end_phase()
    m.start_phase()
    last_block(m, L, B, io, C)


def kernel(**inputs):
    import concourse.bacc as bacc
    from concourse.bass_utils import run_bass_kernel_spmd

    nc = bacc.Bacc("TRN2", target_bir_lowering=False, num_devices=1)
    arrays, io = {}, {}
    for name, value in inputs.items():
        a = np.ascontiguousarray(value)
        arrays[f"in_{name}"] = a
        io[name] = nc.dram_tensor(f"in_{name}", a.shape, mybir.dt.from_np(a.dtype), kind="ExternalInput").ap()
    io["out"] = nc.dram_tensor("out_x", inputs["x"].shape, F32, kind="ExternalOutput").ap()
    program(nc, io)
    return run_bass_kernel_spmd(nc, [arrays], core_ids=[0]).results[0]["out_x"]
```

```python
from contextlib import ExitStack, contextmanager

import numpy as np

import concourse.bass as bass
from concourse import mybir

F32 = mybir.dt.float32
F32R = mybir.dt.float32r
I32 = mybir.dt.int32
U32 = mybir.dt.uint32
ALU = mybir.AluOpType
ACT = mybir.ActivationFunctionType
AX = mybir.AxisListType
P = 128
NT = 256
KT = 8
RMS_EPS, LN_EPS = 1e-6, 1e-5
LOWEST = -3.0e38


class Done:

    def __init__(self, sem, value):
        self.sem, self.value = sem, value


class Queue:

    def __init__(self, nc, eng, name):
        self.eng, self.sem, self.n, self.waited = eng, nc.alloc_semaphore(f"{name}_done"), 0, {}

    def wait(self, *dones):
        for d in dones:
            if d is None:
                continue
            if isinstance(d, (list, tuple)):
                self.wait(*d)
            elif self.waited.get(d.sem.num, 0) < d.value:
                self.eng.wait_ge(d.sem, d.value)
                self.waited[d.sem.num] = d.value

    def __call__(self, ins, *args, after=(), **kw):
        self.wait(*after)
        ins(*args, **kw).then_inc(self.sem, 1)
        self.n += 1
        return Done(self.sem, self.n)

    def reset(self):
        self.n, self.waited = 0, {}


class Count:

    def __init__(self, nc, name, unit=1):
        self.sem, self.unit, self.n, self.loop = nc.alloc_semaphore(name), unit, 0, None

    def by(self, ins):
        ins.then_inc(self.sem, self.unit)
        self.n += 1

    def wait(self, q, but=0):
        value = (self.n - but) * self.unit
        assert value > 0
        if self.loop is not None:
            reg, per = self.loop
            value = reg * (per * self.unit) + value
        q.eng.wait_ge(self.sem, value)

    def done(self):
        assert self.loop is None
        return Done(self.sem, self.n * self.unit)


@contextmanager
def rounds(nc, n, counts):
    start = {c: c.n for c in counts}
    with nc.Fori(0, n) as reg:
        for c, per in counts.items():
            c.loop = (reg, per)
        yield reg
        for c, per in counts.items():
            assert c.n == start[c] + per, (c.sem, c.n - start[c], per)
            c.loop = None
            c.n = start[c] + n * per


class Pair:

    def __init__(self, hi, lo, plain=None):
        self.hi, self.lo, self.plain = hi, lo, plain


class Machine:

    SLOTS = 3

    def __init__(self, nc):
        self.nc = nc
        self.pe = Queue(nc, nc.tensor, "pe")
        self.act = Queue(nc, nc.scalar, "act")
        self.dve = Queue(nc, nc.vector, "dve")
        self.pool = Queue(nc, nc.gpsimd, "pool")
        self.sp = Queue(nc, nc.sync, "sp")
        self.queues = [self.pe, self.act, self.dve, self.pool, self.sp]
        S = self.SLOTS
        self.loaded = [Count(nc, f"weights_loaded{s}", 16) for s in range(S)]
        self.hi_made = [[Count(nc, f"weights_hi{s}_{q}") for q in range(2)] for s in range(S)]
        self.lo_made = [[Count(nc, f"weights_lo{s}_{q}") for q in range(2)] for s in range(S)]
        self.computed = [Count(nc, f"weights_used{s}") for s in range(S)]
        self.evicted = [Count(nc, f"bank_evicted{s}") for s in range(S)]
        self.product = Count(nc, "ffn_product")
        self.product_hi = Count(nc, "ffn_product_hi")
        self.params_in = Count(nc, "params_in", 16)
        self.misc_in = Count(nc, "misc_in", 16)
        self.ring = [*self.loaded, *sum(self.hi_made, []), *sum(self.lo_made, []), *self.computed, *self.evicted]
        self.counts = [*self.ring, self.product, self.product_hi, self.params_in, self.misc_in]
        self.bank = [nc.alloc_psum_tensor(f"bank{b}", [P, 512], F32) for b in range(8)]
        self.read = [[] for _ in range(8)]
        self.slot, self.lo, self.hi = [], [], []
        self.slots_at = self.next_address()
        for s in range(S):
            raw, lo = self.shared((f"weights{s}", F32), (f"weights_low{s}", F32R), shape=[P, KT, 256])
            self.slot.append(raw)
            self.lo.append(lo)
            self.hi.append(self.sb(f"weights_high{s}", [P, KT, 256], F32R))
        self.next_slot = 0

    def sb(self, name, shape, dt=F32):
        return self.nc.alloc_sbuf_tensor(name, shape, dt)

    def next_address(self):
        return (self.nc.sbuf_base + 31) // 32 * 32

    def shared(self, *names, shape):
        at = self.next_address()
        return [self.sb(names[0][0], shape, names[0][1])] + \
               [self.nc.alloc_sbuf_tensor_at(n, shape, dt, offset=at) for n, dt in names[1:]]

    def pair(self, name, tiles):
        hi, hi32 = self.shared((f"{name}_hi", F32R), (f"{name}_hi_plain", F32), shape=[P, tiles, NT])
        lo, lo32 = self.shared((f"{name}_lo", F32R), (f"{name}_lo_plain", F32), shape=[P, tiles, NT])
        return Pair(hi, lo, (hi32, lo32))

    def start_phase(self):
        for q in self.queues:
            q.reset()
        self.read = [[] for _ in range(8)]
        self.next_slot = 0
        for c in self.counts:
            c.n = 0
        for s in range(self.SLOTS):
            self.computed[s].by(self.prime(self.nc.tensor))
            self.evicted[s].by(self.prime(self.nc.scalar))

    @staticmethod
    def prime(eng):
        return eng.nop()

    def end_phase(self):
        sems = [q.sem.num for q in self.queues] + [c.sem.num for c in self.counts]
        assert sorted(sems) == list(range(min(sems), max(sems) + 1)), sems
        self.nc.all_engine_barrier(sems_to_clear=range(min(sems), max(sems) + 1))

    def matmuls(self, steps, after=(), bank=None):
        self.pe.wait(*after)
        if bank is not None:
            self.pe.wait(*self.read[bank])
        for out, lhsT, rhs, start, stop in steps[:-1]:
            self.nc.tensor.matmul(out, lhsT, rhs, start=start, stop=stop)
        out, lhsT, rhs, start, stop = steps[-1]
        return self.pe(self.nc.tensor.matmul, out, lhsT, rhs, start=start, stop=stop)

    def load_block(self, src, dst=None):
        s = self.next_slot
        self.next_slot = (s + 1) % self.SLOTS
        self.computed[s].wait(self.sp)
        self.loaded[s].by(self.nc.sync.dma_start(self.slot[s][:, :, :] if dst is None else dst(s), src))
        return s

    def halves(self, t):
        return [t[:, :, q * P:(q + 1) * P] for q in range(2)]

    def split_next(self, second=None):
        s = self.next_slot
        raw, hi, lo = self.halves(self.slot[s]), self.halves(self.hi[s]), self.halves(self.lo[s])
        self.loaded[s].wait(self.act, but=-1)
        for q in range(2):
            self.hi_made[s][q].by(self.nc.scalar.copy(hi[q], raw[q]))
        for q in range(2):
            by = second if second and q == 1 else self.pool
            self.hi_made[s][q].wait(by)
            self.lo_made[s][q].by(by.eng.tensor_tensor(lo[q], raw[q], hi[q].bitcast(F32), ALU.subtract))

    def block_products(self, s, x):
        self.evicted[s].wait(self.pe)
        for m in range(2):
            self.lo_made[s][m].wait(self.pe)
            hi, lo = self.halves(self.hi[s])[m], self.halves(self.lo[s])[m]
            out = self.bank[s][:, m * NT:(m + 1) * NT]
            for k in range(KT):
                self.nc.tensor.matmul(out, hi[:, k, :], x.hi[:, k, :], start=(k == 0), stop=False)
                self.nc.tensor.matmul(out, hi[:, k, :], x.lo[:, k, :], start=False, stop=False)
                ins = self.nc.tensor.matmul(out, lo[:, k, :], x.hi[:, k, :], start=False, stop=(k == KT - 1))
        self.computed[s].by(ins)

    def release(self, s, last):
        self.pe.wait(last)
        self.computed[s].by(self.prime(self.nc.tensor))

    def settle_banks(self):
        for s in range(self.SLOTS):
            self.pe.wait(*self.read[s])
            self.read[s] = []

    def streamed(self):
        for s in range(self.SLOTS):
            self.read[s] = [self.evicted[s].done()]

    def split(self, src, pair, after=(), tiles=KT):
        out = []
        for i in range(tiles // 2):
            two = slice(2 * i, 2 * i + 2)
            hi = self.act(self.nc.scalar.copy, pair.hi[:, two, :], src[:, two, :], after=after[i])
            out.append(self.dve(self.nc.vector.tensor_tensor, pair.lo[:, two, :], src[:, two, :],
                                pair.hi[:, two, :].bitcast(F32), ALU.subtract, after=(hi,)))
        return out

    def project(self, x, block_src, n_blocks, dst, tile0, after=(), ahead=True):
        S = self.SLOTS
        self.settle_banks()
        self.pe.wait(*after)
        full = n_blocks // S if ahead or n_blocks % S else n_blocks // S - 1

        def block(n, ahead=True):
            s = self.load_block(block_src(n))
            if ahead:
                self.split_next()
            self.block_products(s, x)
            self.computed[s].wait(self.act)
            at = n * 2 + tile0
            self.evicted[s].by(self.nc.scalar.copy(
                dst[:, at:at + 2, :] if isinstance(at, int) else dst[:, bass.ds(at, 2), :],
                self.bank[s][:, :].rearrange("p (a n) -> p a n", a=2)))

        if full > 1:
            with rounds(self.nc, full, {c: 1 for c in self.ring}) as j:
                for b in range(S):
                    block(j * S + b)
        else:
            full = 0
        for b in range(full * S, n_blocks):
            block(b, ahead or b < n_blocks - 1)
        self.streamed()
        return [self.evicted[s].done() for s in range(S)]

    def project_with(self, x, block_src, evict, after=(), ahead=True):
        self.settle_banks()
        self.pe.wait(*after)
        for b in range(4):
            s = self.load_block(block_src(b))
            if ahead or b < 3:
                self.split_next()
            self.block_products(s, x)
            evict(b, s)
        self.streamed()


def columns(w, layer, col):
    if not isinstance(col, int):
        cols = bass.ds(col, 256)
    else:
        cols = slice(col, col + 256)
    return w[bass.ds(layer, 1), :, cols].rearrange("o (k p) c -> p (o k) c", p=P)


def rms_norm(m, x, gain, out, tmp, stat, bank, eps=RMS_EPS, after=()):
    nc = m.nc
    squares = []
    for i in range(4):
        two = slice(2 * i, 2 * i + 2)
        squares.append(m.act(nc.scalar.square, tmp[:, two, :], x[:, two, :], after=after))
    for k in range(KT):
        m.pe.wait(squares[k // 2])
        if k == 0:
            m.pe.wait(*m.read[bank])
        ins = nc.tensor.matmul(m.bank[bank][:, 0:NT], m.ones[:, :], tmp[:, k, :], start=(k == 0), stop=(k == KT - 1))
    ins.then_inc(m.pe.sem, 1)
    m.pe.n += 1
    summed = Done(m.pe.sem, m.pe.n)
    mean = m.dve(nc.vector.tensor_scalar, stat, m.bank[bank][:, 0:NT], 1.0 / (KT * P), eps, ALU.mult, ALU.add, after=(summed,))
    m.read[bank] = [mean]
    inv = m.dve(nc.vector.reciprocal, stat, stat, after=(mean,))
    root = m.act(nc.scalar.activation, stat, stat, ACT.Sqrt, after=(inv,))
    dones = []
    for k in range(KT):
        dones.append(m.dve(nc.vector.scalar_tensor_tensor, out=out[:, k, :], in0=x[:, k, :], scalar=gain[:, k:k + 1],
                           in1=stat, op0=ALU.mult, op1=ALU.mult, after=(root,)))
    return dones


def norm_to_pair(m, x, gain, pair, tmp, stat, bank, after=()):
    d = rms_norm(m, x, gain, tmp, tmp, stat, bank, after=after)
    return m.split(tmp, pair, after=[(d[2 * i + 1],) for i in range(KT // 2)])


def add_normed(m, x, y, gain, tmp, stat, bank, after=()):
    nc = m.nc
    normed = rms_norm(m, y, gain, y, tmp, stat, bank, after=after)
    return m.dve(nc.vector.tensor_tensor, x[:, :, :], x[:, :, :], y[:, :, :], ALU.add, after=(normed[-1],))


def ffn(m, h, w_in, w_out, layer, d_ff, gated, silu, y, after=(), ahead=True):
    nc = m.nc
    n = d_ff // 256
    m.settle_banks()
    for b in range(4, 8):
        m.pe.wait(*m.read[b])
    m.pe.wait(*after)
    bank2 = [m.bank[s][:, :].rearrange("p (a n) -> p a n", a=2) for s in range(m.SLOTS)]
    used = {}

    def gate(j):
        s = used["gate"] = m.load_block(columns(w_in, layer, j * 256))
        m.split_next(m.dve)
        m.block_products(s, h)
        m.computed[s].wait(m.act)
        if "up" in used:
            m.evicted[used["up"]].wait(m.act)
        m.evicted[s].by(nc.scalar.activation(silu[:, :, :], bank2[s], ACT.Silu))

    def up(j):
        s = used["up"] = m.load_block(columns(w_in, layer, j * 256 + d_ff))
        m.split_next(m.dve)
        m.block_products(s, h)
        m.evicted[used["gate"]].wait(m.dve)
        m.computed[s].wait(m.dve)
        m.product.by(nc.vector.tensor_tensor(silu[:, :, :], silu[:, :, :], bank2[s], ALU.mult))
        m.product.wait(m.act)
        if "out" in used:
            m.computed[used["out"]].wait(m.act)
        m.product_hi.by(nc.scalar.copy(gated.hi[:, :, :], silu[:, :, :]))
        m.product_hi.wait(m.dve)
        m.evicted[s].by(nc.vector.tensor_tensor(gated.lo[:, :, :], silu[:, :, :], gated.hi[:, :, :].bitcast(F32),
                                                ALU.subtract))

    def out(j, first=False, last=False):
        rows = w_out[bass.ds(layer, 1), bass.ds(j * 256, 256), :].rearrange("o (k p) c -> p (o k) c", p=P)
        wide = lambda t: t[:, :, :].rearrange("p (k q) c -> p k (q c)", k=2)
        s = used["out"] = m.load_block(rows, lambda s: wide(m.slot[s]))
        if ahead or not last:
            m.split_next(m.dve)
        m.evicted[used["up"]].wait(m.pe)
        for q in range(2):
            m.lo_made[s][q].wait(m.pe)
        hi, lo = wide(m.hi[s]), wide(m.lo[s])
        for k in range(2):
            for t in range(KT):
                to, at = m.bank[4 + t // 2][:, t % 2 * NT:(t % 2 + 1) * NT], slice(t * P, (t + 1) * P)
                nc.tensor.matmul(to, hi[:, k, at], gated.hi[:, k, :], start=(first and k == 0 and t % 2 == 0), stop=False,
                                 skip_group_check=True)
                nc.tensor.matmul(to, hi[:, k, at], gated.lo[:, k, :], start=False, stop=False, skip_group_check=True)
                ins = nc.tensor.matmul(to, lo[:, k, at], gated.hi[:, k, :], start=False, stop=(last and k == 1),
                                       skip_group_check=True)
        m.computed[s].by(ins)

    gate(0)
    up(0)
    gate(1)
    out(0, first=True)
    up(1)
    events = {c: 1 for c in [*m.ring, m.product, m.product_hi] if c is not m.evicted[used["out"]]}
    with rounds(nc, n - 2, events) as j:
        gate(j + 2)
        out(j + 1)
        up(j + 2)
    out(n - 1, last=True)
    m.streamed()
    dones = []
    for b in range(4):
        d = m.act(nc.scalar.copy, y[:, 2 * b:2 * b + 2, :], m.bank[4 + b][:, :].rearrange("p (a n) -> p a n", a=2),
                  after=(m.computed[used["out"]].done(),))
        m.read[4 + b] = [d]
        dones.append(d)
    return dones


def to_columns(m, rows, n_rows, cols, bank, after=()):
    nc = m.nc
    t = m.pe(nc.tensor.transpose, m.bank[bank][:, 0:n_rows], rows[0:n_rows, :], m.ident[0:n_rows, 0:n_rows],
             after=(*after, *m.read[bank]))
    d = m.dve(nc.vector.tensor_copy, cols, m.bank[bank][:, 0:n_rows], after=(t,))
    m.read[bank] = [d]
    return d


def softplus(m, x, out, a, b, after=()):
    nc = m.nc
    d = m.dve(nc.vector.scalar_tensor_tensor, out=a, in0=x, scalar=-1.0, in1=x, op0=ALU.mult, op1=ALU.max, after=after)
    e = m.act(nc.scalar.activation, a, a, ACT.Exp, scale=-1.0, after=(d,))
    d = m.dve(nc.vector.tensor_scalar, b, a, 2.0, None, ALU.add, after=(e,))
    d = m.dve(nc.vector.reciprocal, b, b, after=(d,))
    z = m.dve(nc.vector.tensor_tensor, a, a, b, ALU.mult, after=(d,))
    d = m.dve(nc.vector.tensor_tensor, b, a, a, ALU.mult, after=(z,))
    d = m.dve(nc.vector.tensor_scalar, out, b, 2.0 / 17, None, ALU.mult, after=(d,))
    for k in range(7, 0, -1):
        d = m.dve(nc.vector.scalar_tensor_tensor, out=out, in0=out, scalar=2.0 / (2 * k + 1), in1=b,
                  op0=ALU.add, op1=ALU.mult, after=(d,))
    d = m.dve(nc.vector.scalar_tensor_tensor, out=out, in0=out, scalar=2.0, in1=a, op0=ALU.add, op1=ALU.mult, after=(d,))
    return m.dve(nc.vector.scalar_tensor_tensor, out=out, in0=x, scalar=0.0, in1=out, op0=ALU.max, op1=ALU.add, after=(d,))


def make_constants(m):
    nc = m.nc
    m.ones = m.sb("ones", [P, P])
    m.ident = m.sb("ident", [P, P])
    m.upto = m.sb("mask_s_le_t", [P, P])
    m.from_ = m.sb("mask_s_ge_t", [P, P])
    m.level = m.sb("level_masks", [P, 7, P])
    m.onehot = m.sb("onehot_columns", [P, 16, 16])
    m.pick = m.sb("row_pickers", [16, 16, P])
    xor = m.slot[0][:, 0, 0:P].bitcast(I32)
    srow = m.slot[0][:, 0, P:2 * P].bitcast(I32)
    tmp = m.slot[0][:, 1, 0:P].bitcast(I32)
    ones = m.pool(nc.gpsimd.memset, m.ones[:, :], 1.0)
    big = m.pool(nc.gpsimd.memset, m.onehot[:, :, :], 1.0)
    big2 = m.pool(nc.gpsimd.memset, m.pick[:, :, :], 1.0)
    out = [
        m.pool(nc.gpsimd.affine_select, out=m.ident[:, :], in_=m.ones[:, :], compare_op=ALU.is_equal, fill=0.0,
               base=0, pattern=[[-1, P]], channel_multiplier=1, after=(ones,)),
        m.pool(nc.gpsimd.affine_select, out=m.upto[:, :], in_=m.ones[:, :], compare_op=ALU.is_ge, fill=0.0,
               base=0, pattern=[[1, P]], channel_multiplier=-1),
        m.pool(nc.gpsimd.affine_select, out=m.from_[:, :], in_=m.ones[:, :], compare_op=ALU.is_ge, fill=0.0,
               base=0, pattern=[[-1, P]], channel_multiplier=1),
        m.pool(nc.gpsimd.affine_select, out=m.onehot[:, :, :], in_=m.onehot[:, :, :], compare_op=ALU.is_equal, fill=0.0,
               base=0, pattern=[[1, 16], [-1, 16]], channel_multiplier=0, after=(big,)),
        m.pool(nc.gpsimd.affine_select, out=m.pick[:, :, :], in_=m.pick[:, :, :], compare_op=ALU.is_equal, fill=0.0,
               base=0, pattern=[[-1, 16], [0, P]], channel_multiplier=1, after=(big2,)),
    ]
    s = m.pool(nc.gpsimd.iota, xor, pattern=[[1, P]], base=0, channel_multiplier=0)
    t = m.pool(nc.gpsimd.iota, srow, pattern=[[0, P]], base=0, channel_multiplier=1)
    x = m.dve(nc.vector.tensor_tensor, xor, xor, srow, ALU.bitwise_xor, after=(s, t))
    d = None
    for l in range(7):
        d = m.dve(nc.vector.tensor_scalar, tmp, xor, l, None, ALU.logical_shift_right, after=(x, d))
        d = m.dve(nc.vector.tensor_scalar, m.level[:, l, :], tmp, 1.0, None, ALU.is_equal, after=(d,))
        d = m.dve(nc.vector.tensor_tensor, m.level[:, l, :], m.level[:, l, :], m.upto[:, :], ALU.mult, after=(d, out[1]))
    return out + [d]


class Layer:

    GLU_A, GLU_G, QKV, Z, GATES, TILES = 0, 8, 16, 40, 48, 64
    NORMS = ["ffn1_norm_pre", "ffn1_norm_post", "mix_norm_pre", "mix_norm_post", "ffn2_norm_pre", "ffn2_norm_post",
             "cnv_dw_b", "cnv_ln_g", "cnv_ln_b", "cnv_b_o"]

    def __init__(self, m):
        sb = m.sb
        self.x, self.y = (sb(n, [P, KT, NT]) for n in ("residual", "branch"))
        self.stat = sb("stat", [P, NT])
        self.proj = sb("proj", [P, self.TILES, NT])
        conv_at = m.next_address()
        self.conv = sb("gdn_conv", [P, 24, NT])
        at = lambda name, tile: m.nc.alloc_sbuf_tensor_at(name, [P, KT, NT], F32R, offset=conv_at + tile * NT * 4)
        self.operand = m.pair("operand", KT)
        self.operand2 = Pair(at("operand2_hi", 8), at("operand2_lo", 16))
        self.silu = sb("ffn_silu", [P, 2, NT])
        self.gated = m.pair("ffn_gated", 2)
        self.rows = sb("param_rows", [P, 4, P])
        self.cols = sb("param_cols", [P, 97])
        self.gdn_w = sb("gdn_conv_cols", [P, 4 * 24])
        self.dw_w = sb("cnv_dw_cols", [P, 31 * KT])
        self.w_ab = sb("w_beta_a", [P, KT, 16])
        self.head = sb("head_params", [8, 4])
        self.hrow = sb("head_rows", [8, 6, NT])
        self.tok = sb("token_cols", [P, 2, 4, 8])
        self.q2 = [sb(f"q_decayed{g}", [P, 4, P]) for g in range(2)]
        self.norm16 = sb("row_norms", [16, NT])
        eight = lambda t, a: t[:, a:a + 4, :].rearrange("p a (b n) -> p (a b) n", b=2)
        hi, lo = self.operand.plain
        names = ["D", "A", "KB", "T", "TT", "QK", "VB", "KX"]
        homes = [[(self.proj, 4 * i) for i in range(8)],
                 [(self.proj, 32), (self.proj, 36), (hi, 0), (hi, 4), (lo, 0), (lo, 4), (self.y, 0), (self.y, 4)]]
        self.delta = [{n: eight(*at) for n, at in zip(names, home)} for home in homes]


def load_layer_params(m, L, io, l):
    nc = m.nc
    one = lambda a: a[bass.ds(l, 1), :].rearrange("o (k c) -> (o k) c", c=P)
    sp = nc.sync
    m.params_in.by(sp.dma_start(L.w_ab[:, :, :], io["mix_w_in"][bass.ds(l, 1), :, 4096:4112].rearrange(
        "o (k p) c -> p (o k) c", p=P)))
    for i, name in enumerate(L.NORMS):
        m.params_in.by(sp.dma_start(L.rows[8 * i:8 * i + 8, 0, :], one(io[name])))
    m.params_in.by(sp.dma_start(L.rows[80:96, 0, :], one(io["cnv_pw1_b"])))
    m.params_in.by(sp.dma_start(L.rows[96:97, 0, :], one(io["gdn_norm_w"])))
    m.params_in.by(sp.dma_start(L.rows[0:96, 1, :], io["gdn_conv_w"][bass.ds(l, 1), :, :].rearrange(
        "o t (k c) -> (o t k) c", c=P)))
    for i, (a, b) in enumerate(((0, 16), (16, 31))):
        m.params_in.by(sp.dma_start(L.rows[0:(b - a) * KT, 2 + i, :], io["cnv_dw_w"][bass.ds(l, 1), a:b, :].rearrange(
            "o t (k c) -> (o t k) c", c=P)))
    m.params_in.by(sp.dma_start(L.head[:, 0:1], io["gdn_a_log"][bass.ds(l, 1), :].rearrange("o h -> h o")))
    m.params_in.by(sp.dma_start(L.head[:, 1:2], io["gdn_dt_bias"][bass.ds(l, 1), :].rearrange("o h -> h o")))
    there = m.params_in.done()
    d = [to_columns(m, L.rows[:, 0, :], 97, L.cols[:, :], 4, after=(there,)),
         to_columns(m, L.rows[:, 1, :], 96, L.gdn_w[:, :], 5, after=(there,)),
         to_columns(m, L.rows[:, 2, :], 128, L.dw_w[:, 0:128], 6, after=(there,)),
         to_columns(m, L.rows[:, 3, :], 120, L.dw_w[:, 128:248], 7, after=(there,))]
    d.append(m.dve(nc.vector.tensor_scalar, L.cols[:, 8:16], L.cols[:, 8:16], 0.5, None, ALU.mult, after=(d[0],)))
    d.append(m.dve(nc.vector.tensor_scalar, L.cols[:, 40:48], L.cols[:, 40:48], 0.5, None, ALU.mult, after=(d[0],)))
    return d[-1]


def depthwise(m, src, dst, weight, taps, centre, tiles, bias=None, after=()):
    nc = m.nc
    last = {}
    order = [centre] + [k for k in range(taps) if k != centre]
    for k in order:
        s = k - centre
        for c in tiles:
            w = weight(k, c)
            if k == centre:
                if bias is None:
                    last[c] = m.dve(nc.vector.tensor_scalar, dst(c), src(c), w, None, ALU.mult, after=after)
                else:
                    last[c] = m.dve(nc.vector.tensor_scalar, dst(c), src(c), w, bias(c), ALU.mult, ALU.add, after=after)
                continue
            to, frm = (slice(-s, NT), slice(0, NT + s)) if s < 0 else (slice(0, NT - s), slice(s, NT))
            last[c] = m.dve(nc.vector.scalar_tensor_tensor, out=dst(c)[:, to], in0=src(c)[:, frm], scalar=w,
                            in1=dst(c)[:, to], op0=ALU.mult, op1=ALU.add, after=(last[c],))
    return last


def head_sums(m, squares, n_rows, out, bank, eps, scale=1.0, per_row=1, after=()):
    nc = m.nc
    steps = []
    n = n_rows * per_row
    for i in range(n):
        steps.append((m.bank[bank][0:n_rows, 0:NT], m.onehot[:, i // per_row, 0:n_rows], squares(i), i == 0, i == n - 1))
    s = m.matmuls(steps, after=after, bank=bank)
    d = m.dve(nc.vector.tensor_scalar, out, m.bank[bank][0:n_rows, 0:NT], scale, eps, ALU.mult, ALU.add, after=(s,))
    m.read[bank] = [d]
    d = m.dve(nc.vector.reciprocal, out, out, after=(d,))
    return m.act(nc.scalar.activation, out, out, ACT.Sqrt, after=(d,))


def spread_row(m, bank, half, rows, n_rows, j, after=()):
    return m.matmuls([(m.bank[bank][:, half * NT:(half + 1) * NT], m.pick[0:n_rows, j, :], rows, True, True)],
                     after=after, bank=bank)


def conformer(m, L, glu_in):
    nc = m.nc
    proj = L.proj
    for k in range(KT):
        s = m.act(nc.scalar.activation, proj[:, L.GLU_G + k, :], proj[:, L.GLU_G + k, :], ACT.Sigmoid,
                  bias=L.cols[:, 88 + k:89 + k], after=glu_in)
        d = m.dve(nc.vector.scalar_tensor_tensor, out=proj[:, L.GLU_G + k, :], in0=proj[:, L.GLU_A + k, :],
                  scalar=L.cols[:, 80 + k:81 + k], in1=proj[:, L.GLU_G + k, :], op0=ALU.add, op1=ALU.mult, after=(s,))
    return depthwise(m, lambda c: proj[:, L.GLU_G + c, :], lambda c: proj[:, L.GLU_A + c, :],
                     lambda k, c: L.dw_w[:, 8 * k + c:8 * k + c + 1], 31, 30, range(KT),
                     bias=lambda c: L.cols[:, 48 + c:49 + c], after=(d,))


def conformer_norm(m, L, conv_done, bank):
    nc = m.nc
    last = [conv_done[c] for c in range(KT)]
    glu, tmp = (L.proj[:, t:t + KT, :] for t in (L.GLU_A, L.GLU_G))
    wide = lambda a: a.unsqueeze(1).to_broadcast([P, KT, NT])
    s = m.matmuls([(m.bank[bank][:, 0:NT], m.ones[:, :], glu[:, k, :], k == 0, k == KT - 1) for k in range(KT)],
                  after=last, bank=bank)
    mean = m.act(nc.scalar.mul, L.stat[:, :], m.bank[bank][:, 0:NT], 1.0 / (KT * P), after=(s,))
    m.read[bank] = [mean]
    c = m.dve(nc.vector.tensor_tensor, glu[:, :, :], glu[:, :, :], wide(L.stat[:, :]), ALU.subtract, after=(mean,))
    sq = m.act(nc.scalar.square, tmp[:, 0:KT, :], glu[:, :, :], after=(c,))
    s = m.matmuls([(m.bank[bank][:, 0:NT], m.ones[:, :], tmp[:, k, :], k == 0, k == KT - 1) for k in range(KT)],
                  after=(sq,), bank=bank)
    v = m.dve(nc.vector.tensor_scalar, L.stat[:, :], m.bank[bank][:, 0:NT], 1.0 / (KT * P), LN_EPS, ALU.mult, ALU.add, after=(s,))
    m.read[bank] = [v]
    v = m.dve(nc.vector.reciprocal, L.stat[:, :], L.stat[:, :], after=(v,))
    v = m.act(nc.scalar.activation, L.stat[:, :], L.stat[:, :], ACT.Sqrt, after=(v,))
    v = m.dve(nc.vector.tensor_tensor, glu[:, :, :], glu[:, :, :], wide(L.stat[:, :]), ALU.mult, after=(v,))
    return [m.act(nc.scalar.activation, glu[:, k, :], glu[:, k, :], ACT.Silu, bias=L.cols[:, 64 + k:65 + k],
                  scale=L.cols[:, 56 + k:57 + k], after=(v,)) for k in range(KT)]


def head_scalars(m, L, h, after):
    nc = m.nc
    hrow, head, b = L.hrow, L.head, 4
    s = m.matmuls([(m.bank[b][0:8, i * NT:(i + 1) * NT], L.w_ab[:, k, 8 * i:8 * i + 8], h[:, k, :], k == 0, k == KT - 1)
                   for i in range(2) for k in range(KT)], after=(*after, m.params_in.done()), bank=b)
    beta = m.act(nc.scalar.activation, hrow[:, 0, :], m.bank[b][0:8, 0:NT], ACT.Sigmoid, after=(s,))
    e = m.act(nc.scalar.activation, head[:, 2:3], head[:, 0:1], ACT.Exp, after=(m.params_in.done(),))
    a = m.dve(nc.vector.tensor_scalar, hrow[:, 3, :], m.bank[b][0:8, NT:2 * NT], head[:, 1:2], None, ALU.add, after=(beta,))
    m.read[b] = [beta, a]
    sp = softplus(m, hrow[:, 3, :], hrow[:, 1, :], hrow[:, 4, :], hrow[:, 5, :], after=(a,))
    g = m.dve(nc.vector.tensor_scalar, hrow[:, 1, :], hrow[:, 1, :], head[:, 2:3], -1.0, ALU.mult, ALU.mult, after=(sp, e))
    one = m.dve(nc.vector.memset, hrow[:, 4, :], 1.0, after=(sp,))
    for c in range(2):
        at = slice(c * P, (c + 1) * P)
        G = m.dve(nc.vector.tensor_tensor_scan, hrow[:, 2, at], hrow[:, 4, at], hrow[:, 1, at], 0.0, ALU.mult, ALU.add,
                  after=(g, one))
    b = 5
    m.pe.wait(*m.read[b])
    for c in range(2):
        for i, r in enumerate((0, 2)):
            t = m.pe(nc.tensor.transpose, m.bank[b][:, (2 * c + i) * 8:(2 * c + i) * 8 + 8],
                     hrow[:, r, c * P:(c + 1) * P], m.ident[0:8, 0:8], after=(G, beta))
    cp = m.dve(nc.vector.tensor_copy, L.tok[:, :, 0:2, :],
               m.bank[b][:, 0:32].rearrange("p (c i h) -> p c i h", c=2, i=2), after=(t,))
    m.read[b] = [cp]
    x = m.act(nc.scalar.activation, L.tok[:, 1, 3, :], L.tok[:, 1, 1, :], ACT.Exp, after=(cp,))
    d = m.dve(nc.vector.tensor_tensor, L.tok[:, 1, 2, :], L.tok[:, 1, 0, :], L.tok[:, 1, 3, :], ALU.mult, after=(x,))
    return G, d


def delta_rule(m, L, taps_done, row_G, tok_cols, projected):
    nc = m.nc
    conv, proj, tok = L.conv, L.proj, L.tok
    silu = {}
    for i in range(6):
        four = slice(4 * i, 4 * i + 4)
        silu[i] = m.act(nc.scalar.activation, conv[:, four, :], conv[:, four, :], ACT.Silu,
                        after=[taps_done[c] for c in range(4 * i, 4 * i + 4)])
    sq = [m.act(nc.scalar.square, proj[:, L.QKV + 4 * i:L.QKV + 4 * i + 4, :], conv[:, 4 * i:4 * i + 4, :],
                after=(silu[i], taps_done[23])) for i in range(4)]
    n = head_sums(m, lambda i: proj[:, L.QKV + i, :], 16, L.norm16[:, :], 6, 1e-6, after=sq)
    kv = {}
    for i in range(8):
        b = i % 4
        for half in range(2):
            s = spread_row(m, b, half, L.norm16[:, :], 16, 2 * i + half, after=(n,) if half == 0 else ())
        two = slice(2 * i, 2 * i + 2)
        kv[i] = m.dve(nc.vector.scalar_tensor_tensor, out=conv[:, two, :], in0=conv[:, two, :],
                      scalar=P ** -0.5 if i < 4 else 1.0,
                      in1=m.bank[b][:, :].rearrange("p (a n) -> p a n", a=2), op0=ALU.mult, op1=ALU.mult, after=(s,))
        m.read[b] = [kv[i]]
    qk_ready = [kv[7], silu[5], *sq, *projected]

    buf = L.delta
    m4 = lambda b: m.bank[b][:, :].rearrange("p (h n) -> p h n", h=4)
    ch = lambda t, c: t[:, 4 * c:4 * c + 4, :]
    head = lambda i, g: slice(8 * i + 4 * g, 8 * i + 4 * g + 4)
    D = [{} for _ in range(2)]

    for g in range(2):
        B, r = buf[g], D[g]
        b0 = 4 * g
        for i in range(4):
            s = spread_row(m, b0 + i // 2, i % 2, L.hrow[:, 2, :], 8, 4 * g + i, after=(row_G, *qk_ready))
            s2 = spread_row(m, b0 + 2 + i // 2, i % 2, L.hrow[:, 0, :], 8, 4 * g + i)
        for i in range(4):
            h = 4 * g + i
            G = m.bank[b0 + i // 2][:, (i % 2) * NT:(i % 2 + 1) * NT]
            for c in range(2):
                dd = m.dve(nc.vector.tensor_scalar, B["D"][:, 4 * c + i, :], G[:, c * P:(c + 1) * P],
                           tok[:, c, 1, h:h + 1], 0.0, ALU.subtract, ALU.min, after=(s, tok_cols))
            dl = m.dve(nc.vector.tensor_tensor, tok[:, 0, 2, h:h + 1], G[:, P - 1:P], tok[:, 0, 1, h:h + 1], ALU.subtract)
        for i in range(4):
            G = m.bank[b0 + i // 2][:, (i % 2) * NT:(i % 2 + 1) * NT]
            ge = m.act(nc.scalar.activation, L.q2[g][:, i, :], G[:, P:2 * P], ACT.Exp, after=(dl,))
        r["end"] = m.act(nc.scalar.activation, tok[:, 0, 3, 4 * g:4 * g + 4], tok[:, 0, 2, 4 * g:4 * g + 4], ACT.Exp, after=(dl,))
        r["E"] = m.act(nc.scalar.activation, B["D"], B["D"], ACT.Exp, after=(dd,))
        for i in range(2):
            kb = m.dve(nc.vector.tensor_tensor, B["KB"].rearrange("p (h c) n -> p h (c n)", c=2)[:, 2 * i:2 * i + 2, :],
                       conv[:, 8 + 4 * g + 2 * i:8 + 4 * g + 2 * i + 2, :],
                       m.bank[b0 + 2 + i][:, :].rearrange("p (a n) -> p a n", a=2), ALU.mult, after=(s2,))
        r["q2"] = m.dve(nc.vector.tensor_tensor, L.q2[g][:, :, :], L.q2[g][:, :, :], conv[:, head(0, g), P:2 * P], ALU.mult, after=(ge,))
        r["D"] = m.dve(nc.vector.tensor_tensor, B["D"], B["D"], m.upto[:, :].unsqueeze(1).to_broadcast([P, 8, P]),
                       ALU.mult, after=(r["E"],))
        r["kb"] = kb
        for i in range(4):
            m.read[b0 + i] = [dd, ge, dl, kb]

    for g in range(2):
        B, r, b0 = buf[g], D[g], 4 * g
        KB = B["KB"].rearrange("p (h c) n -> p h c n", c=2)
        for c in range(2):
            steps = [(m4(b0 + c)[:, i, :], conv[:, 8 + 4 * g + i, c * P:(c + 1) * P], KB[:, i, c, :], True, True) for i in range(4)]
            a = m.matmuls(steps, after=(r["kb"],), bank=b0 + c)
            steps = [(m4(b0 + 2 + c)[:, i, :], conv[:, 8 + 4 * g + i, c * P:(c + 1) * P],
                      conv[:, 4 * g + i, c * P:(c + 1) * P], True, True) for i in range(4)]
            q = m.matmuls(steps, bank=b0 + 2 + c)
            r["A", c] = m.dve(nc.vector.tensor_tensor, ch(B["A"], c), m4(b0 + c), ch(B["D"], c), ALU.mult, after=(a, r["D"]))
            r["QK", c] = m.dve(nc.vector.tensor_tensor, ch(B["QK"], c), m4(b0 + 2 + c), ch(B["D"], c), ALU.mult, after=(q,))
            m.read[b0 + c] = [r["A", c]]
            m.read[b0 + 2 + c] = [r["QK", c]]

    for g in range(2):
        B, r, b0 = buf[g], D[g], 4 * g
        for c in range(2):
            for i, what in ((2, 0), (1, 2)):
                b = b0 + c + what
                m.pe.wait(*m.read[b])
                for j in range(4):
                    t = m.pe(nc.tensor.transpose, m4(b)[:, j, :], conv[:, 8 * i + 4 * g + j, c * P:(c + 1) * P], m.ident[:, :])
                for j in range(4):
                    h = 4 * g + j
                    if i == 2:
                        dst, f = B["VB"], tok[:, c, 0, h:h + 1]
                    else:
                        dst, f = B["KX"], tok[:, c, 3 if c == 0 else 2, h:h + 1]
                    cp = m.act(nc.scalar.activation, dst[:, 4 * c + j, :], m4(b)[:, j, :], ACT.Copy, scale=f,
                               after=(t, r["end"], tok_cols))
                m.read[b] = [cp]
        r["tok"] = cp

    eye = m.ident[:, :].unsqueeze(1).to_broadcast([P, 4, P])
    for l in range(7):
        mask = m.level[:, l, :].unsqueeze(1).to_broadcast([P, 4, P])
        for g in range(2):
            B, r, b0 = buf[g], D[g], 4 * g
            for c in range(2):
                r["L", c] = m.dve(nc.vector.tensor_tensor, ch(B["KB"], c), ch(B["A"], c), mask, ALU.mult,
                                  after=(r["A", 1], r.get(("M", c)), r.get(("TT", c))))
        for g in range(2):
            B, r, b0 = buf[g], D[g], 4 * g
            for c in range(2):
                pr = range(4 * c, 4 * c + 4)
                mm = m.matmuls([(m4(b0 + c)[:, p % 4, :], B["KB"][:, p, :], m.ident[:, :] if l == 0 else B["T"][:, p, :],
                                 True, True) for p in pr], after=(r["L", c], r.get(("T", c))), bank=b0 + c)
                if l == 0:
                    r["T", c] = m.dve(nc.vector.tensor_tensor, ch(B["T"], c), eye, m4(b0 + c), ALU.subtract, after=(mm,))
                    r["TT", c] = m.dve(nc.vector.tensor_tensor, ch(B["TT"], c), eye, ch(B["KB"], c), ALU.subtract,
                                       after=(r["L", c],))
                    m.read[b0 + c] = [r["T", c]]
                    r["M", c] = mm
                    continue
                cp = m.act(nc.scalar.copy, ch(B["D"], c), m4(b0 + c), after=(mm, r["QK", c], r.get(("TTp", c))))
                m.read[b0 + c] = [cp]
                r["M", c], r["Mc", c] = mm, cp
        if l == 0:
            continue
        for g in range(2):
            B, r, b0 = buf[g], D[g], 4 * g
            for c in range(2):
                pr = range(4 * c, 4 * c + 4)
                if l < 6:
                    r["Tp", c] = m.matmuls([(m4(b0 + 2 + c)[:, p % 4, :], B["TT"][:, p, :], B["D"][:, p, :], True, True)
                                            for p in pr], after=(r["Mc", c], r["TT", c]), bank=b0 + 2 + c)
                r["TTp", c] = m.matmuls([(m4(b0 + c)[:, p % 4, :], B["D"][:, p, :], B["TT"][:, p, :], True, True)
                                         for p in pr], after=(r["Mc", c], r["TT", c]), bank=b0 + c)
                if l < 6:
                    r["T", c] = m.dve(nc.vector.tensor_tensor, ch(B["T"], c), ch(B["T"], c), m4(b0 + 2 + c), ALU.subtract,
                                      after=(r["Tp", c],))
                    m.read[b0 + 2 + c] = [r["T", c]]
                r["TT", c] = m.dve(nc.vector.tensor_tensor, ch(B["TT"], c), ch(B["TT"], c), m4(b0 + c), ALU.subtract,
                                   after=(r["TTp", c],))
                m.read[b0 + c] = [r["TT", c]]

    done = []
    for g in range(2):
        B, r, b0 = buf[g], D[g], 4 * g
        W, S, V = B["T"][:, 0:4, :], B["T"][:, 4:8, :], B["A"]
        r["v0p"] = m.matmuls([(m4(b0)[:, i, :], B["TT"][:, i, :], B["VB"][:, i, :], True, True) for i in range(4)],
                             after=(r["TT", 0], r["tok"]), bank=b0)
        wp = m.matmuls([(m4(b0 + 1)[:, i, :], B["KX"][:, 4 + i, :], B["TT"][:, 4 + i, :], True, True) for i in range(4)],
                       after=(r["TT", 1],), bank=b0 + 1)
        r["v0"] = m.act(nc.scalar.copy, V[:, 0:4, :], m4(b0), after=(r["v0p"],))
        r["w"] = m.act(nc.scalar.mul, W, m4(b0 + 1), -1.0, after=(wp,))
        m.read[b0], m.read[b0 + 1] = [r["v0"]], [r["w"]]
    for g in range(2):
        B, r, b0 = buf[g], D[g], 4 * g
        W, S, V = B["T"][:, 0:4, :], B["T"][:, 4:8, :], B["A"]
        s = m.matmuls([(m4(b0 + 2)[:, i, :], B["KX"][:, i, :], V[:, i, :], True, True) for i in range(4)],
                      after=(r["v0"],), bank=b0 + 2)
        r["S"] = m.act(nc.scalar.copy, S, m4(b0 + 2), after=(s,))
        m.read[b0 + 2] = [r["S"]]
    for g in range(2):
        B, r, b0 = buf[g], D[g], 4 * g
        W, S, V = B["T"][:, 0:4, :], B["T"][:, 4:8, :], B["A"]
        steps = []
        for i in range(4):
            steps.append((m4(b0 + 3)[:, i, :], B["TT"][:, 4 + i, :], B["VB"][:, 4 + i, :], True, False))
            steps.append((m4(b0 + 3)[:, i, :], W[:, i, :], S[:, i, :], False, True))
        v = m.matmuls(steps, after=(r["S"], r["w"]), bank=b0 + 3)
        r["v1"] = m.act(nc.scalar.copy, V[:, 4:8, :], m4(b0 + 3), after=(v,))
        m.read[b0 + 3] = [r["v1"]]
    for g in range(2):
        B, r, b0 = buf[g], D[g], 4 * g
        W, S, V = B["T"][:, 0:4, :], B["T"][:, 4:8, :], B["A"]
        o0 = m.matmuls([(m4(b0)[:, i, :], V[:, i, :], B["QK"][:, i, :], True, True) for i in range(4)], bank=b0)
        steps = []
        for i in range(4):
            steps.append((m4(b0 + 1)[:, i, :], S[:, i, :], L.q2[g][:, i, :], True, False))
            steps.append((m4(b0 + 1)[:, i, :], V[:, 4 + i, :], B["QK"][:, 4 + i, :], False, True))
        o1 = m.matmuls(steps, after=(r["v1"], r["q2"]), bank=b0 + 1)
        c0 = m.act(nc.scalar.copy, conv[:, head(0, g), 0:P], m4(b0), after=(o0,))
        c1 = m.act(nc.scalar.copy, conv[:, head(0, g), P:NT], m4(b0 + 1), after=(o1,))
        m.read[b0], m.read[b0 + 1] = [c0], [c1]
        done += [c0, c1]

    sq = m.act(nc.scalar.square, conv[:, 8:16, :], conv[:, 0:8, :], after=done)
    n = head_sums(m, lambda i: conv[:, 8 + i, :], 8, L.norm16[0:8, :], 2, RMS_EPS, scale=1.0 / P, after=(sq,))
    z = m.act(nc.scalar.activation, proj[:, L.Z:L.Z + 8, :], proj[:, L.Z:L.Z + 8, :], ACT.Silu)
    out = []
    for i in range(4):
        for half in range(2):
            s = spread_row(m, 4 + i, half, L.norm16[0:8, :], 8, 2 * i + half, after=(n,))
        two = slice(2 * i, 2 * i + 2)
        d = m.dve(nc.vector.scalar_tensor_tensor, out=conv[:, two, :], in0=conv[:, two, :], scalar=L.cols[:, 96:97],
                  in1=m.bank[4 + i][:, :].rearrange("p (a n) -> p a n", a=2), op0=ALU.mult, op1=ALU.mult, after=(s,))
        m.read[4 + i] = [d]
        out.append(m.dve(nc.vector.tensor_tensor, conv[:, two, :], conv[:, two, :], proj[:, L.Z + 2 * i:L.Z + 2 * i + 2, :],
                         ALU.mult, after=(d, z)))
    return out


def mixer(m, L, io, l, normed):
    nc = m.nc
    w = io["mix_w_in"]
    proj, conv = L.proj, L.conv
    x = L.operand
    G, tok_cols = head_scalars(m, L, L.y, normed)
    glu_in = m.project(x, lambda b: columns(w, l, b * 256 + 4112), 8, proj, L.GLU_A, after=normed)
    conv_done = conformer(m, L, glu_in)
    qkv_in = m.project(x, lambda b: columns(w, l, b * 256), 12, proj, L.QKV)
    taps_done = depthwise(m, lambda c: proj[:, L.QKV + c, :], lambda c: conv[:, c, :],
                          lambda k, c: L.gdn_w[:, 24 * k + c:24 * k + c + 1], 4, 3, range(24), after=qkv_in)
    m.project(x, lambda b: columns(w, l, b * 256 + 3072), 4, proj, L.Z)
    gates_in = m.project(x, lambda b: columns(w, l, b * 256 + 6160), 8, proj, L.GATES)
    conf = conformer_norm(m, L, conv_done, 7)
    gate = m.act(nc.scalar.activation, proj[:, L.GATES:L.GATES + 16, :], proj[:, L.GATES:L.GATES + 16, :], ACT.Sigmoid,
                 after=gates_in)

    two = lambda t, b: t[:, 2 * b:2 * b + 2, :]
    bank2 = lambda s: m.bank[s][:, :].rearrange("p (a n) -> p a n", a=2)
    branch = {}

    def evict_conf(b, s):
        m.computed[s].wait(m.dve)
        m.dve.wait(gate)
        for i in range(2):
            t = 2 * b + i
            ins = nc.vector.scalar_tensor_tensor(out=proj[:, L.GATES + 8 + t, :],
                                                 in0=m.bank[s][:, i * NT:(i + 1) * NT], scalar=L.cols[:, 72 + t:73 + t],
                                                 in1=proj[:, L.GATES + 8 + t, :], op0=ALU.add, op1=ALU.mult)
        m.evicted[s].by(ins)

    def evict_gdn(b, s):
        m.computed[s].wait(m.dve)
        m.evicted[s].by(nc.vector.tensor_tensor(two(L.y, b), bank2(s), proj[:, L.GATES + 2 * b:L.GATES + 2 * b + 2, :],
                                                ALU.mult))
        branch[b] = m.dve(nc.vector.tensor_tensor, two(L.y, b), two(L.y, b),
                          proj[:, L.GATES + 8 + 2 * b:L.GATES + 10 + 2 * b, :], ALU.add, after=(m.evicted[s].done(),))

    def evict_out(b, s):
        m.computed[s].wait(m.act)
        m.evicted[s].by(nc.scalar.copy(two(L.y, b), bank2(s)))
        branch["out", b] = m.evicted[s].done()

    conf = m.split(proj[:, L.GLU_A:L.GLU_A + 8, :], x, after=[conf[2 * i:2 * i + 2] for i in range(4)])
    m.project_with(x, lambda b: columns(io["cnv_w_o"], l, b * 256), evict_conf, after=conf)
    o = delta_rule(m, L, taps_done, G, tok_cols, gates_in)
    o = m.split(conv, L.operand2, after=[(o[i],) for i in range(4)])
    m.project_with(L.operand2, lambda b: columns(io["gdn_w_o"], l, b * 256), evict_gdn, after=o)
    y = m.split(L.y, x, after=[(branch[b],) for b in range(4)])
    m.project_with(x, lambda b: columns(io["mix_w_out"], l, b * 256), evict_out, after=y)
    return [branch["out", b] for b in range(4)]


def layer(m, L, io, l):
    d_ff = io["ffn1_w_out"].shape[1]
    g = lambda i: L.cols[:, 8 * i:8 * i + 8]
    stat, scratch = L.stat[:, :], L.operand.plain[0]
    m.split_next()
    params = load_layer_params(m, L, io, l)
    n = norm_to_pair(m, L.x, g(0), L.operand, L.y, stat, 3, after=(params,))
    y = ffn(m, L.operand, io["ffn1_w_in"], io["ffn1_w_out"], l, d_ff, L.gated, L.silu, L.y, after=n)
    d = add_normed(m, L.x, L.y, g(1), scratch, stat, 3, after=y)
    n = norm_to_pair(m, L.x, g(2), L.operand, L.y, stat, 3, after=(d,))
    y = mixer(m, L, io, l, n)
    d = add_normed(m, L.x, L.y, g(3), scratch, stat, 3, after=y)
    n = norm_to_pair(m, L.x, g(4), L.operand, L.y, stat, 3, after=(d,))
    y = ffn(m, L.operand, io["ffn2_w_in"], io["ffn2_w_out"], l, d_ff, L.gated, L.silu, L.y, after=n, ahead=False)
    return add_normed(m, L.x, L.y, g(5), scratch, stat, 3, after=y)


def turn_in(m, x, rows, bank0=0, after=()):
    nc = m.nc
    out = []
    for k in range(KT):
        b = bank0 + k % 4
        m.pe.wait(*m.read[b])
        for t in range(2):
            tr = m.pe(nc.tensor.transpose, m.bank[b][:, t * P:(t + 1) * P], rows[:, t, k * P:(k + 1) * P], m.ident[:, :],
                      after=after)
        c = m.act(nc.scalar.copy, x[:, k, :], m.bank[b][:, 0:NT], after=(tr,))
        m.read[b] = [c]
        out.append(c)
    return out


def turn_out(m, rows, x, bank0=0, after=()):
    nc = m.nc
    out = []
    for t in range(2):
        for half in range(2):
            b = bank0 + 2 * t + half
            m.pe.wait(*m.read[b])
            for k in range(4):
                tr = m.pe(nc.tensor.transpose, m.bank[b][:, k * P:(k + 1) * P], x[:, 4 * half + k, t * P:(t + 1) * P],
                          m.ident[:, :], after=after)
            c = m.act(nc.scalar.copy, rows[:, t, half * 512:half * 512 + 512], m.bank[b][:, :], after=(tr,))
            m.read[b] = [c]
            out.append(c)
    return out


class Block:

    XM, O, XL, LRU_GATE, MERGE, LRU_X, LRU_F = 0, 8, 16, 24, 32, 48, 56

    def __init__(self, m, L):
        self.L = L
        sb = m.sb
        self.bias = sb("gate_bias", [4, 4])
        self.rows = L.proj[0:4, self.LRU_F:self.LRU_F + 8, :]
        self.c_cols = sb("c_by_token", [P, 2, 2, 4])
        self.lam = sb("lru_decay", [P, 2, 16])


def load_block_params(m, L, B, io):
    nc = m.nc
    sp = nc.sync
    rows = lambda a: a[0:1].rearrange("o (k c) -> (o k) c", c=P) if len(a.shape) == 2 else a[0:1].rearrange("o t (k c) -> (o t k) c", c=P)
    for i, group in enumerate((("norm1_g_2", "mlstm_conv_w_2", "mlstm_conv_b_2", "mlstm_norm_g_2", "lru_conv_w_2",
                                "lru_conv_b_2", "norm2_g_2"), ("lru_b_r_2", "lru_b_i_2", "lru_lambda_2"))):
        at = 0
        for name in group:
            r = rows(io[name])
            m.params_in.by(sp.dma_start(L.rows[at:at + r.shape[0], i, :], r))
            at += r.shape[0]
    m.params_in.by(sp.dma_start(L.w_ab[:, :, :], io["w_in_2"][0:1, :, 2048:2064].rearrange("o (k p) c -> p (o k) c", p=P)))
    for k in range(4):
        m.params_in.by(sp.dma_start(B.bias[:, k:k + 1], io["b_gates_2"][0:1, 4 * k:4 * k + 4].rearrange("o h -> h o")))
    there = m.params_in.done()
    return [to_columns(m, L.rows[:, 0, :], 104, L.dw_w[:, 0:104], 4, after=(there,)),
            to_columns(m, L.rows[:, 1, :], 48, L.dw_w[:, 104:152], 5, after=(there,))]


def mlstm_gates(m, L, B, normed):
    nc = m.nc
    R = B.rows
    h = L.y
    for d in range(2):
        s = m.matmuls([(m.bank[4 + d][0:4, i * NT:(i + 1) * NT], L.w_ab[:, k, 8 * d + 4 * i:8 * d + 4 * i + 4], h[:, k, :],
                        k == 0, k == KT - 1) for i in range(2) for k in range(KT)], after=(*normed, m.params_in.done()), bank=4 + d)
        x = m.dve(nc.vector.tensor_scalar, R[:, d, :], m.bank[4 + d][0:4, NT:2 * NT], B.bias[:, 2 * d + 1:2 * d + 2], -1.0,
                  ALU.add, ALU.mult, after=(s,))
    sp = softplus(m, R[:, 0:2, :], R[:, 2:4, :], R[:, 4:6, :], R[:, 6:8, :], after=(x,))
    one = m.dve(nc.vector.memset, R[:, 4:6, :], 1.0, after=(sp,))
    rev = lambda a, d: a if d == 0 else a[:, ::-1]
    for d in range(2):
        b = m.dve(nc.vector.tensor_tensor_scan, rev(R[:, 6 + d, :], d), rev(R[:, 4 + d, :], d), rev(R[:, 2 + d, :], d), 0.0,
                  ALU.mult, ALU.subtract, after=(one,))
        c = m.dve(nc.vector.scalar_tensor_tensor, out=R[:, d, :], in0=m.bank[4 + d][0:4, 0:NT], scalar=B.bias[:, 2 * d:2 * d + 1],
                  in1=R[:, 6 + d, :], op0=ALU.add, op1=ALU.subtract, after=(b,))
        m.read[4 + d] = [c]
        M = m.dve(nc.vector.tensor_tensor_scan, rev(R[:, 4 + d, :], d), rev(R[:, d, :], d), rev(R[:, d, :], d), 0.0,
                  ALU.max, ALU.max, after=(c,))
        s = m.dve(nc.vector.tensor_tensor, R[:, 2 + d, :], R[:, 6 + d, :], R[:, 4 + d, :], ALU.add, after=(M,))
    em = m.act(nc.scalar.activation, R[:, 2:4, :], R[:, 2:4, :], ACT.Exp, scale=-1.0, after=(s,))
    bk = 6
    m.pe.wait(*m.read[bk])
    for d in range(2):
        for t in range(2):
            tr = m.pe(nc.tensor.transpose, m.bank[bk][:, (2 * d + t) * 4:(2 * d + t) * 4 + 4], R[:, d, t * P:(t + 1) * P],
                      m.ident[0:4, 0:4], after=(s,))
    cp = m.dve(nc.vector.tensor_copy, B.c_cols[:, :, :, :], m.bank[bk][:, 0:16].rearrange("p (d t h) -> p d t h", d=2, t=2),
               after=(tr,))
    m.read[bk] = [cp]
    return [M, em, cp]


def head_block(io, name):
    return io[name][0].rearrange("h (k p) e -> p (h k) e", p=P)


def mlstm(m, L, B, io, projected, gates):
    nc = m.nc
    proj, conv = L.proj, L.conv
    taps = depthwise(m, lambda c: proj[:, B.XM + c, :], lambda c: conv[:, c, :],
                     lambda k, c: L.dw_w[:, 8 + 8 * k + c:9 + 8 * k + c], 4, 2, range(KT),
                     bias=lambda c: L.dw_w[:, 40 + c:41 + c], after=projected)
    xc = m.act(nc.scalar.activation, conv[:, 0:8, :], conv[:, 0:8, :], ACT.Silu, after=[taps[c] for c in range(8)])
    values = L.operand.plain[1][:, :, :].rearrange("p a n -> p (a n)").rearrange("p (t e) -> p t e", t=2)
    bank2 = lambda b: m.bank[b][:, :].rearrange("p (a n) -> p a n", a=2)
    ready = []
    sv = m.load_block(head_block(io, "mlstm_w_v_2"))
    sq = m.load_block(head_block(io, "mlstm_w_q_2"))
    sk = m.load_block(head_block(io, "mlstm_w_k_2"))
    m.loaded[sv].wait(m.pe)
    for h in range(4):
        p = m.matmuls([(m.bank[h][:, t * NT:(t + 1) * NT], proj[:, B.XM + 2 * h + k, t * P:(t + 1) * P],
                        m.slot[sv][:, 2 * h + k, :], k == 0, k == 1) for t in range(2) for k in range(2)],
                      after=projected, bank=h)
        c = m.act(nc.scalar.copy, values[:, :, h * NT:(h + 1) * NT], bank2(h), after=(p,))
        m.read[h] = [c]
        ready.append(c)
    m.release(sv, p)
    for s, at in ((sq, 8), (sk, 16)):
        m.loaded[s].wait(m.pe)
        for h in range(4):
            b = h if at == 8 else 4 + h
            p = m.matmuls([(m.bank[b][:, e * NT:(e + 1) * NT], m.slot[s][:, 2 * h + k, e * P:(e + 1) * P], conv[:, 2 * h + k, :],
                            k == 0, k == 1) for e in range(2) for k in range(2)], after=(xc,), bank=b)
            c = m.act(nc.scalar.copy, conv[:, at + 2 * h:at + 2 * h + 2, :], bank2(b), after=(p,))
            m.read[b] = [c]
            ready.append(c)
        m.release(s, p)

    H = L.operand.plain[0]
    E = lambda d, h: L.y[:, 4 * (h % 2) + 2 * d:4 * (h % 2) + 2 * d + 2, :]
    den = [L.silu, L.gated.plain[0]]
    used, wrote = {}, {}
    for h in range(4):
        sb = h % 2
        score = m.matmuls([(m.bank[sb][:, t * NT:(t + 1) * NT], conv[:, 16 + 2 * h + e, t * P:(t + 1) * P],
                            conv[:, 8 + 2 * h + e, :], e == 0, e == 1) for t in range(2) for e in range(2)],
                          after=ready, bank=sb)
        for d in range(2):
            ms = m.matmuls([(m.bank[2 + d][:, 0:NT], m.pick[0:4, h, :], B.rows[:, 4 + d, :], True, True),
                            (m.bank[2 + d][:, NT:2 * NT], m.pick[0:4, h, :], B.rows[:, 2 + d, :], True, True)],
                           after=gates, bank=2 + d)
            e = E(d, h)
            span = [slice(0, NT), slice(P, NT)] if d == 0 else [slice(0, P), slice(0, NT)]
            for t in range(2):
                w = m.dve(nc.vector.tensor_scalar, e[:, t, span[t]], m.bank[2 + d][:, span[t]], B.c_cols[:, d, t, h:h + 1], 0.0,
                          ALU.subtract, ALU.max, after=(ms, *gates, used.get((d, sb))))
            for t in range(2):
                x = m.act(nc.scalar.activation, e[:, t, span[t]], e[:, t, span[t]], ACT.Exp, scale=-1.0, after=(w,))
            for t in range(2):
                diag = slice(t * P, (t + 1) * P)
                k = m.dve(nc.vector.tensor_tensor, e[:, t, diag], e[:, t, diag], (m.upto if d == 0 else m.from_)[:, :],
                          ALU.mult, after=(x,))
            for t in range(2):
                pr = m.dve(nc.vector.scalar_tensor_tensor, out=e[:, t, span[t]], in0=m.bank[sb][:, t * NT + span[t].start:t * NT + span[t].stop],
                           scalar=NT ** -0.5, in1=e[:, t, span[t]], op0=ALU.mult, op1=ALU.mult, after=(k, score))
            m.read[sb] = [pr]
            order = (0, 1) if d == 0 else (1, 0)
            dn = m.matmuls([(m.bank[4 + d][:, span[t]], m.ones[:, :], e[:, t, span[t]], i == 0, i == 1)
                            for i, t in enumerate(order)], after=(pr,), bank=4 + d)
            nm = m.matmuls([(m.bank[6 + d][:, v * NT + span[t].start:v * NT + span[t].stop],
                             values[:, t, h * NT + v * P:h * NT + (v + 1) * P], e[:, t, span[t]], i == 0, i == 1)
                            for v in range(2) for i, t in enumerate(order)], bank=6 + d)
            used[d, sb] = nm
            r = den[d][:, 0, :]
            a = m.act(nc.scalar.activation, r, m.bank[4 + d][:, 0:NT], ACT.Abs, after=(dn, wrote.get(d)))
            m.read[4 + d] = [a]
            a = m.dve(nc.vector.tensor_tensor, r, r, m.bank[2 + d][:, NT:2 * NT], ALU.max, after=(a,))
            m.read[2 + d] = [a]
            a = m.dve(nc.vector.reciprocal, r, r, after=(a,))
            rr = r.unsqueeze(1).to_broadcast([P, 2, NT])
            Hh = H[:, 2 * h:2 * h + 2, :]
            if d == 0:
                a = m.dve(nc.vector.tensor_tensor, Hh, bank2(6), rr, ALU.mult, after=(a, nm))
                m.read[6] = [a]
                first = a
            else:
                a = m.dve(nc.vector.tensor_tensor, e, bank2(7), rr, ALU.mult, after=(a, nm))
                m.read[7] = [a]
                a = m.dve(nc.vector.tensor_tensor, Hh, Hh, e, ALU.add, after=(a, first))
                used[d, sb] = a
            wrote[d] = a
    sg = m.act(nc.scalar.activation, proj[:, B.O:B.O + 8, :], proj[:, B.O:B.O + 8, :], ACT.Sigmoid, after=projected)
    sq = m.act(nc.scalar.square, L.y[:, :, :], H[:, :, :], after=(a,))
    n = head_sums(m, lambda i: L.y[:, i, :], 4, L.norm16[0:4, :], 0, RMS_EPS, scale=1.0 / NT, per_row=2, after=(sq,))
    out = []
    for h in range(4):
        s = spread_row(m, 1 + h, 0, L.norm16[0:4, :], 4, h, after=(n,))
        for v in range(2):
            t = 2 * h + v
            a = m.dve(nc.vector.scalar_tensor_tensor, out=H[:, t, :], in0=H[:, t, :], scalar=L.dw_w[:, 48 + t:49 + t],
                      in1=m.bank[1 + h][:, 0:NT], op0=ALU.mult, op1=ALU.mult, after=(s,))
            out.append(m.dve(nc.vector.tensor_tensor, H[:, t, :], H[:, t, :], proj[:, B.O + t, :], ALU.mult, after=(a, sg)))
        m.read[1 + h] = [a]
    return out


def rg_lru(m, L, B, io, projected, conv_free):
    nc = m.nc
    proj, conv = L.proj, L.conv
    X = proj[:, B.LRU_X:B.LRU_X + 8, :]
    taps = depthwise(m, lambda c: proj[:, B.XL + c, :], lambda c: proj[:, B.LRU_X + c, :],
                     lambda k, c: L.dw_w[:, 56 + 8 * k + c:57 + 8 * k + c], 4, 2, range(KT),
                     bias=lambda c: L.dw_w[:, 88 + c:89 + c], after=projected)
    taps = [taps[c] for c in range(8)]
    ng = m.dve(nc.vector.tensor_scalar, B.lam[:, 0, :], L.dw_w[:, 104 + 32:104 + 48], -1.0, None, ALU.mult)
    sp = softplus(m, B.lam[:, 0, :], B.lam[:, 1, :], L.cols[:, 0:16], L.cols[:, 16:32], after=(ng,))
    pos = m.dve(nc.vector.tensor_scalar, B.lam[:, 1, :], B.lam[:, 1, :], 8.0, None, ALU.mult, after=(sp,))
    neg = m.dve(nc.vector.tensor_scalar, B.lam[:, 0, :], B.lam[:, 1, :], -1.0, None, ALU.mult, after=(pos,))
    pairs = lambda a: a[0].rearrange("d n c e -> c (d n) e")
    view = lambda s: m.slot[s][:, :, :].rearrange("p k c -> p (k c)").rearrange("p (j e) -> p j e", e=P)
    sr = m.load_block(pairs(io["lru_w_r_2"]), view)
    si = m.load_block(pairs(io["lru_w_i_2"]), view)
    m.loaded[sr].wait(m.pe)
    m.loaded[si].wait(m.pe)
    R, I, T, A2 = conv[:, 0:8, :], conv[:, 8:16, :], conv[:, 16:24, :], L.y
    gl = m.act(nc.scalar.activation, proj[:, B.LRU_GATE:B.LRU_GATE + 8, :], proj[:, B.LRU_GATE:B.LRU_GATE + 8, :], ACT.Gelu,
               after=projected)
    free = [*conv_free]
    results = []
    for d in range(2):
        rd, idn = [], []
        for w, dst, b0, bias, out in ((sr, R, 0, 104, rd), (si, I, 4, 120, idn)):
            for n in range(8):
                b = b0 + n // 2
                s = m.matmuls([(m.bank[b][:, n % 2 * NT:(n % 2 + 1) * NT], view(w)[:, 8 * d + n, :], X[:, n, :], True, True)],
                              after=(taps[n],), bank=b if n % 2 == 0 else None)
                if n % 2:
                    for q in range(2):
                        k = n - 1 + q
                        c = m.act(nc.scalar.activation, dst[:, k, :], m.bank[b][:, q * NT:(q + 1) * NT], ACT.Sigmoid,
                                  bias=L.dw_w[:, bias + 8 * d + k:bias + 8 * d + k + 1], after=(s, *free))
                        out.append(c)
                    m.read[b] = [c]
        th, aa, a2, v = [], [], [], []
        for n in range(8):
            th.append(m.act(nc.scalar.activation, T[:, n, :], R[:, n, :], ACT.Tanh, scale=B.lam[:, 1, 8 * d + n:8 * d + n + 1],
                            after=(rd[n], neg)))
            aa.append(m.act(nc.scalar.activation, R[:, n, :], R[:, n, :], ACT.Exp, scale=B.lam[:, 0, 8 * d + n:8 * d + n + 1],
                            after=(th[n],)))
        ix = m.dve(nc.vector.tensor_tensor, I, I, X, ALU.mult, after=(idn[-1],))
        for n in range(0, 8, 4):
            f = slice(n, n + 4)
            q = m.dve(nc.vector.tensor_tensor, A2[:, f, :], R[:, f, :], R[:, f, :], ALU.mult, after=(aa[n + 3], *free))
            q = m.dve(nc.vector.scalar_tensor_tensor, out=T[:, f, :], in0=A2[:, f, :], scalar=1.0, in1=T[:, f, :], op0=ALU.add,
                      op1=ALU.mult, after=(q,))
            q = m.act(nc.scalar.activation, T[:, f, :], T[:, f, :], ACT.Sqrt, after=(q,))
            q = m.dve(nc.vector.tensor_tensor, T[:, f, :], T[:, f, :], I[:, f, :], ALU.mult, after=(q, ix))
            v += [q] * 4
        for n in range(8):
            if d == 0:
                sc = m.dve(nc.vector.tensor_tensor_scan, proj[:, B.LRU_F + n, :], R[:, n, :], T[:, n, :], 0.0, ALU.mult, ALU.add,
                           after=(v[n],))
            else:
                sc = m.dve(nc.vector.tensor_tensor_scan, A2[:, n, ::-1], R[:, n, ::-1], T[:, n, ::-1], 0.0, ALU.mult, ALU.add,
                           after=(v[n],))
        free = [sc]
    m.release(sr, s)
    m.release(si, s)
    F = proj[:, B.LRU_F:B.LRU_F + 8, :]
    a = m.dve(nc.vector.tensor_tensor, F, F, A2[:, :, :], ALU.add, after=(sc,))
    return [m.dve(nc.vector.tensor_tensor, F, F, proj[:, B.LRU_GATE:B.LRU_GATE + 8, :], ALU.mult, after=(a, gl))]


def merge(m, L, B, io, y_m, y_l, gates):
    nc = m.nc
    two = lambda t, b: t[:, 2 * b:2 * b + 2, :]
    bank2 = lambda s: m.bank[s][:, :].rearrange("p (a n) -> p a n", a=2)
    F = L.proj[:, B.LRU_F:B.LRU_F + 8, :]
    merge_m, merge_l = (L.proj[:, t:t + 8, :] for t in (B.MERGE, B.MERGE + 8))
    g = m.act(nc.scalar.activation, L.proj[:, B.MERGE:B.MERGE + 16, :], L.proj[:, B.MERGE:B.MERGE + 16, :], ACT.Sigmoid, after=gates)
    done = {}

    def evict_m(b, s):
        m.computed[s].wait(m.dve)
        m.dve.wait(g)
        m.evicted[s].by(nc.vector.tensor_tensor(two(merge_m, b), bank2(s), two(merge_m, b), ALU.mult))
        done["m", b] = m.evicted[s].done()

    def evict_l(b, s):
        m.computed[s].wait(m.dve)
        m.evicted[s].by(nc.vector.tensor_tensor(two(L.y, b), bank2(s), two(merge_l, b), ALU.mult))
        done["l", b] = m.dve(nc.vector.tensor_tensor, two(L.y, b), two(L.y, b), two(merge_m, b), ALU.add,
                             after=(m.evicted[s].done(), done["m", b]))

    def evict_out(b, s):
        m.computed[s].wait(m.dve)
        m.evicted[s].by(nc.vector.tensor_tensor(two(L.x, b), two(L.x, b), bank2(s), ALU.add))
        done["x", b] = m.evicted[s].done()

    m.split_next()
    y_m = m.split(L.operand.plain[0], L.operand2, after=[(*y_m, *y_l)] * 4)
    y_l = m.split(F, L.operand, after=[(y_m[-1],)] * 4)
    m.project_with(L.operand2, lambda b: columns(io["w_branch_mlstm_2"], 0, b * 256), evict_m, after=y_m)
    m.project_with(L.operand, lambda b: columns(io["w_branch_lru_2"], 0, b * 256), evict_l, after=y_l)
    y = m.split(L.y, L.operand2, after=[(done["l", b],) for b in range(4)])
    m.project_with(L.operand2, lambda b: columns(io["w_out_2"], 0, b * 256), evict_out, after=y)
    return [done["x", b] for b in range(4)]


class Peer:

    HEADS, TOP, KEYS, GROUP = 8, 16, 128, 8
    STEPS = 32

    def __init__(self, m, L):
        flat = lambda t: t.rearrange("p a n -> p (a n)")
        G = self.GROUP
        self.u = m.nc.alloc_sbuf_tensor_at("expert_u_rows", [P, G, KT * P], F32, offset=m.slots_at)
        v = flat(L.proj[:, :, :]).rearrange("p (s d) -> p s d", s=2 * G)
        self.v = [v[:, p * G:(p + 1) * G, :] for p in range(2)]
        self.gain = flat(m.slot[2][:, 0:4, :])
        self.keys = flat(L.operand.plain[0][:, :, :]).rearrange("p (j n) -> p j n", n=P)
        self.h_tok, self.x_tok = (flat(a[:, :, :]).rearrange("p (t d) -> p t d", t=2) for a in L.operand.plain)
        diag = flat(L.x[:, :, :]).rearrange("p (s n) -> p s n", n=P)
        self.diag = [diag[:, p * G:(p + 1) * G, :] for p in range(2)]
        self.scores = flat(L.conv[:, 0:17, :]).rearrange("p (j n) -> p j n", n=P)
        self.lists = flat(L.conv[:, 17:18, :]).rearrange("p (j n) -> p j n", n=P)
        self.pairs = L.conv[:, 18, :]
        self.match = L.conv[:, 19, :].rearrange("p (a b) -> p a b", a=16)
        tables, at = flat(L.conv[:, 20:22, :]), [0]

        def table(n, dt=F32):
            at[0] += n
            t = tables[:, at[0] - n:at[0]]
            return t if dt == F32 else t.bitcast(dt)

        two = lambda t: t.rearrange("p (s k) -> p s k", s=2)
        self.top, self.top_i, self.top_f = two(table(32)), two(table(32, U32)), two(table(32))
        self.best, self.pos = table(16), table(16, U32)
        self.half, self.half_i, self.row = ([table(16, dt) for _ in range(2)] for dt in (F32, U32, F32))
        self.index, self.gate = ([table(16, dt) for _ in range(2)] for dt in (U32, F32))
        self.sum, self.inv = table(1), table(1)
        self.counting, self.counting_i = table(16), table(16, I32)
        self.dots, self.acts, self.weights = ([table(G) for _ in range(2)] for _ in range(3))
        self.ss = table(4)


class PeerCounts:
    def __init__(self, m):
        c = lambda name, unit=1: Count(m.nc, name, unit)
        G = Peer.GROUP
        self.u_in = [c(f"u_in{s}", 16) for s in range(G)]
        self.u_used = [c(f"u_used{s}") for s in range(G)]
        self.v_in = [[c(f"v_in{p}_{s}", 16) for s in range(G)] for p in range(2)]
        self.v_used = [[c(f"v_used{p}_{s}") for s in range(G)] for p in range(2)]
        self.slot_free, self.turn = c("gather_slot_free"), c("choose_turn")
        self.step, self.exp, self.chosen = c("choose_step"), c("softmax_exp"), c("head_chosen")
        self.gelu, self.weighed, self.diag, self.added = (c(n) for n in ("gelu", "weighed", "diag", "added"))
        self.per_round = {c: 4 for c in [*self.u_in, *self.u_used, self.gelu, self.weighed, self.diag, self.added]}
        self.per_round.update({c: 2 for c in [*sum(self.v_in, []), *sum(self.v_used, []), self.exp, self.chosen]})
        self.per_round[self.step] = 2 * Peer.STEPS

    def prime(self, m):
        for c in [*self.u_used, self.step, self.gelu, self.weighed]:
            c.by(m.prime(m.nc.vector))
        for c in [*sum(self.v_used, []), self.diag]:
            c.by(m.prime(m.nc.tensor))


def choose_experts(m, K, C, n, parity):
    nc, v = m.nc, m.nc.vector

    def step(ins, *args, alone=True, **kw):
        if alone:
            C.step.wait(m.dve)
            if ins in (v.max, v.max_index, v.match_replace):
                v.sem_inc(C.turn.sem, 1)
        C.step.by(ins(*args, **kw))

    def best16(lists, top, top_i):
        for at in (0, 8):
            for j, x in enumerate(lists):
                step(v.max, top[j][:, at:at + 8], x, alone=j == 0)
            for j, x in enumerate(lists):
                step(v.max_index, top_i[j][:, at:at + 8], top[j][:, at:at + 8], x, alone=j == 0)
            if at == 0:
                for j, x in enumerate(lists):
                    step(v.match_replace, x, top[j][:, 0:8], x, LOWEST, alone=j == 0)

    step(v.tensor_copy, K.lists, K.scores[:, bass.ds(n * 2, 2), :])
    best16([K.lists[:, s, :] for s in range(2)], [K.top[:, s, :] for s in range(2)], [K.top_i[:, s, :] for s in range(2)])
    rows = lambda a: a.unsqueeze(2).to_broadcast([P, 16, 16])
    cols = lambda a: a.unsqueeze(1).to_broadcast([P, 16, 16])
    step(v.tensor_copy, K.top_f, K.top_i)
    step(v.tensor_tensor, K.pairs.rearrange("p (a b) -> p a b", a=16), rows(K.top[:, 0, :]), cols(K.top[:, 1, :]), ALU.add,
         alone=False)
    best16([K.pairs], [K.best], [K.pos])
    for i, (op, by) in enumerate(((ALU.logical_shift_right, 4), (ALU.bitwise_and, 15))):
        step(v.tensor_scalar, K.half_i[i], K.pos, by, None, op, alone=i == 0)
    for i in range(2):
        step(v.tensor_copy, K.half[i], K.half_i[i], alone=i == 0)
    for i in range(2):
        step(v.tensor_tensor, K.match, rows(K.half[i]), cols(K.counting), ALU.is_equal)
        step(v.tensor_tensor, K.match, K.match, cols(K.top_f[:, i, :]), ALU.mult)
        step(v.tensor_reduce, K.row[i], K.match, AX.X, ALU.add)
    step(v.scalar_tensor_tensor, out=K.row[0], in0=K.row[0], scalar=float(K.KEYS), in1=K.row[1], op0=ALU.mult, op1=ALU.add)
    C.step.wait(m.dve)
    C.chosen.by(v.tensor_copy(K.index[parity], K.row[0]))
    step(v.tensor_scalar, K.gate[parity], K.best, K.best[:, 0:1], None, ALU.subtract, alone=False)
    C.step.wait(m.act)
    C.exp.by(nc.scalar.activation(K.gate[parity], K.gate[parity], ACT.Exp, accum_out=K.sum))
    C.exp.wait(m.dve)
    step(v.reciprocal, K.inv, K.sum, alone=False)
    step(v.tensor_scalar, K.gate[parity], K.gate[parity], K.inv, None, ALU.mult)


def add_group(m, K, C, t, p):
    x = K.x_tok[:, t, :]
    C.v_used[p][-1].wait(m.dve)
    C.added.wait(m.dve)
    for half in range(2):
        at = slice(half * 512, half * 512 + 512)
        ins = m.nc.vector.tensor_tensor(x[:, at], x[:, at], m.bank[2 * p + half][:, :], ALU.add)
    C.added.by(ins)


def run_group(m, K, io, C, t, parity, p):
    nc = m.nc
    G = K.GROUP
    first = p * G
    for table, rows, arrived, used in ((io["peer_u_2"][0], K.u, C.u_in, C.u_used),
                                       (io["peer_v_2"][0], K.v[p], C.v_in[p], C.v_used[p])):
        for s in range(G):
            used[s].wait(m.pool)
            nc.gpsimd.sem_inc(C.slot_free.sem, 1)
            arrived[s].by(nc.gpsimd.indirect_dma_start(
                out=rows[:, s, :], out_offset=None, in_=table,
                in_offset=bass.IndirectOffsetOnAxis(ap=K.index[parity][:, first + s:first + s + 1], axis=0)))
    for s in range(G):
        C.u_in[s].wait(m.dve)
        C.u_used[s].by(nc.vector.tensor_tensor_reduce(out=K.u[:, s, :], in0=K.u[:, s, :], in1=K.h_tok[:, t, :], scale=1.0,
                                                      scalar=0.0, op0=ALU.mult, op1=ALU.add, accum_out=K.dots[p][:, s:s + 1]))
    C.u_used[-1].wait(m.act)
    C.weighed.wait(m.act)
    C.gelu.by(nc.scalar.activation(K.acts[p], K.dots[p], ACT.Gelu))
    C.gelu.wait(m.dve)
    C.diag.wait(m.dve)
    C.step.wait(m.dve)
    C.weighed.by(nc.vector.tensor_tensor(K.weights[p], K.acts[p], K.gate[parity][:, first:first + G], ALU.mult))
    C.weighed.wait(m.act)
    C.v_used[p][-1].wait(m.act)
    for s in range(G):
        ins = nc.scalar.activation(K.diag[p][:, s, :], m.ident[:, :], ACT.Copy, scale=K.weights[p][:, s:s + 1])
    C.diag.by(ins)
    C.diag.wait(m.pe)
    C.added.wait(m.pe)
    for s in range(G):
        C.v_in[p][s].wait(m.pe)
        for half in range(2):
            ins = nc.tensor.matmul(m.bank[2 * p + half][:, :], K.diag[p][:, s, :], K.v[p][:, s, half * 512:half * 512 + 512],
                                   start=(s == 0), stop=(s == G - 1))
        C.v_used[p][s].by(ins)
    add_group(m, K, C, t, 1 - p)


def run_experts(m, K, io, t, C):
    for half in range(2):
        ins = m.nc.vector.memset(m.bank[2 + half][:, :], 0.0)
    C.added.by(ins)
    with rounds(m.nc, K.HEADS // 2, C.per_round) as j:
        for parity in range(2):
            C.chosen.wait(m.pool)
            run_group(m, K, io, C, t, parity, 0)
            choose_experts(m, K, C, j * 2 + (t * K.HEADS + parity + 1), 1 - parity)
            run_group(m, K, io, C, t, parity, 1)
    add_group(m, K, C, t, 1)
    C.added.wait(m.dve)


def peer(m, L, io, C, x_done, h2):
    nc = m.nc
    K = Peer(m, L)
    q_in = m.project(L.operand, lambda b: columns(io["peer_w_q_2"], 0, b * 256), 8, L.proj, 0, after=h2, ahead=False)
    view = lambda s: m.slot[s][:, :, :].rearrange("p k c -> p (k c)").rearrange("p (j e) -> p j e", e=P)
    sk = m.load_block(io["peer_sub_keys_2"][0].rearrange("h s n c -> n (h s) c"), view)
    m.loaded[sk].wait(m.pe)
    four = lambda b: m.bank[b][:, :].rearrange("p (j n) -> p j n", j=4)
    keys = []
    for i in range(4):
        m.pe.wait(*m.read[i])
        for j in range(4):
            tr = m.pe(nc.tensor.transpose, m.bank[i][:, j * P:(j + 1) * P], view(sk)[:, 4 * i + j, :], m.ident[:, :])
        c = m.act(nc.scalar.copy, K.keys[:, 4 * i:4 * i + 4, :], four(i), after=(tr,))
        m.read[i] = [c]
        keys.append(c)
    scored = [m.dve(nc.vector.memset, K.scores[:, 32:34, :], 0.0, after=keys)]
    for t in range(2):
        for i in range(4):
            b = 4 * t + i
            s = m.matmuls([(m.bank[b][:, j * P:(j + 1) * P], L.proj[:, 4 * i + j, t * P:(t + 1) * P], K.keys[:, 4 * i + j, :], True, True)
                           for j in range(4)], after=(*q_in, *keys), bank=b)
            c = m.act(nc.scalar.copy, K.scores[:, 16 * t + 4 * i:16 * t + 4 * i + 4, :], four(b), after=(s,))
            m.read[b] = [c]
            scored.append(c)
    ht = turn_out(m, K.h_tok, L.y, 4, after=(*h2, s))
    xt = turn_out(m, K.x_tok, L.x, 4, after=x_done)
    i = m.pool(nc.gpsimd.iota, K.counting_i, pattern=[[1, 16]], base=0, channel_multiplier=0, after=(s,))
    i = m.dve(nc.vector.tensor_copy, K.counting, K.counting_i, after=(i,))
    m.sp.wait(s)
    m.misc_in.by(nc.sync.dma_start(K.gain, io["final_norm_g_2"].unsqueeze(0).to_broadcast([P, KT * P])))
    gain = m.misc_in.done()
    C.prime(m)
    m.dve.wait(*scored, i)
    choose_experts(m, K, C, 0, 0)
    m.pool.wait(s, *keys)
    m.dve.wait(*xt, *ht)
    for t in range(2):
        run_experts(m, K, io, t, C)
    a = C.added.done()
    for t in range(2):
        x = K.x_tok[:, t, :]
        ss, r = K.ss[:, 2 * t:2 * t + 1], K.ss[:, 2 * t + 1:2 * t + 2]
        q = m.act(nc.scalar.activation, K.h_tok[:, t, :], x, ACT.Square, accum_out=ss, after=(a,))
        q = m.dve(nc.vector.tensor_scalar, r, ss, 1.0 / (KT * P), RMS_EPS, ALU.mult, ALU.add, after=(q,))
        q = m.dve(nc.vector.reciprocal, r, r, after=(q,))
        q = m.act(nc.scalar.activation, r, r, ACT.Sqrt, after=(q,))
        q = m.dve(nc.vector.scalar_tensor_tensor, out=x, in0=x, scalar=r, in1=K.gain, op0=ALU.mult, op1=ALU.mult, after=(q, gain))
        m.sp.wait(q)
        m.misc_in.by(nc.sync.dma_start(io["out"][0, t * P:(t + 1) * P, :], x))
    m.sp.wait(m.misc_in.done())


def last_block(m, L, B, io, C):
    m.split_next()
    params = load_block_params(m, L, B, io)
    n = norm_to_pair(m, L.x, L.dw_w[:, 0:8], L.operand, L.y, L.stat[:, :], 3, after=params)
    w = io["w_in_2"]
    gates = mlstm_gates(m, L, B, n)
    first = m.project(L.operand, lambda b: columns(w, 0, b * 256), 8, L.proj, B.XM, after=n)
    rest = m.project(L.operand, lambda b: columns(w, 0, b * 256 + 2064), 16, L.proj, B.XL, ahead=False)
    y_m = mlstm(m, L, B, io, (*first, *rest), gates)
    y_l = rg_lru(m, L, B, io, rest, y_m)
    x = merge(m, L, B, io, y_m, y_l, rest)
    h2 = norm_to_pair(m, L.x, L.dw_w[:, 96:104], L.operand, L.y, L.stat[:, :], 3, after=x)
    peer(m, L, io, C, x, h2)


def program(nc, io):
    m = Machine(nc)
    L = Layer(m)
    B = Block(m, L)
    C = PeerCounts(m)
    m.start_phase()
    made = make_constants(m)
    rows = L.proj[:, 0:8, :].rearrange("p a b -> p (a b)").rearrange("p (t c) -> p t c", t=2)
    m.misc_in.by(nc.sync.dma_start(rows, io["x"][0].rearrange("(t p) c -> p t c", p=P)))
    turn_in(m, L.x, rows, after=(m.misc_in.done(), *made))
    m.end_phase()
    with nc.Fori(0, io["ffn1_w_in"].shape[0]) as l:
        m.start_phase()
        layer(m, L, io, l)
        m.end_phase()
    m.start_phase()
    last_block(m, L, B, io, C)


def kernel(**inputs):
    import concourse.bacc as bacc
    from concourse.bass_utils import run_bass_kernel_spmd

    nc = bacc.Bacc("TRN2", target_bir_lowering=False, num_devices=1)
    arrays, io = {}, {}
    for name, value in inputs.items():
        a = np.ascontiguousarray(value)
        arrays[f"in_{name}"] = a
        io[name] = nc.dram_tensor(f"in_{name}", a.shape, mybir.dt.from_np(a.dtype), kind="ExternalInput").ap()
    io["out"] = nc.dram_tensor("out_x", inputs["x"].shape, F32, kind="ExternalOutput").ap()
    program(nc, io)
    return run_bass_kernel_spmd(nc, [arrays], core_ids=[0]).results[0]["out_x"]
```

```python
from contextlib import contextmanager
from itertools import zip_longest

import numpy as np

import concourse.bass as bass
from concourse import mybir

F32 = mybir.dt.float32
F32R = mybir.dt.float32r
I32 = mybir.dt.int32
U32 = mybir.dt.uint32
ALU = mybir.AluOpType
ACT = mybir.ActivationFunctionType
AX = mybir.AxisListType
P = 128
NT = 256
KT = 8
RMS_EPS, LN_EPS = 1e-6, 1e-5
LOWEST = -3.0e38


class Done:

    def __init__(self, sem, value):
        self.sem, self.value = sem, value


class Queue:

    def __init__(self, nc, eng, name):
        self.eng, self.sem, self.n, self.waited = eng, nc.alloc_semaphore(f"{name}_done"), 0, {}

    def wait(self, *dones):
        for d in dones:
            if d is None:
                continue
            if isinstance(d, (list, tuple)):
                self.wait(*d)
            elif self.waited.get(d.sem.num, 0) < d.value:
                self.eng.wait_ge(d.sem, d.value)
                self.waited[d.sem.num] = d.value

    def __call__(self, ins, *args, after=(), **kw):
        self.wait(*after)
        ins(*args, **kw).then_inc(self.sem, 1)
        self.n += 1
        return Done(self.sem, self.n)

    def reset(self):
        self.n, self.waited = 0, {}


class Count:

    def __init__(self, nc, name, unit=1):
        self.sem, self.unit, self.n, self.loop = nc.alloc_semaphore(name), unit, 0, None

    def by(self, ins):
        ins.then_inc(self.sem, self.unit)
        self.n += 1

    def wait(self, q, but=0):
        value = (self.n - but) * self.unit
        assert value > 0
        if self.loop is not None:
            reg, per = self.loop
            value = reg * (per * self.unit) + value
        q.eng.wait_ge(self.sem, value)

    def done(self):
        assert self.loop is None
        return Done(self.sem, self.n * self.unit)


@contextmanager
def rounds(nc, n, counts):
    start = {c: c.n for c in counts}
    with nc.Fori(0, n) as reg:
        for c, per in counts.items():
            c.loop = (reg, per)
        yield reg
        for c, per in counts.items():
            assert c.n == start[c] + per, (c.sem, c.n - start[c], per)
            c.loop = None
            c.n = start[c] + n * per


class Pair:

    def __init__(self, hi, lo, plain=None):
        self.hi, self.lo, self.plain = hi, lo, plain


class Machine:

    SLOTS = 3

    def __init__(self, nc):
        self.nc = nc
        self.pe = Queue(nc, nc.tensor, "pe")
        self.act = Queue(nc, nc.scalar, "act")
        self.dve = Queue(nc, nc.vector, "dve")
        self.pool = Queue(nc, nc.gpsimd, "pool")
        self.sp = Queue(nc, nc.sync, "sp")
        self.queues = [self.pe, self.act, self.dve, self.pool, self.sp]
        S = self.SLOTS
        self.loaded = [Count(nc, f"weights_loaded{s}", 16) for s in range(S)]
        self.hi_made = [[Count(nc, f"weights_hi{s}_{q}") for q in range(2)] for s in range(S)]
        self.lo_made = [[Count(nc, f"weights_lo{s}_{q}") for q in range(2)] for s in range(S)]
        self.computed = [Count(nc, f"weights_used{s}") for s in range(S)]
        self.evicted = [Count(nc, f"bank_evicted{s}") for s in range(S)]
        self.product = Count(nc, "ffn_product")
        self.product_hi = Count(nc, "ffn_product_hi")
        self.params_in = Count(nc, "params_in", 16)
        self.misc_in = Count(nc, "misc_in", 16)
        self.ring = [*self.loaded, *sum(self.hi_made, []), *sum(self.lo_made, []), *self.computed, *self.evicted]
        self.counts = [*self.ring, self.product, self.product_hi, self.params_in, self.misc_in]
        self.bank = [nc.alloc_psum_tensor(f"bank{b}", [P, 512], F32) for b in range(8)]
        self.read = [[] for _ in range(8)]
        self.slot, self.lo, self.hi = [], [], []
        self.slots_at = self.next_address()
        for s in range(S):
            raw, lo = self.shared((f"weights{s}", F32), (f"weights_low{s}", F32R), shape=[P, KT, 256])
            self.slot.append(raw)
            self.lo.append(lo)
            self.hi.append(self.sb(f"weights_high{s}", [P, KT, 256], F32R))
        self.next_slot = 0

    def sb(self, name, shape, dt=F32):
        return self.nc.alloc_sbuf_tensor(name, shape, dt)

    def next_address(self):
        return (self.nc.sbuf_base + 31) // 32 * 32

    def shared(self, *names, shape):
        at = self.next_address()
        return [self.sb(names[0][0], shape, names[0][1])] + \
               [self.nc.alloc_sbuf_tensor_at(n, shape, dt, offset=at) for n, dt in names[1:]]

    def pair(self, name, tiles):
        hi, hi32 = self.shared((f"{name}_hi", F32R), (f"{name}_hi_plain", F32), shape=[P, tiles, NT])
        lo, lo32 = self.shared((f"{name}_lo", F32R), (f"{name}_lo_plain", F32), shape=[P, tiles, NT])
        return Pair(hi, lo, (hi32, lo32))

    def start_phase(self):
        for q in self.queues:
            q.reset()
        self.read = [[] for _ in range(8)]
        self.next_slot = 0
        for c in self.counts:
            c.n = 0
        for s in range(self.SLOTS):
            self.computed[s].by(self.prime(self.nc.tensor))
            self.evicted[s].by(self.prime(self.nc.scalar))

    @staticmethod
    def prime(eng):
        return eng.nop()

    def end_phase(self):
        sems = [q.sem.num for q in self.queues] + [c.sem.num for c in self.counts]
        assert sorted(sems) == list(range(min(sems), max(sems) + 1)), sems
        self.nc.all_engine_barrier(sems_to_clear=range(min(sems), max(sems) + 1))

    def matmuls(self, steps, after=(), bank=None):
        self.pe.wait(*after)
        if bank is not None:
            self.pe.wait(*self.read[bank])
        for out, lhsT, rhs, start, stop in steps[:-1]:
            self.nc.tensor.matmul(out, lhsT, rhs, start=start, stop=stop)
        out, lhsT, rhs, start, stop = steps[-1]
        return self.pe(self.nc.tensor.matmul, out, lhsT, rhs, start=start, stop=stop)

    def load_block(self, src, dst=None):
        s = self.next_slot
        self.next_slot = (s + 1) % self.SLOTS
        self.computed[s].wait(self.sp)
        self.loaded[s].by(self.nc.sync.dma_start(self.slot[s][:, :, :] if dst is None else dst(s), src))
        return s

    def halves(self, t):
        return [t[:, :, q * P:(q + 1) * P] for q in range(2)]

    def split_next(self, second=None):
        s = self.next_slot
        raw, hi, lo = self.halves(self.slot[s]), self.halves(self.hi[s]), self.halves(self.lo[s])
        self.loaded[s].wait(self.act, but=-1)
        for q in range(2):
            self.hi_made[s][q].by(self.nc.scalar.copy(hi[q], raw[q]))
        for q in range(2):
            by = second if second and q == 1 else self.pool
            self.hi_made[s][q].wait(by)
            self.lo_made[s][q].by(by.eng.tensor_tensor(lo[q], raw[q], hi[q].bitcast(F32), ALU.subtract))

    def block_products(self, s, x, ready=()):
        self.evicted[s].wait(self.pe)
        for m in range(2):
            self.lo_made[s][m].wait(self.pe)
            hi, lo = self.halves(self.hi[s])[m], self.halves(self.lo[s])[m]
            out = self.bank[s][:, m * NT:(m + 1) * NT]
            for k in range(KT):
                if m == 0 and k % 2 == 0:
                    self.pe.wait(*ready[k // 2:k // 2 + 1])
                self.nc.tensor.matmul(out, hi[:, k, :], x.hi[:, k, :], start=(k == 0), stop=False)
                self.nc.tensor.matmul(out, hi[:, k, :], x.lo[:, k, :], start=False, stop=False)
                ins = self.nc.tensor.matmul(out, lo[:, k, :], x.hi[:, k, :], start=False, stop=(k == KT - 1))
        self.computed[s].by(ins)

    def release(self, s, last):
        self.pe.wait(last)
        self.computed[s].by(self.prime(self.nc.tensor))

    def settle_banks(self):
        for s in range(self.SLOTS):
            self.pe.wait(*self.read[s])
            self.read[s] = []

    def streamed(self):
        for s in range(self.SLOTS):
            self.read[s] = [self.evicted[s].done()]

    def split(self, src, pair, after, tiles=KT, make=None):
        hi, lo = [], []

        def low(i):
            two = slice(2 * i, 2 * i + 2)
            lo.append(self.dve(self.nc.vector.tensor_tensor, pair.lo[:, two, :], src[:, two, :],
                               pair.hi[:, two, :].bitcast(F32), ALU.subtract, after=(hi[i],)))

        for i in range(tiles // 2):
            two = slice(2 * i, 2 * i + 2)
            made = make(i) if make else None
            hi.append(self.act(self.nc.scalar.copy, pair.hi[:, two, :], src[:, two, :], after=(*after[i], made)))
            if i:
                low(i - 1)
        low(tiles // 2 - 1)
        return lo

    def project(self, x, block_src, n_blocks, dst, tile0, after=(), ahead=True, side=None):
        S = self.SLOTS
        self.settle_banks()
        full = n_blocks // S if ahead or n_blocks % S else n_blocks // S - 1

        def block(n, ahead=True, ready=()):
            s = self.load_block(block_src(n))
            if ahead:
                self.split_next()
            self.block_products(s, x, ready)
            self.computed[s].wait(self.act)
            at = n * 2 + tile0
            self.evicted[s].by(self.nc.scalar.copy(
                dst[:, at:at + 2, :] if isinstance(at, int) else dst[:, bass.ds(at, 2), :],
                self.bank[s][:, :].rearrange("p (a n) -> p a n", a=2)))

        if full > 1 and side is None:
            self.pe.wait(*after)
            with rounds(self.nc, full, {c: 1 for c in self.ring}) as j:
                for b in range(S):
                    block(j * S + b)
        else:
            full = 0
        for b in range(full * S, n_blocks):
            block(b, ahead or b < n_blocks - 1, after if b == 0 else ())
            next(side or iter(()), None)
        self.streamed()
        return [self.evicted[s].done() for s in range(S)]

    def project_with(self, x, block_src, evict, after=(), ahead=True, side=None):
        self.settle_banks()
        for b in range(4):
            s = self.load_block(block_src(b))
            if ahead or b < 3:
                self.split_next()
            self.block_products(s, x, after if b == 0 else ())
            evict(b, s)
            next(side or iter(()), None)
        self.streamed()


def finish(steps):
    for _ in steps:
        pass


def columns(w, layer, col):
    if not isinstance(col, int):
        cols = bass.ds(col, 256)
    else:
        cols = slice(col, col + 256)
    return w[bass.ds(layer, 1), :, cols].rearrange("o (k p) c -> p (o k) c", p=P)


def inverse_rms(m, x, tmp, stat, bank, after):
    nc = m.nc
    squares = []
    for i in range(KT // 2):
        two = slice(2 * i, 2 * i + 2)
        s = m.act(nc.scalar.square, tmp[:, two, :], x[:, two, :], after=after[i])
        squares.append(m.dve(nc.vector.tensor_tensor, tmp[:, 2 * i, :], tmp[:, 2 * i, :], tmp[:, 2 * i + 1, :], ALU.add,
                             after=(s,)))
    m.pe.wait(*m.read[bank])
    for i, s in enumerate(squares):
        summed = m.pe(nc.tensor.matmul, m.bank[bank][:, 0:NT], m.ones[:, :], tmp[:, 2 * i, :], start=(i == 0),
                      stop=(i == KT // 2 - 1), after=(s,))
    mean = m.dve(nc.vector.tensor_scalar, stat, m.bank[bank][:, 0:NT], 1.0 / (KT * P), RMS_EPS, ALU.mult, ALU.add,
                 after=(summed,))
    m.read[bank] = [mean]
    inv = m.dve(nc.vector.reciprocal, stat, stat, after=(mean,))
    return m.act(nc.scalar.activation, stat, stat, ACT.Sqrt, after=(inv,))


def scale_two(m, i, x, gain, out, stat, after):
    for k in (2 * i, 2 * i + 1):
        d = m.dve(m.nc.vector.scalar_tensor_tensor, out=out[:, k, :], in0=x[:, k, :], scalar=gain[:, k:k + 1],
                  in1=stat, op0=ALU.mult, op1=ALU.mult, after=after)
    return d


def norm_to_pair(m, x, gain, pair, tmp, stat, bank, after, gain_in=None):
    root = inverse_rms(m, x, tmp, stat, bank, after)
    gain_in = gain_in and gain_in()
    return m.split(tmp, pair, after=[()] * (KT // 2),
                   make=lambda i: scale_two(m, i, x, gain, tmp, stat, (root, gain_in)))


def add_normed(m, x, y, gain, tmp, stat, bank, after):
    root = inverse_rms(m, y, tmp, stat, bank, after)
    out = []
    for i in range(KT // 2):
        two = slice(2 * i, 2 * i + 2)
        d = scale_two(m, i, y, gain, y, stat, (root,))
        q = m.dve if i % 2 else m.pool
        out.append(q(q.eng.tensor_tensor, x[:, two, :], x[:, two, :], y[:, two, :], ALU.add, after=(d,)))
    return [(d,) for d in out]


def ffn(m, h, w_in, w_out, layer, d_ff, gated, silu, y, after=(), ahead=True):
    nc = m.nc
    n = d_ff // 256
    m.settle_banks()
    for b in range(4, 8):
        m.pe.wait(*m.read[b])
    bank2 = [m.bank[s][:, :].rearrange("p (a n) -> p a n", a=2) for s in range(m.SLOTS)]
    used = {}

    def gate(j, ready=()):
        s = used["gate"] = m.load_block(columns(w_in, layer, j * 256))
        m.split_next(m.dve)
        m.block_products(s, h, ready)
        m.computed[s].wait(m.act)
        if "up" in used:
            m.evicted[used["up"]].wait(m.act)
        m.evicted[s].by(nc.scalar.activation(silu[:, :, :], bank2[s], ACT.Silu))

    def up(j):
        s = used["up"] = m.load_block(columns(w_in, layer, j * 256 + d_ff))
        m.split_next(m.dve)
        m.block_products(s, h)
        m.evicted[used["gate"]].wait(m.dve)
        m.computed[s].wait(m.dve)
        m.product.by(nc.vector.tensor_tensor(silu[:, :, :], silu[:, :, :], bank2[s], ALU.mult))
        m.product.wait(m.act)
        if "out" in used:
            m.computed[used["out"]].wait(m.act)
        m.product_hi.by(nc.scalar.copy(gated.hi[:, :, :], silu[:, :, :]))
        m.product_hi.wait(m.dve)
        m.evicted[s].by(nc.vector.tensor_tensor(gated.lo[:, :, :], silu[:, :, :], gated.hi[:, :, :].bitcast(F32),
                                                ALU.subtract))

    def out(j, first=False, last=False):
        rows = w_out[bass.ds(layer, 1), bass.ds(j * 256, 256), :].rearrange("o (k p) c -> p (o k) c", p=P)
        wide = lambda t: t[:, :, :].rearrange("p (k q) c -> p k (q c)", k=2)
        s = used["out"] = m.load_block(rows, lambda s: wide(m.slot[s]))
        if ahead or not last:
            m.split_next(m.dve)
        m.evicted[used["up"]].wait(m.pe)
        for q in range(2):
            m.lo_made[s][q].wait(m.pe)
        hi, lo = wide(m.hi[s]), wide(m.lo[s])
        for k in range(2):
            for t in range(KT):
                to, at = m.bank[4 + t // 2][:, t % 2 * NT:(t % 2 + 1) * NT], slice(t * P, (t + 1) * P)
                nc.tensor.matmul(to, hi[:, k, at], gated.hi[:, k, :], start=(first and k == 0 and t % 2 == 0), stop=False,
                                 skip_group_check=True)
                nc.tensor.matmul(to, hi[:, k, at], gated.lo[:, k, :], start=False, stop=False, skip_group_check=True)
                ins = nc.tensor.matmul(to, lo[:, k, at], gated.hi[:, k, :], start=False, stop=(last and k == 1),
                                       skip_group_check=True)
        m.computed[s].by(ins)

    gate(0, after)
    up(0)
    gate(1)
    out(0, first=True)
    up(1)
    events = {c: 1 for c in [*m.ring, m.product, m.product_hi] if c is not m.evicted[used["out"]]}
    with rounds(nc, n - 2, events) as j:
        gate(j + 2)
        out(j + 1)
        up(j + 2)
    out(n - 1, last=True)
    m.streamed()
    dones = []
    for b in range(4):
        d = m.dve(nc.vector.tensor_copy, y[:, 2 * b:2 * b + 2, :], m.bank[4 + b][:, :].rearrange("p (a n) -> p a n", a=2),
                  after=(m.computed[used["out"]].done(),))
        m.read[4 + b] = [d]
        dones.append((d,))
    return dones


def to_columns(m, rows, n_rows, cols, bank, after=()):
    nc = m.nc
    t = m.pe(nc.tensor.transpose, m.bank[bank][:, 0:n_rows], rows[0:n_rows, :], m.ident[0:n_rows, 0:n_rows],
             after=(*after, *m.read[bank]))
    d = m.dve(nc.vector.tensor_copy, cols, m.bank[bank][:, 0:n_rows], after=(t,))
    m.read[bank] = [d]
    return d


def softplus(m, x, out, a, b, after=()):
    nc = m.nc
    d = m.dve(nc.vector.scalar_tensor_tensor, out=a, in0=x, scalar=-1.0, in1=x, op0=ALU.mult, op1=ALU.max, after=after)
    e = m.act(nc.scalar.activation, a, a, ACT.Exp, scale=-1.0, after=(d,))
    d = m.dve(nc.vector.tensor_scalar, b, a, 2.0, None, ALU.add, after=(e,))
    d = m.dve(nc.vector.reciprocal, b, b, after=(d,))
    z = m.dve(nc.vector.tensor_tensor, a, a, b, ALU.mult, after=(d,))
    d = m.dve(nc.vector.tensor_tensor, b, a, a, ALU.mult, after=(z,))
    d = m.dve(nc.vector.tensor_scalar, out, b, 2.0 / 17, None, ALU.mult, after=(d,))
    for k in range(7, 0, -1):
        d = m.dve(nc.vector.scalar_tensor_tensor, out=out, in0=out, scalar=2.0 / (2 * k + 1), in1=b,
                  op0=ALU.add, op1=ALU.mult, after=(d,))
    d = m.dve(nc.vector.scalar_tensor_tensor, out=out, in0=out, scalar=2.0, in1=a, op0=ALU.add, op1=ALU.mult, after=(d,))
    return m.dve(nc.vector.scalar_tensor_tensor, out=out, in0=x, scalar=0.0, in1=out, op0=ALU.max, op1=ALU.add, after=(d,))


def make_constants(m):
    nc = m.nc
    m.ones = m.sb("ones", [P, P])
    m.ident = m.sb("ident", [P, P])
    m.upto = m.sb("mask_s_le_t", [P, P])
    m.from_ = m.sb("mask_s_ge_t", [P, P])
    m.level = m.sb("level_masks", [P, 7, P])
    m.onehot = m.sb("onehot_columns", [P, 16, 16])
    m.pick = m.sb("row_pickers", [16, 16, P])
    xor = m.slot[0][:, 0, 0:P].bitcast(I32)
    srow = m.slot[0][:, 0, P:2 * P].bitcast(I32)
    tmp = m.slot[0][:, 1, 0:P].bitcast(I32)
    ones = m.pool(nc.gpsimd.memset, m.ones[:, :], 1.0)
    big = m.pool(nc.gpsimd.memset, m.onehot[:, :, :], 1.0)
    big2 = m.pool(nc.gpsimd.memset, m.pick[:, :, :], 1.0)
    out = [
        m.pool(nc.gpsimd.affine_select, out=m.ident[:, :], in_=m.ones[:, :], compare_op=ALU.is_equal, fill=0.0,
               base=0, pattern=[[-1, P]], channel_multiplier=1, after=(ones,)),
        m.pool(nc.gpsimd.affine_select, out=m.upto[:, :], in_=m.ones[:, :], compare_op=ALU.is_ge, fill=0.0,
               base=0, pattern=[[1, P]], channel_multiplier=-1),
        m.pool(nc.gpsimd.affine_select, out=m.from_[:, :], in_=m.ones[:, :], compare_op=ALU.is_ge, fill=0.0,
               base=0, pattern=[[-1, P]], channel_multiplier=1),
        m.pool(nc.gpsimd.affine_select, out=m.onehot[:, :, :], in_=m.onehot[:, :, :], compare_op=ALU.is_equal, fill=0.0,
               base=0, pattern=[[1, 16], [-1, 16]], channel_multiplier=0, after=(big,)),
        m.pool(nc.gpsimd.affine_select, out=m.pick[:, :, :], in_=m.pick[:, :, :], compare_op=ALU.is_equal, fill=0.0,
               base=0, pattern=[[-1, 16], [0, P]], channel_multiplier=1, after=(big2,)),
    ]
    s = m.pool(nc.gpsimd.iota, xor, pattern=[[1, P]], base=0, channel_multiplier=0)
    t = m.pool(nc.gpsimd.iota, srow, pattern=[[0, P]], base=0, channel_multiplier=1)
    x = m.dve(nc.vector.tensor_tensor, xor, xor, srow, ALU.bitwise_xor, after=(s, t))
    d = None
    for l in range(7):
        d = m.dve(nc.vector.tensor_scalar, tmp, xor, l, None, ALU.logical_shift_right, after=(x, d))
        d = m.dve(nc.vector.tensor_scalar, m.level[:, l, :], tmp, 1.0, None, ALU.is_equal, after=(d,))
        d = m.dve(nc.vector.tensor_tensor, m.level[:, l, :], m.level[:, l, :], m.upto[:, :], ALU.mult, after=(d, out[1]))
    return out + [d]


class Layer:

    GLU_A, GLU_G, QKV, Z, GATES, TILES = 0, 8, 16, 40, 48, 64
    NORMS = ["ffn1_norm_pre", "ffn1_norm_post", "mix_norm_pre", "mix_norm_post", "ffn2_norm_pre", "ffn2_norm_post",
             "cnv_dw_b", "cnv_ln_g", "cnv_ln_b", "cnv_b_o"]

    def __init__(self, m):
        sb = m.sb
        self.x, self.y = (sb(n, [P, KT, NT]) for n in ("residual", "branch"))
        self.stat = sb("stat", [P, NT])
        self.proj = sb("proj", [P, self.TILES, NT])
        conv_at = m.next_address()
        self.conv = sb("gdn_conv", [P, 24, NT])
        at = lambda name, tile: m.nc.alloc_sbuf_tensor_at(name, [P, KT, NT], F32R, offset=conv_at + tile * NT * 4)
        self.operand = m.pair("operand", KT)
        self.operand2 = Pair(at("operand2_hi", 8), at("operand2_lo", 16))
        self.silu = sb("ffn_silu", [P, 2, NT])
        self.gated = m.pair("ffn_gated", 2)
        self.rows = sb("param_rows", [P, 4, P])
        self.cols = sb("param_cols", [P, 97])
        self.gdn_w = sb("gdn_conv_cols", [P, 4 * 24])
        self.dw_w = sb("cnv_dw_cols", [P, 31 * KT])
        self.w_ab = sb("w_beta_a", [P, KT, 16])
        self.head = sb("head_params", [8, 4])
        self.hrow = sb("head_rows", [8, 6, NT])
        self.tok = sb("token_cols", [P, 2, 4, 8])
        self.q2 = [sb(f"q_decayed{g}", [P, 4, P]) for g in range(2)]
        self.norm16 = sb("row_norms", [16, NT])
        eight = lambda t, a: t[:, a:a + 4, :].rearrange("p a (b n) -> p (a b) n", b=2)
        hi, lo = self.operand.plain
        names = ["D", "A", "KB", "T", "TT", "QK", "VB", "KX"]
        homes = [[(self.proj, 4 * i) for i in range(8)],
                 [(self.proj, 32), (self.proj, 36), (hi, 0), (hi, 4), (lo, 0), (lo, 4), (self.y, 0), (self.y, 4)]]
        self.delta = [{n: eight(*at) for n, at in zip(names, home)} for home in homes]


def load_layer_params(m, L, io, l):
    nc = m.nc
    one = lambda a: a[bass.ds(l, 1), :].rearrange("o (k c) -> (o k) c", c=P)
    sp = nc.sync
    m.params_in.by(sp.dma_start(L.w_ab[:, :, :], io["mix_w_in"][bass.ds(l, 1), :, 4096:4112].rearrange(
        "o (k p) c -> p (o k) c", p=P)))
    for i, name in enumerate(L.NORMS):
        m.params_in.by(sp.dma_start(L.rows[8 * i:8 * i + 8, 0, :], one(io[name])))
    m.params_in.by(sp.dma_start(L.rows[80:96, 0, :], one(io["cnv_pw1_b"])))
    m.params_in.by(sp.dma_start(L.rows[96:97, 0, :], one(io["gdn_norm_w"])))
    m.params_in.by(sp.dma_start(L.rows[0:96, 1, :], io["gdn_conv_w"][bass.ds(l, 1), :, :].rearrange(
        "o t (k c) -> (o t k) c", c=P)))
    for i, (a, b) in enumerate(((0, 16), (16, 31))):
        m.params_in.by(sp.dma_start(L.rows[0:(b - a) * KT, 2 + i, :], io["cnv_dw_w"][bass.ds(l, 1), a:b, :].rearrange(
            "o t (k c) -> (o t k) c", c=P)))
    m.params_in.by(sp.dma_start(L.head[:, 0:1], io["gdn_a_log"][bass.ds(l, 1), :].rearrange("o h -> h o")))
    m.params_in.by(sp.dma_start(L.head[:, 1:2], io["gdn_dt_bias"][bass.ds(l, 1), :].rearrange("o h -> h o")))


def turn_layer_params(m, L):
    nc = m.nc
    m.split_next()
    there = m.params_in.done()
    d = [to_columns(m, L.rows[:, 0, :], 97, L.cols[:, :], 4, after=(there,)),
         to_columns(m, L.rows[:, 1, :], 96, L.gdn_w[:, :], 5, after=(there,)),
         to_columns(m, L.rows[:, 2, :], 128, L.dw_w[:, 0:128], 6, after=(there,)),
         to_columns(m, L.rows[:, 3, :], 120, L.dw_w[:, 128:248], 7, after=(there,))]
    d.append(m.dve(nc.vector.tensor_scalar, L.cols[:, 8:16], L.cols[:, 8:16], 0.5, None, ALU.mult, after=(d[0],)))
    d.append(m.dve(nc.vector.tensor_scalar, L.cols[:, 40:48], L.cols[:, 40:48], 0.5, None, ALU.mult, after=(d[0],)))
    return d[-1]


def depthwise(m, last, src, dst, weight, taps, centre, tiles, bias=None, after=(), piece=None):
    nc, n = m.nc, 0
    order = [centre] + [k for k in range(taps) if k != centre]
    for k in order:
        s = k - centre
        for c in tiles:
            if piece and n and n % piece == 0:
                yield
            n += 1
            w = weight(k, c)
            if k == centre:
                if bias is None:
                    last[c] = m.dve(nc.vector.tensor_scalar, dst(c), src(c), w, None, ALU.mult, after=after)
                else:
                    last[c] = m.dve(nc.vector.tensor_scalar, dst(c), src(c), w, bias(c), ALU.mult, ALU.add, after=after)
                continue
            to, frm = (slice(-s, NT), slice(0, NT + s)) if s < 0 else (slice(0, NT - s), slice(s, NT))
            last[c] = m.dve(nc.vector.scalar_tensor_tensor, out=dst(c)[:, to], in0=src(c)[:, frm], scalar=w,
                            in1=dst(c)[:, to], op0=ALU.mult, op1=ALU.add, after=(last[c],))


def head_sums(m, squares, n_rows, out, bank, eps, scale=1.0, per_row=1, after=()):
    nc = m.nc
    steps = []
    n = n_rows * per_row
    for i in range(n):
        steps.append((m.bank[bank][0:n_rows, 0:NT], m.onehot[:, i // per_row, 0:n_rows], squares(i), i == 0, i == n - 1))
    s = m.matmuls(steps, after=after, bank=bank)
    d = m.dve(nc.vector.tensor_scalar, out, m.bank[bank][0:n_rows, 0:NT], scale, eps, ALU.mult, ALU.add, after=(s,))
    m.read[bank] = [d]
    d = m.dve(nc.vector.reciprocal, out, out, after=(d,))
    return m.act(nc.scalar.activation, out, out, ACT.Sqrt, after=(d,))


def spread_row(m, bank, half, rows, n_rows, j, after=()):
    return m.matmuls([(m.bank[bank][:, half * NT:(half + 1) * NT], m.pick[0:n_rows, j, :], rows, True, True)],
                     after=after, bank=bank)


def conformer(m, L, glu_in):
    nc = m.nc
    proj = L.proj
    for k in range(KT):
        s = m.act(nc.scalar.activation, proj[:, L.GLU_G + k, :], proj[:, L.GLU_G + k, :], ACT.Sigmoid,
                  bias=L.cols[:, 88 + k:89 + k], after=glu_in)
        d = m.dve(nc.vector.scalar_tensor_tensor, out=proj[:, L.GLU_G + k, :], in0=proj[:, L.GLU_A + k, :],
                  scalar=L.cols[:, 80 + k:81 + k], in1=proj[:, L.GLU_G + k, :], op0=ALU.add, op1=ALU.mult, after=(s,))
    done = {}
    finish(depthwise(m, done, lambda c: proj[:, L.GLU_G + c, :], lambda c: proj[:, L.GLU_A + c, :],
                     lambda k, c: L.dw_w[:, 8 * k + c:8 * k + c + 1], 31, 30, range(KT),
                     bias=lambda c: L.cols[:, 48 + c:49 + c], after=(d,)))
    return done


def conformer_norm(m, L, conv_done, bank, out):
    nc = m.nc
    last = [conv_done[c] for c in range(KT)]
    glu, tmp = (L.proj[:, t:t + KT, :] for t in (L.GLU_A, L.GLU_G))
    halves = [slice(0, 4), slice(4, 8)]
    wide = lambda a: a.unsqueeze(1).to_broadcast([P, 4, NT])
    s = m.matmuls([(m.bank[bank][:, 0:NT], m.ones[:, :], glu[:, k, :], k == 0, k == KT - 1) for k in range(KT)],
                  after=last, bank=bank)
    mean = m.act(nc.scalar.mul, L.stat[:, :], m.bank[bank][:, 0:NT], 1.0 / (KT * P), after=(s,))
    m.read[bank] = [mean]
    centred = [m.dve(nc.vector.tensor_tensor, glu[:, f, :], glu[:, f, :], wide(L.stat[:, :]), ALU.subtract, after=(mean,))
               for f in halves]
    yield
    sq = []
    for f, c in zip(halves, centred):
        sq.append(m.act(nc.scalar.square, tmp[:, f, :], glu[:, f, :], after=(c,)))
        yield
    s = m.matmuls([(m.bank[bank][:, 0:NT], m.ones[:, :], tmp[:, k, :], k == 0, k == KT - 1) for k in range(KT)],
                  after=sq, bank=bank)
    v = m.dve(nc.vector.tensor_scalar, L.stat[:, :], m.bank[bank][:, 0:NT], 1.0 / (KT * P), LN_EPS, ALU.mult, ALU.add, after=(s,))
    m.read[bank] = [v]
    v = m.dve(nc.vector.reciprocal, L.stat[:, :], L.stat[:, :], after=(v,))
    yield
    v = m.act(nc.scalar.activation, L.stat[:, :], L.stat[:, :], ACT.Sqrt, after=(v,))
    scaled = [m.dve(nc.vector.tensor_tensor, glu[:, f, :], glu[:, f, :], wide(L.stat[:, :]), ALU.mult, after=(v,))
              for f in halves]
    yield
    for i in range(4):
        out.append([m.act(nc.scalar.activation, glu[:, k, :], glu[:, k, :], ACT.Silu, bias=L.cols[:, 64 + k:65 + k],
                          scale=L.cols[:, 56 + k:57 + k], after=(scaled[i // 2],)) for k in (2 * i, 2 * i + 1)])
        if i % 2:
            yield


def head_scalars(m, L, h, after):
    nc = m.nc
    hrow, head, b = L.hrow, L.head, 4
    m.pe.wait(m.params_in.done(), *m.read[b])
    for i in range(2):
        for k in range(KT):
            m.pe.wait(after[k // 2])
            s = m.pe(nc.tensor.matmul, m.bank[b][0:8, i * NT:(i + 1) * NT], L.w_ab[:, k, 8 * i:8 * i + 8], h[:, k, :],
                     start=(k == 0), stop=(k == KT - 1))
    beta = m.act(nc.scalar.activation, hrow[:, 0, :], m.bank[b][0:8, 0:NT], ACT.Sigmoid, after=(s,))
    e = m.act(nc.scalar.activation, head[:, 2:3], head[:, 0:1], ACT.Exp, after=(m.params_in.done(),))
    a = m.dve(nc.vector.tensor_scalar, hrow[:, 3, :], m.bank[b][0:8, NT:2 * NT], head[:, 1:2], None, ALU.add, after=(beta,))
    m.read[b] = [beta, a]
    sp = softplus(m, hrow[:, 3, :], hrow[:, 1, :], hrow[:, 4, :], hrow[:, 5, :], after=(a,))
    g = m.dve(nc.vector.tensor_scalar, hrow[:, 1, :], hrow[:, 1, :], head[:, 2:3], -1.0, ALU.mult, ALU.mult, after=(sp, e))
    one = m.dve(nc.vector.memset, hrow[:, 4, :], 1.0, after=(sp,))
    for c in range(2):
        at = slice(c * P, (c + 1) * P)
        G = m.dve(nc.vector.tensor_tensor_scan, hrow[:, 2, at], hrow[:, 4, at], hrow[:, 1, at], 0.0, ALU.mult, ALU.add,
                  after=(g, one))
    return beta, G


def scalars_by_token(m, L, beta, G):
    nc = m.nc
    hrow, b = L.hrow, 5
    m.pe.wait(*m.read[b])
    for c in range(2):
        for i, r in enumerate((0, 2)):
            t = m.pe(nc.tensor.transpose, m.bank[b][:, (2 * c + i) * 8:(2 * c + i) * 8 + 8],
                     hrow[:, r, c * P:(c + 1) * P], m.ident[0:8, 0:8], after=(G, beta))
    cp = m.dve(nc.vector.tensor_copy, L.tok[:, :, 0:2, :],
               m.bank[b][:, 0:32].rearrange("p (c i h) -> p c i h", c=2, i=2), after=(t,))
    m.read[b] = [cp]
    x = m.act(nc.scalar.activation, L.tok[:, 1, 3, :], L.tok[:, 1, 1, :], ACT.Exp, after=(cp,))
    d = m.dve(nc.vector.tensor_tensor, L.tok[:, 1, 2, :], L.tok[:, 1, 0, :], L.tok[:, 1, 3, :], ALU.mult, after=(x,))
    return d


def delta_inputs(m, L, taps_done, silu, sq):
    nc, conv, proj = m.nc, L.conv, L.proj
    for i in range(6):
        four = slice(4 * i, 4 * i + 4)
        silu.append(m.act(nc.scalar.activation, conv[:, four, :], conv[:, four, :], ACT.Silu,
                          after=[taps_done[c] for c in range(4 * i, 4 * i + 4)]))
        if i < 4:
            sq.append(m.act(nc.scalar.square, proj[:, L.QKV + 4 * i:L.QKV + 4 * i + 4, :], conv[:, four, :],
                            after=(silu[i], taps_done[23])))
        yield


def delta_rule(m, L, silu, sq, row_G, tok_cols, projected):
    nc = m.nc
    conv, proj, tok = L.conv, L.proj, L.tok
    n = head_sums(m, lambda i: proj[:, L.QKV + i, :], 16, L.norm16[:, :], 6, 1e-6, after=sq)
    kv = {}
    for i in range(8):
        b = i % 4
        for half in range(2):
            s = spread_row(m, b, half, L.norm16[:, :], 16, 2 * i + half, after=(n,) if half == 0 else ())
        two = slice(2 * i, 2 * i + 2)
        kv[i] = m.dve(nc.vector.scalar_tensor_tensor, out=conv[:, two, :], in0=conv[:, two, :],
                      scalar=P ** -0.5 if i < 4 else 1.0,
                      in1=m.bank[b][:, :].rearrange("p (a n) -> p a n", a=2), op0=ALU.mult, op1=ALU.mult, after=(s,))
        m.read[b] = [kv[i]]
    qk_ready = [kv[7], silu[5], *sq, *projected]

    buf = L.delta
    m4 = lambda b: m.bank[b][:, :].rearrange("p (h n) -> p h n", h=4)
    ch = lambda t, c: t[:, 4 * c:4 * c + 4, :]
    head = lambda i, g: slice(8 * i + 4 * g, 8 * i + 4 * g + 4)
    D = [{} for _ in range(2)]

    for g in range(2):
        B, r = buf[g], D[g]
        b0 = 4 * g
        for i in range(4):
            s = spread_row(m, b0 + i // 2, i % 2, L.hrow[:, 2, :], 8, 4 * g + i, after=(row_G, *qk_ready))
            s2 = spread_row(m, b0 + 2 + i // 2, i % 2, L.hrow[:, 0, :], 8, 4 * g + i)
        for i in range(4):
            h = 4 * g + i
            G = m.bank[b0 + i // 2][:, (i % 2) * NT:(i % 2 + 1) * NT]
            for c in range(2):
                dd = m.dve(nc.vector.tensor_scalar, B["D"][:, 4 * c + i, :], G[:, c * P:(c + 1) * P],
                           tok[:, c, 1, h:h + 1], 0.0, ALU.subtract, ALU.min, after=(s, tok_cols))
            dl = m.dve(nc.vector.tensor_tensor, tok[:, 0, 2, h:h + 1], G[:, P - 1:P], tok[:, 0, 1, h:h + 1], ALU.subtract)
        for i in range(4):
            G = m.bank[b0 + i // 2][:, (i % 2) * NT:(i % 2 + 1) * NT]
            ge = m.act(nc.scalar.activation, L.q2[g][:, i, :], G[:, P:2 * P], ACT.Exp, after=(dl,))
        r["end"] = m.act(nc.scalar.activation, tok[:, 0, 3, 4 * g:4 * g + 4], tok[:, 0, 2, 4 * g:4 * g + 4], ACT.Exp, after=(dl,))
        r["E"] = m.act(nc.scalar.activation, B["D"], B["D"], ACT.Exp, after=(dd,))
        for i in range(2):
            kb = m.dve(nc.vector.tensor_tensor, B["KB"].rearrange("p (h c) n -> p h (c n)", c=2)[:, 2 * i:2 * i + 2, :],
                       conv[:, 8 + 4 * g + 2 * i:8 + 4 * g + 2 * i + 2, :],
                       m.bank[b0 + 2 + i][:, :].rearrange("p (a n) -> p a n", a=2), ALU.mult, after=(s2,))
        r["q2"] = m.dve(nc.vector.tensor_tensor, L.q2[g][:, :, :], L.q2[g][:, :, :], conv[:, head(0, g), P:2 * P], ALU.mult, after=(ge,))
        r["D"] = m.dve(nc.vector.tensor_tensor, B["D"], B["D"], m.upto[:, :].unsqueeze(1).to_broadcast([P, 8, P]),
                       ALU.mult, after=(r["E"],))
        r["kb"] = kb
        for i in range(4):
            m.read[b0 + i] = [dd, ge, dl, kb]

    for g in range(2):
        B, r, b0 = buf[g], D[g], 4 * g
        KB = B["KB"].rearrange("p (h c) n -> p h c n", c=2)
        for c in range(2):
            steps = [(m4(b0 + c)[:, i, :], conv[:, 8 + 4 * g + i, c * P:(c + 1) * P], KB[:, i, c, :], True, True) for i in range(4)]
            a = m.matmuls(steps, after=(r["kb"],), bank=b0 + c)
            steps = [(m4(b0 + 2 + c)[:, i, :], conv[:, 8 + 4 * g + i, c * P:(c + 1) * P],
                      conv[:, 4 * g + i, c * P:(c + 1) * P], True, True) for i in range(4)]
            q = m.matmuls(steps, bank=b0 + 2 + c)
            r["A", c] = m.dve(nc.vector.tensor_tensor, ch(B["A"], c), m4(b0 + c), ch(B["D"], c), ALU.mult, after=(a, r["D"]))
            r["QK", c] = m.dve(nc.vector.tensor_tensor, ch(B["QK"], c), m4(b0 + 2 + c), ch(B["D"], c), ALU.mult, after=(q,))
            m.read[b0 + c] = [r["A", c]]
            m.read[b0 + 2 + c] = [r["QK", c]]

    for g in range(2):
        B, r, b0 = buf[g], D[g], 4 * g
        for c in range(2):
            for i, what in ((2, 0), (1, 2)):
                b = b0 + c + what
                m.pe.wait(*m.read[b])
                for j in range(4):
                    t = m.pe(nc.tensor.transpose, m4(b)[:, j, :], conv[:, 8 * i + 4 * g + j, c * P:(c + 1) * P], m.ident[:, :])
                for j in range(4):
                    h = 4 * g + j
                    if i == 2:
                        dst, f = B["VB"], tok[:, c, 0, h:h + 1]
                    else:
                        dst, f = B["KX"], tok[:, c, 3 if c == 0 else 2, h:h + 1]
                    cp = m.act(nc.scalar.activation, dst[:, 4 * c + j, :], m4(b)[:, j, :], ACT.Copy, scale=f,
                               after=(t, r["end"], tok_cols))
                m.read[b] = [cp]
        r["tok"] = cp

    eye = m.ident[:, :].unsqueeze(1).to_broadcast([P, 4, P])
    for l in range(7):
        mask = m.level[:, l, :].unsqueeze(1).to_broadcast([P, 4, P])
        for g in range(2):
            B, r, b0 = buf[g], D[g], 4 * g
            for c in range(2):
                r["L", c] = m.dve(nc.vector.tensor_tensor, ch(B["KB"], c), ch(B["A"], c), mask, ALU.mult,
                                  after=(r["A", 1], r.get(("M", c)), r.get(("TT", c))))
        for g in range(2):
            B, r, b0 = buf[g], D[g], 4 * g
            for c in range(2):
                pr = range(4 * c, 4 * c + 4)
                mm = m.matmuls([(m4(b0 + c)[:, p % 4, :], B["KB"][:, p, :], m.ident[:, :] if l == 0 else B["T"][:, p, :],
                                 True, True) for p in pr], after=(r["L", c], r.get(("T", c))), bank=b0 + c)
                if l == 0:
                    r["T", c] = m.dve(nc.vector.tensor_tensor, ch(B["T"], c), eye, m4(b0 + c), ALU.subtract, after=(mm,))
                    r["TT", c] = m.dve(nc.vector.tensor_tensor, ch(B["TT"], c), eye, ch(B["KB"], c), ALU.subtract,
                                       after=(r["L", c],))
                    m.read[b0 + c] = [r["T", c]]
                    r["M", c] = mm
                    continue
                cp = m.act(nc.scalar.copy, ch(B["D"], c), m4(b0 + c), after=(mm, r["QK", c], r.get(("TTp", c))))
                m.read[b0 + c] = [cp]
                r["M", c], r["Mc", c] = mm, cp
        if l == 0:
            continue
        for g in range(2):
            B, r, b0 = buf[g], D[g], 4 * g
            for c in range(2):
                pr = range(4 * c, 4 * c + 4)
                if l < 6:
                    r["Tp", c] = m.matmuls([(m4(b0 + 2 + c)[:, p % 4, :], B["TT"][:, p, :], B["D"][:, p, :], True, True)
                                            for p in pr], after=(r["Mc", c], r["TT", c]), bank=b0 + 2 + c)
                r["TTp", c] = m.matmuls([(m4(b0 + c)[:, p % 4, :], B["D"][:, p, :], B["TT"][:, p, :], True, True)
                                         for p in pr], after=(r["Mc", c], r["TT", c]), bank=b0 + c)
                if l < 6:
                    r["T", c] = m.dve(nc.vector.tensor_tensor, ch(B["T"], c), ch(B["T"], c), m4(b0 + 2 + c), ALU.subtract,
                                      after=(r["Tp", c],))
                    m.read[b0 + 2 + c] = [r["T", c]]
                r["TT", c] = m.dve(nc.vector.tensor_tensor, ch(B["TT"], c), ch(B["TT"], c), m4(b0 + c), ALU.subtract,
                                   after=(r["TTp", c],))
                m.read[b0 + c] = [r["TT", c]]

    done = []
    for g in range(2):
        B, r, b0 = buf[g], D[g], 4 * g
        W, S, V = B["T"][:, 0:4, :], B["T"][:, 4:8, :], B["A"]
        r["v0p"] = m.matmuls([(m4(b0)[:, i, :], B["TT"][:, i, :], B["VB"][:, i, :], True, True) for i in range(4)],
                             after=(r["TT", 0], r["tok"]), bank=b0)
        wp = m.matmuls([(m4(b0 + 1)[:, i, :], B["KX"][:, 4 + i, :], B["TT"][:, 4 + i, :], True, True) for i in range(4)],
                       after=(r["TT", 1],), bank=b0 + 1)
        r["v0"] = m.act(nc.scalar.copy, V[:, 0:4, :], m4(b0), after=(r["v0p"],))
        r["w"] = m.act(nc.scalar.mul, W, m4(b0 + 1), -1.0, after=(wp,))
        m.read[b0], m.read[b0 + 1] = [r["v0"]], [r["w"]]
    for g in range(2):
        B, r, b0 = buf[g], D[g], 4 * g
        W, S, V = B["T"][:, 0:4, :], B["T"][:, 4:8, :], B["A"]
        s = m.matmuls([(m4(b0 + 2)[:, i, :], B["KX"][:, i, :], V[:, i, :], True, True) for i in range(4)],
                      after=(r["v0"],), bank=b0 + 2)
        r["S"] = m.act(nc.scalar.copy, S, m4(b0 + 2), after=(s,))
        m.read[b0 + 2] = [r["S"]]
    for g in range(2):
        B, r, b0 = buf[g], D[g], 4 * g
        W, S, V = B["T"][:, 0:4, :], B["T"][:, 4:8, :], B["A"]
        steps = []
        for i in range(4):
            steps.append((m4(b0 + 3)[:, i, :], B["TT"][:, 4 + i, :], B["VB"][:, 4 + i, :], True, False))
            steps.append((m4(b0 + 3)[:, i, :], W[:, i, :], S[:, i, :], False, True))
        v = m.matmuls(steps, after=(r["S"], r["w"]), bank=b0 + 3)
        r["v1"] = m.act(nc.scalar.copy, V[:, 4:8, :], m4(b0 + 3), after=(v,))
        m.read[b0 + 3] = [r["v1"]]
    for g in range(2):
        B, r, b0 = buf[g], D[g], 4 * g
        W, S, V = B["T"][:, 0:4, :], B["T"][:, 4:8, :], B["A"]
        o0 = m.matmuls([(m4(b0)[:, i, :], V[:, i, :], B["QK"][:, i, :], True, True) for i in range(4)], bank=b0)
        steps = []
        for i in range(4):
            steps.append((m4(b0 + 1)[:, i, :], S[:, i, :], L.q2[g][:, i, :], True, False))
            steps.append((m4(b0 + 1)[:, i, :], V[:, 4 + i, :], B["QK"][:, 4 + i, :], False, True))
        o1 = m.matmuls(steps, after=(r["v1"], r["q2"]), bank=b0 + 1)
        c0 = m.act(nc.scalar.copy, conv[:, head(0, g), 0:P], m4(b0), after=(o0,))
        c1 = m.act(nc.scalar.copy, conv[:, head(0, g), P:NT], m4(b0 + 1), after=(o1,))
        m.read[b0], m.read[b0 + 1] = [c0], [c1]
        done += [c0, c1]

    sq = m.act(nc.scalar.square, conv[:, 8:16, :], conv[:, 0:8, :], after=done)
    n = head_sums(m, lambda i: conv[:, 8 + i, :], 8, L.norm16[0:8, :], 2, RMS_EPS, scale=1.0 / P, after=(sq,))
    z = m.act(nc.scalar.activation, proj[:, L.Z:L.Z + 8, :], proj[:, L.Z:L.Z + 8, :], ACT.Silu)
    out = []
    for i in range(4):
        for half in range(2):
            s = spread_row(m, 4 + i, half, L.norm16[0:8, :], 8, 2 * i + half, after=(n,))
        two = slice(2 * i, 2 * i + 2)
        d = m.dve(nc.vector.scalar_tensor_tensor, out=conv[:, two, :], in0=conv[:, two, :], scalar=L.cols[:, 96:97],
                  in1=m.bank[4 + i][:, :].rearrange("p (a n) -> p a n", a=2), op0=ALU.mult, op1=ALU.mult, after=(s,))
        m.read[4 + i] = [d]
        out.append(m.dve(nc.vector.tensor_tensor, conv[:, two, :], conv[:, two, :], proj[:, L.Z + 2 * i:L.Z + 2 * i + 2, :],
                         ALU.mult, after=(d, z)))
    return out


def mixer(m, L, io, l, normed):
    nc = m.nc
    w = io["mix_w_in"]
    proj, conv = L.proj, L.conv
    x = L.operand
    beta, G = head_scalars(m, L, L.y, normed)
    glu_in = m.project(x, lambda b: columns(w, l, b * 256 + 4112), 8, proj, L.GLU_A, after=normed)
    tok_cols = scalars_by_token(m, L, beta, G)
    conv_done = conformer(m, L, glu_in)
    qkv_in = m.project(x, lambda b: columns(w, l, b * 256), 12, proj, L.QKV)
    m.project(x, lambda b: columns(w, l, b * 256 + 3072), 4, proj, L.Z)
    conf, taps_done, silu, sq = [], {}, [], []
    side = zip_longest(conformer_norm(m, L, conv_done, 7, conf),
                 depthwise(m, taps_done, lambda c: proj[:, L.QKV + c, :], lambda c: conv[:, c, :],
                           lambda k, c: L.gdn_w[:, 24 * k + c:24 * k + c + 1], 4, 3, range(24), after=qkv_in, piece=16))
    gates_in = m.project(x, lambda b: columns(w, l, b * 256 + 6160), 8, proj, L.GATES, side=side)
    finish(side)
    gate = [m.act(nc.scalar.activation, proj[:, t:t + 8, :], proj[:, t:t + 8, :], ACT.Sigmoid, after=gates_in)
            for t in (L.GATES + 8, L.GATES)]

    two = lambda t, b: t[:, 2 * b:2 * b + 2, :]
    bank2 = lambda s: m.bank[s][:, :].rearrange("p (a n) -> p a n", a=2)
    branch = {}

    def evict_conf(b, s):
        m.computed[s].wait(m.dve)
        m.dve.wait(*gate)
        for i in range(2):
            t = 2 * b + i
            ins = nc.vector.scalar_tensor_tensor(out=proj[:, L.GATES + 8 + t, :],
                                                 in0=m.bank[s][:, i * NT:(i + 1) * NT], scalar=L.cols[:, 72 + t:73 + t],
                                                 in1=proj[:, L.GATES + 8 + t, :], op0=ALU.add, op1=ALU.mult)
        m.evicted[s].by(ins)

    def evict_gdn(b, s):
        m.computed[s].wait(m.dve)
        m.evicted[s].by(nc.vector.tensor_tensor(two(L.y, b), bank2(s), proj[:, L.GATES + 2 * b:L.GATES + 2 * b + 2, :],
                                                ALU.mult))
        branch[b] = m.dve(nc.vector.tensor_tensor, two(L.y, b), two(L.y, b),
                          proj[:, L.GATES + 8 + 2 * b:L.GATES + 10 + 2 * b, :], ALU.add, after=(m.evicted[s].done(),))

    def evict_out(b, s):
        m.computed[s].wait(m.act)
        m.evicted[s].by(nc.scalar.copy(two(L.y, b), bank2(s)))
        branch["out", b] = m.evicted[s].done()

    side = delta_inputs(m, L, taps_done, silu, sq)
    conf = m.split(proj[:, L.GLU_A:L.GLU_A + 8, :], x, after=conf)
    m.project_with(x, lambda b: columns(io["cnv_w_o"], l, b * 256), evict_conf, after=conf,
                   side=side)
    finish(side)
    o = delta_rule(m, L, silu, sq, G, tok_cols, gates_in)
    o = m.split(conv, L.operand2, after=[(o[i],) for i in range(4)])
    m.project_with(L.operand2, lambda b: columns(io["gdn_w_o"], l, b * 256), evict_gdn, after=o)
    y = m.split(L.y, x, after=[(branch[b],) for b in range(4)])
    m.project_with(x, lambda b: columns(io["mix_w_out"], l, b * 256), evict_out, after=y)
    return [(branch["out", b],) for b in range(4)]


def layer(m, L, io, l):
    d_ff = io["ffn1_w_out"].shape[1]
    g = lambda i: L.cols[:, 8 * i:8 * i + 8]
    stat, scratch = L.stat[:, :], L.operand.plain[0]
    load_layer_params(m, L, io, l)
    n = norm_to_pair(m, L.x, g(0), L.operand, L.y, stat, 3, after=[()] * 4, gain_in=lambda: turn_layer_params(m, L))
    y = ffn(m, L.operand, io["ffn1_w_in"], io["ffn1_w_out"], l, d_ff, L.gated, L.silu, L.y, after=n)
    d = add_normed(m, L.x, L.y, g(1), scratch, stat, 3, after=y)
    n = norm_to_pair(m, L.x, g(2), L.operand, L.y, stat, 3, after=d)
    y = mixer(m, L, io, l, n)
    d = add_normed(m, L.x, L.y, g(3), scratch, stat, 3, after=y)
    n = norm_to_pair(m, L.x, g(4), L.operand, L.y, stat, 3, after=d)
    y = ffn(m, L.operand, io["ffn2_w_in"], io["ffn2_w_out"], l, d_ff, L.gated, L.silu, L.y, after=n, ahead=False)
    return add_normed(m, L.x, L.y, g(5), scratch, stat, 3, after=y)


def turn_in(m, x, rows, bank0=0, after=()):
    nc = m.nc
    out = []
    for k in range(KT):
        b = bank0 + k % 4
        m.pe.wait(*m.read[b])
        for t in range(2):
            tr = m.pe(nc.tensor.transpose, m.bank[b][:, t * P:(t + 1) * P], rows[:, t, k * P:(k + 1) * P], m.ident[:, :],
                      after=after)
        c = m.act(nc.scalar.copy, x[:, k, :], m.bank[b][:, 0:NT], after=(tr,))
        m.read[b] = [c]
        out.append(c)
    return out


def turn_out(m, rows, x, bank0=0, after=()):
    nc = m.nc
    out = []
    for t in range(2):
        for half in range(2):
            b = bank0 + 2 * t + half
            m.pe.wait(*m.read[b])
            for k in range(4):
                tr = m.pe(nc.tensor.transpose, m.bank[b][:, k * P:(k + 1) * P], x[:, 4 * half + k, t * P:(t + 1) * P],
                          m.ident[:, :], after=after)
            c = m.act(nc.scalar.copy, rows[:, t, half * 512:half * 512 + 512], m.bank[b][:, :], after=(tr,))
            m.read[b] = [c]
            out.append(c)
    return out


class Block:

    XM, O, XL, LRU_GATE, MERGE, LRU_X, LRU_F = 0, 8, 16, 24, 32, 48, 56

    def __init__(self, m, L):
        self.L = L
        sb = m.sb
        self.bias = sb("gate_bias", [4, 4])
        self.rows = L.hrow[0:4, :, :]
        self.cum = L.q2[0][0:4, :, :].rearrange("p a n -> p (a n)").rearrange("p (d n) -> p d n", d=2)
        self.lru_w = [L.proj[:, t:t + 8, :].rearrange("p a n -> p (a n)").rearrange("p (j e) -> p j e", e=P)
                      for t in (self.MERGE, self.MERGE + 8)]
        self.c_cols = sb("c_by_token", [P, 2, 2, 4])
        self.lam = sb("lru_decay", [P, 2, 16])


def load_block_params(m, L, B, io):
    nc = m.nc
    sp = nc.sync
    rows = lambda a: a[0:1].rearrange("o (k c) -> (o k) c", c=P) if len(a.shape) == 2 else a[0:1].rearrange("o t (k c) -> (o t k) c", c=P)
    for i, group in enumerate((("norm1_g_2", "mlstm_conv_w_2", "mlstm_conv_b_2", "mlstm_norm_g_2", "lru_conv_w_2",
                                "lru_conv_b_2", "norm2_g_2"), ("lru_b_r_2", "lru_b_i_2", "lru_lambda_2"))):
        at = 0
        for name in group:
            r = rows(io[name])
            m.params_in.by(sp.dma_start(L.rows[at:at + r.shape[0], i, :], r))
            at += r.shape[0]
    m.params_in.by(sp.dma_start(L.w_ab[:, :, :], io["w_in_2"][0:1, :, 2048:2064].rearrange("o (k p) c -> p (o k) c", p=P)))
    for k in range(4):
        m.params_in.by(sp.dma_start(B.bias[:, k:k + 1], io["b_gates_2"][0:1, 4 * k:4 * k + 4].rearrange("o h -> h o")))


def turn_block_params(m, L):
    m.split_next()
    there = m.params_in.done()
    return [to_columns(m, L.rows[:, 0, :], 104, L.dw_w[:, 0:104], 4, after=(there,)),
            to_columns(m, L.rows[:, 1, :], 48, L.dw_w[:, 104:152], 5, after=(there,))]


def mlstm_gates(m, L, B, normed):
    nc = m.nc
    R = B.rows
    h = L.y
    for d in range(2):
        m.pe.wait(m.params_in.done(), *m.read[4 + d])
        for i in range(2):
            for k in range(KT):
                m.pe.wait(normed[k // 2])
                s = m.pe(nc.tensor.matmul, m.bank[4 + d][0:4, i * NT:(i + 1) * NT],
                         L.w_ab[:, k, 8 * d + 4 * i:8 * d + 4 * i + 4], h[:, k, :], start=(k == 0), stop=(k == KT - 1))
        x = m.dve(nc.vector.tensor_scalar, R[:, d, :], m.bank[4 + d][0:4, NT:2 * NT], B.bias[:, 2 * d + 1:2 * d + 2], -1.0,
                  ALU.add, ALU.mult, after=(s,))
    sp = softplus(m, R[:, 0:2, :], R[:, 2:4, :], R[:, 4:6, :], B.cum, after=(x,))
    one = m.dve(nc.vector.memset, R[:, 4:6, :], 1.0, after=(sp,))
    rev = lambda a, d: a if d == 0 else a[:, ::-1]
    for d in range(2):
        b = m.dve(nc.vector.tensor_tensor_scan, rev(B.cum[:, d, :], d), rev(R[:, 4 + d, :], d), rev(R[:, 2 + d, :], d), 0.0,
                  ALU.mult, ALU.subtract, after=(one,))
        c = m.dve(nc.vector.scalar_tensor_tensor, out=R[:, d, :], in0=m.bank[4 + d][0:4, 0:NT], scalar=B.bias[:, 2 * d:2 * d + 1],
                  in1=B.cum[:, d, :], op0=ALU.add, op1=ALU.subtract, after=(b,))
        m.read[4 + d] = [c]
        M = m.dve(nc.vector.tensor_tensor_scan, rev(R[:, 4 + d, :], d), rev(R[:, d, :], d), rev(R[:, d, :], d), 0.0,
                  ALU.max, ALU.max, after=(c,))
        m_row = m.dve(nc.vector.tensor_tensor, R[:, 2 + d, :], B.cum[:, d, :], R[:, 4 + d, :], ALU.add, after=(M,))
    return M, m_row


def gates_by_token(m, B, M, m_row):
    nc, R, bk = m.nc, B.rows, 6
    em = m.act(nc.scalar.activation, R[:, 2:4, :], R[:, 2:4, :], ACT.Exp, scale=-1.0, after=(m_row,))
    m.pe.wait(*m.read[bk])
    for d in range(2):
        for t in range(2):
            tr = m.pe(nc.tensor.transpose, m.bank[bk][:, (2 * d + t) * 4:(2 * d + t) * 4 + 4], R[:, d, t * P:(t + 1) * P],
                      m.ident[0:4, 0:4], after=(M,))
    cp = m.dve(nc.vector.tensor_copy, B.c_cols[:, :, :, :], m.bank[bk][:, 0:16].rearrange("p (d t h) -> p d t h", d=2, t=2),
               after=(tr,))
    m.read[bk] = [cp]
    return [M, em, cp]


def head_block(io, name):
    return io[name][0].rearrange("h (k p) e -> p (h k) e", p=P)


def mlstm(m, L, B, io, projected, taps, gates):
    nc = m.nc
    proj, conv = L.proj, L.conv
    xc = m.act(nc.scalar.activation, conv[:, 0:8, :], conv[:, 0:8, :], ACT.Silu, after=[taps[c] for c in range(8)])
    values = L.operand.plain[1][:, :, :].rearrange("p a n -> p (a n)").rearrange("p (t e) -> p t e", t=2)
    bank2 = lambda b: m.bank[b][:, :].rearrange("p (a n) -> p a n", a=2)
    ready = []
    sv = m.load_block(head_block(io, "mlstm_w_v_2"))
    sq = m.load_block(head_block(io, "mlstm_w_q_2"))
    sk = m.load_block(head_block(io, "mlstm_w_k_2"))
    m.loaded[sv].wait(m.pe)
    for h in range(4):
        p = m.matmuls([(m.bank[h][:, t * NT:(t + 1) * NT], proj[:, B.XM + 2 * h + k, t * P:(t + 1) * P],
                        m.slot[sv][:, 2 * h + k, :], k == 0, k == 1) for t in range(2) for k in range(2)],
                      after=projected, bank=h)
        c = m.act(nc.scalar.copy, values[:, :, h * NT:(h + 1) * NT], bank2(h), after=(p,))
        m.read[h] = [c]
        ready.append(c)
    m.release(sv, p)
    for s, at in ((sq, 8), (sk, 16)):
        m.loaded[s].wait(m.pe)
        for h in range(4):
            b = h if at == 8 else 4 + h
            p = m.matmuls([(m.bank[b][:, e * NT:(e + 1) * NT], m.slot[s][:, 2 * h + k, e * P:(e + 1) * P], conv[:, 2 * h + k, :],
                            k == 0, k == 1) for e in range(2) for k in range(2)], after=(xc,), bank=b)
            c = m.act(nc.scalar.copy, conv[:, at + 2 * h:at + 2 * h + 2, :], bank2(b), after=(p,))
            m.read[b] = [c]
            ready.append(c)
        m.release(s, p)

    H = L.operand.plain[0]
    E = lambda d, h: L.y[:, 4 * (h % 2) + 2 * d:4 * (h % 2) + 2 * d + 2, :]
    den = [L.silu, L.gated.plain[0]]
    used, wrote, first, weighed, scored = {}, {}, {}, {}, {}
    spans = [[slice(0, NT), slice(P, NT)], [slice(0, P), slice(0, NT)]]

    def weigh(h, d):
        sb, e, span = h % 2, E(d, h), spans[d]
        if d == 0:
            scored[h] = m.matmuls([(m.bank[sb][:, t * NT:(t + 1) * NT], conv[:, 16 + 2 * h + e, t * P:(t + 1) * P],
                                    conv[:, 8 + 2 * h + e, :], e == 0, e == 1) for t in range(2) for e in range(2)],
                                  after=ready, bank=sb)
        ms = m.matmuls([(m.bank[2 + d][:, 0:NT], m.pick[0:4, h, :], B.rows[:, 4 + d, :], True, True),
                        (m.bank[2 + d][:, NT:2 * NT], m.pick[0:4, h, :], B.rows[:, 2 + d, :], True, True)],
                       after=gates, bank=2 + d)
        for t in range(2):
            w = m.dve(nc.vector.tensor_scalar, e[:, t, span[t]], m.bank[2 + d][:, span[t]], B.c_cols[:, d, t, h:h + 1], 0.0,
                      ALU.subtract, ALU.max, after=(ms, *gates, used.get((d, sb))))
        for t in range(2):
            x = m.act(nc.scalar.activation, e[:, t, span[t]], e[:, t, span[t]], ACT.Exp, scale=-1.0, after=(w,))
        for t in range(2):
            diag = slice(t * P, (t + 1) * P)
            k = m.dve(nc.vector.tensor_tensor, e[:, t, diag], e[:, t, diag], (m.upto if d == 0 else m.from_)[:, :],
                      ALU.mult, after=(x,))
        for t in range(2):
            weighed[h, d] = m.dve(nc.vector.scalar_tensor_tensor, out=e[:, t, span[t]],
                                  in0=m.bank[sb][:, t * NT + span[t].start:t * NT + span[t].stop],
                                  scalar=NT ** -0.5, in1=e[:, t, span[t]], op0=ALU.mult, op1=ALU.mult, after=(k, scored[h]))
        m.read[sb] = [weighed[h, d]]

    def gather(h, d):
        sb, e, span = h % 2, E(d, h), spans[d]
        order = (0, 1) if d == 0 else (1, 0)
        dn = m.matmuls([(m.bank[4 + d][:, span[t]], m.ones[:, :], e[:, t, span[t]], i == 0, i == 1)
                        for i, t in enumerate(order)], after=(weighed[h, d],), bank=4 + d)
        nm = m.matmuls([(m.bank[6 + d][:, v * NT + span[t].start:v * NT + span[t].stop],
                         values[:, t, h * NT + v * P:h * NT + (v + 1) * P], e[:, t, span[t]], i == 0, i == 1)
                        for v in range(2) for i, t in enumerate(order)], bank=6 + d)
        used[d, sb] = nm
        r = den[d][:, 0, :]
        a = m.act(nc.scalar.activation, r, m.bank[4 + d][:, 0:NT], ACT.Abs, after=(dn, wrote.get(d)))
        m.read[4 + d] = [a]
        a = m.dve(nc.vector.tensor_tensor, r, r, m.bank[2 + d][:, NT:2 * NT], ALU.max, after=(a,))
        m.read[2 + d] = [a]
        a = m.dve(nc.vector.reciprocal, r, r, after=(a,))
        rr = r.unsqueeze(1).to_broadcast([P, 2, NT])
        Hh = H[:, 2 * h:2 * h + 2, :]
        if d == 0:
            a = m.dve(nc.vector.tensor_tensor, Hh, bank2(6), rr, ALU.mult, after=(a, nm))
            m.read[6] = [a]
            first[h] = a
        else:
            a = m.dve(nc.vector.tensor_tensor, e, bank2(7), rr, ALU.mult, after=(a, nm))
            m.read[7] = [a]
            a = m.dve(nc.vector.tensor_tensor, Hh, Hh, e, ALU.add, after=(a, first[h]))
            used[d, sb] = a
        wrote[d] = a
        return a

    order = [(h, d) for h in range(4) for d in range(2)]
    weigh(*order[0])
    for this, ahead in zip(order, [*order[1:], None]):
        if ahead:
            weigh(*ahead)
        a = gather(*this)
    sg = m.act(nc.scalar.activation, proj[:, B.O:B.O + 8, :], proj[:, B.O:B.O + 8, :], ACT.Sigmoid, after=projected)
    sq = m.act(nc.scalar.square, L.y[:, :, :], H[:, :, :], after=(a,))
    n = head_sums(m, lambda i: L.y[:, i, :], 4, L.norm16[0:4, :], 0, RMS_EPS, scale=1.0 / NT, per_row=2, after=(sq,))
    out = []
    for h in range(4):
        s = spread_row(m, 1 + h, 0, L.norm16[0:4, :], 4, h, after=(n,))
        for v in range(2):
            t = 2 * h + v
            a = m.dve(nc.vector.scalar_tensor_tensor, out=H[:, t, :], in0=H[:, t, :], scalar=L.dw_w[:, 48 + t:49 + t],
                      in1=m.bank[1 + h][:, 0:NT], op0=ALU.mult, op1=ALU.mult, after=(s,))
            out.append(m.dve(nc.vector.tensor_tensor, H[:, t, :], H[:, t, :], proj[:, B.O + t, :], ALU.mult, after=(a, sg)))
        m.read[1 + h] = [a]
    return out


def lru_decay(m, L, B):
    nc = m.nc
    ng = m.dve(nc.vector.tensor_scalar, B.lam[:, 0, :], L.dw_w[:, 104 + 32:104 + 48], -1.0, None, ALU.mult)
    sp = softplus(m, B.lam[:, 0, :], B.lam[:, 1, :], L.cols[:, 0:16], L.cols[:, 16:32], after=(ng,))
    pos = m.dve(nc.vector.tensor_scalar, B.lam[:, 1, :], B.lam[:, 1, :], 8.0, None, ALU.mult, after=(sp,))
    return m.dve(nc.vector.tensor_scalar, B.lam[:, 0, :], B.lam[:, 1, :], -1.0, None, ALU.mult, after=(pos,))


def rg_lru(m, L, B, taps, decay, weights_in, gate_in, out):
    nc = m.nc
    proj, conv = L.proj, L.conv
    X = proj[:, B.LRU_X:B.LRU_X + 8, :]
    R, I, T, A2 = conv[:, 0:8, :], conv[:, 8:16, :], conv[:, 16:24, :], L.y
    free = []
    yield
    yield
    for d in range(2):
        gated, th, aa = {}, {}, {}
        for pair in range(4):
            s = {}
            for i, w in enumerate(B.lru_w):
                b = 3 + 2 * i + pair % 2
                s[i] = m.matmuls([(m.bank[b][:, q * NT:(q + 1) * NT], w[:, 8 * d + 2 * pair + q, :], X[:, 2 * pair + q, :],
                                   True, True) for q in range(2)], after=(taps[2 * pair + 1], weights_in), bank=b)
            yield
            for i, (dst, bias) in enumerate(((R, 104), (I, 120))):
                b = 3 + 2 * i + pair % 2
                for q in range(2):
                    n = 2 * pair + q
                    at = bias + 8 * d + n
                    gated[i, n] = m.act(nc.scalar.activation, dst[:, n, :], m.bank[b][:, q * NT:(q + 1) * NT], ACT.Sigmoid,
                                        bias=L.dw_w[:, at:at + 1], after=(s[i], *free))
                m.read[b] = [gated[i, n]]
        for n in range(8):
            th[n] = m.act(nc.scalar.activation, T[:, n, :], R[:, n, :], ACT.Tanh, scale=B.lam[:, 1, 8 * d + n:8 * d + n + 1],
                          after=(gated[0, n], decay))
            aa[n] = m.act(nc.scalar.activation, R[:, n, :], R[:, n, :], ACT.Exp, scale=B.lam[:, 0, 8 * d + n:8 * d + n + 1],
                          after=(th[n],))
            if n % 4 < 3:
                continue
            f = slice(n - 3, n + 1)
            ix = m.dve(nc.vector.tensor_tensor, I[:, f, :], I[:, f, :], X[:, f, :], ALU.mult, after=(gated[1, n],))
            q = m.dve(nc.vector.tensor_tensor, A2[:, f, :], R[:, f, :], R[:, f, :], ALU.mult, after=(aa[n], *free))
            q = m.dve(nc.vector.scalar_tensor_tensor, out=T[:, f, :], in0=A2[:, f, :], scalar=1.0, in1=T[:, f, :], op0=ALU.add,
                      op1=ALU.mult, after=(q,))
            yield
            q = m.act(nc.scalar.activation, T[:, f, :], T[:, f, :], ACT.Sqrt, after=(q,))
            q = m.dve(nc.vector.tensor_tensor, T[:, f, :], T[:, f, :], I[:, f, :], ALU.mult, after=(q, ix))
            for k in range(n - 3, n + 1):
                if d == 0:
                    sc = m.dve(nc.vector.tensor_tensor_scan, proj[:, B.LRU_F + k, :], R[:, k, :], T[:, k, :], 0.0, ALU.mult,
                               ALU.add, after=(q,))
                else:
                    sc = m.dve(nc.vector.tensor_tensor_scan, A2[:, k, ::-1], R[:, k, ::-1], T[:, k, ::-1], 0.0, ALU.mult,
                               ALU.add, after=(q,))
        free = [sc]
    gate = proj[:, B.LRU_GATE:B.LRU_GATE + 8, :]
    gl = m.act(nc.scalar.activation, gate, gate, ACT.Gelu, after=gate_in)
    F = proj[:, B.LRU_F:B.LRU_F + 8, :]
    a = m.dve(nc.vector.tensor_tensor, F, F, A2[:, :, :], ALU.add, after=(sc,))
    out.append(m.dve(nc.vector.tensor_tensor, F, F, gate, ALU.mult, after=(a, gl)))


def merge(m, L, B, io, y_m, y_l, gates):
    nc = m.nc
    two = lambda t, b: t[:, 2 * b:2 * b + 2, :]
    bank2 = lambda s: m.bank[s][:, :].rearrange("p (a n) -> p a n", a=2)
    F = L.proj[:, B.LRU_F:B.LRU_F + 8, :]
    merge_m, merge_l = (L.proj[:, t:t + 8, :] for t in (B.MERGE, B.MERGE + 8))
    g = m.act(nc.scalar.activation, L.proj[:, B.MERGE:B.MERGE + 16, :], L.proj[:, B.MERGE:B.MERGE + 16, :], ACT.Sigmoid, after=gates)
    done = {}

    def evict_m(b, s):
        m.computed[s].wait(m.dve)
        m.dve.wait(g)
        m.evicted[s].by(nc.vector.tensor_tensor(two(merge_m, b), bank2(s), two(merge_m, b), ALU.mult))
        done["m", b] = m.evicted[s].done()

    def evict_l(b, s):
        m.computed[s].wait(m.dve)
        m.evicted[s].by(nc.vector.tensor_tensor(two(L.y, b), bank2(s), two(merge_l, b), ALU.mult))
        done["l", b] = m.dve(nc.vector.tensor_tensor, two(L.y, b), two(L.y, b), two(merge_m, b), ALU.add,
                             after=(m.evicted[s].done(), done["m", b]))

    def evict_out(b, s):
        m.computed[s].wait(m.dve)
        m.evicted[s].by(nc.vector.tensor_tensor(two(L.x, b), two(L.x, b), bank2(s), ALU.add))
        done["x", b] = m.evicted[s].done()

    m.split_next()
    y_m = m.split(L.operand.plain[0], L.operand2, after=[(*y_m, *y_l)] * 4)
    y_l = m.split(F, L.operand, after=[(y_m[-1],)] * 4)
    m.project_with(L.operand2, lambda b: columns(io["w_branch_mlstm_2"], 0, b * 256), evict_m, after=y_m)
    m.project_with(L.operand, lambda b: columns(io["w_branch_lru_2"], 0, b * 256), evict_l, after=y_l)
    y = m.split(L.y, L.operand2, after=[(done["l", b],) for b in range(4)])
    m.project_with(L.operand2, lambda b: columns(io["w_out_2"], 0, b * 256), evict_out, after=y)
    return [(done["x", b],) for b in range(4)]


class Peer:

    HEADS, TOP, KEYS, GROUP = 8, 16, 128, 8
    STEPS = 32

    def __init__(self, m, L):
        flat = lambda t: t.rearrange("p a n -> p (a n)")
        G = self.GROUP
        self.u = m.nc.alloc_sbuf_tensor_at("expert_u_rows", [P, G, KT * P], F32, offset=m.slots_at)
        v = flat(L.proj[:, :, :]).rearrange("p (s d) -> p s d", s=2 * G)
        self.v = [v[:, p * G:(p + 1) * G, :] for p in range(2)]
        self.gain = flat(m.slot[2][:, 0:4, :])
        self.keys = flat(L.operand.plain[0][:, :, :]).rearrange("p (j n) -> p j n", n=P)
        self.h_tok, self.x_tok = (flat(a[:, :, :]).rearrange("p (t d) -> p t d", t=2) for a in L.operand.plain)
        diag = flat(L.x[:, :, :]).rearrange("p (s n) -> p s n", n=P)
        self.diag = [diag[:, p * G:(p + 1) * G, :] for p in range(2)]
        self.scores = flat(L.conv[:, 0:17, :]).rearrange("p (j n) -> p j n", n=P)
        self.lists = flat(L.conv[:, 17:18, :]).rearrange("p (j n) -> p j n", n=P)
        self.pairs = L.conv[:, 18, :]
        self.match = L.conv[:, 19, :].rearrange("p (a b) -> p a b", a=16)
        tables, at = flat(L.conv[:, 20:22, :]), [0]

        def table(n, dt=F32):
            at[0] += n
            t = tables[:, at[0] - n:at[0]]
            return t if dt == F32 else t.bitcast(dt)

        two = lambda t: t.rearrange("p (s k) -> p s k", s=2)
        self.top, self.top_i, self.top_f = two(table(32)), two(table(32, U32)), two(table(32))
        self.best, self.pos = table(16), table(16, U32)
        self.half, self.half_i, self.row = ([table(16, dt) for _ in range(2)] for dt in (F32, U32, F32))
        self.index, self.gate = ([table(16, dt) for _ in range(2)] for dt in (U32, F32))
        self.sum, self.inv = table(1), table(1)
        self.counting, self.counting_i = table(16), table(16, I32)
        self.dots, self.acts, self.weights = ([table(G) for _ in range(2)] for _ in range(3))
        self.ss = table(4)


class PeerCounts:
    def __init__(self, m):
        c = lambda name, unit=1: Count(m.nc, name, unit)
        G = Peer.GROUP
        self.u_in = [c(f"u_in{s}", 16) for s in range(G)]
        self.u_used = [c(f"u_used{s}") for s in range(G)]
        self.v_in = [[c(f"v_in{p}_{s}", 16) for s in range(G)] for p in range(2)]
        self.v_used = [[c(f"v_used{p}_{s}") for s in range(G)] for p in range(2)]
        self.slot_free, self.turn = c("gather_slot_free"), c("choose_turn")
        self.step, self.exp, self.chosen = c("choose_step"), c("softmax_exp"), c("head_chosen")
        self.gelu, self.weighed, self.diag, self.added = (c(n) for n in ("gelu", "weighed", "diag", "added"))
        self.per_round = {c: 4 for c in [*self.u_in, *self.u_used, self.gelu, self.weighed, self.diag, self.added]}
        self.per_round.update({c: 2 for c in [*sum(self.v_in, []), *sum(self.v_used, []), self.exp, self.chosen]})
        self.per_round[self.step] = 2 * Peer.STEPS

    def prime(self, m):
        for c in [*self.u_used, self.step, self.gelu, self.weighed]:
            c.by(m.prime(m.nc.vector))
        for c in [*sum(self.v_used, []), self.diag]:
            c.by(m.prime(m.nc.tensor))


def choose_experts(m, K, C, n, parity):
    nc, v = m.nc, m.nc.vector

    def step(ins, *args, alone=True, **kw):
        if alone:
            C.step.wait(m.dve)
            if ins in (v.max, v.max_index, v.match_replace):
                v.sem_inc(C.turn.sem, 1)
        C.step.by(ins(*args, **kw))

    def best16(lists, top, top_i):
        for at in (0, 8):
            for j, x in enumerate(lists):
                step(v.max, top[j][:, at:at + 8], x, alone=j == 0)
            for j, x in enumerate(lists):
                step(v.max_index, top_i[j][:, at:at + 8], top[j][:, at:at + 8], x, alone=j == 0)
            if at == 0:
                for j, x in enumerate(lists):
                    step(v.match_replace, x, top[j][:, 0:8], x, LOWEST, alone=j == 0)

    step(v.tensor_copy, K.lists, K.scores[:, bass.ds(n * 2, 2), :])
    best16([K.lists[:, s, :] for s in range(2)], [K.top[:, s, :] for s in range(2)], [K.top_i[:, s, :] for s in range(2)])
    rows = lambda a: a.unsqueeze(2).to_broadcast([P, 16, 16])
    cols = lambda a: a.unsqueeze(1).to_broadcast([P, 16, 16])
    step(v.tensor_copy, K.top_f, K.top_i)
    step(v.tensor_tensor, K.pairs.rearrange("p (a b) -> p a b", a=16), rows(K.top[:, 0, :]), cols(K.top[:, 1, :]), ALU.add,
         alone=False)
    best16([K.pairs], [K.best], [K.pos])
    for i, (op, by) in enumerate(((ALU.logical_shift_right, 4), (ALU.bitwise_and, 15))):
        step(v.tensor_scalar, K.half_i[i], K.pos, by, None, op, alone=i == 0)
    for i in range(2):
        step(v.tensor_copy, K.half[i], K.half_i[i], alone=i == 0)
    for i in range(2):
        step(v.tensor_tensor, K.match, rows(K.half[i]), cols(K.counting), ALU.is_equal)
        step(v.tensor_tensor, K.match, K.match, cols(K.top_f[:, i, :]), ALU.mult)
        step(v.tensor_reduce, K.row[i], K.match, AX.X, ALU.add)
    step(v.scalar_tensor_tensor, out=K.row[0], in0=K.row[0], scalar=float(K.KEYS), in1=K.row[1], op0=ALU.mult, op1=ALU.add)
    C.step.wait(m.dve)
    C.chosen.by(v.tensor_copy(K.index[parity], K.row[0]))
    step(v.tensor_scalar, K.gate[parity], K.best, K.best[:, 0:1], None, ALU.subtract, alone=False)
    C.step.wait(m.act)
    C.exp.by(nc.scalar.activation(K.gate[parity], K.gate[parity], ACT.Exp, accum_out=K.sum))
    C.exp.wait(m.dve)
    step(v.reciprocal, K.inv, K.sum, alone=False)
    step(v.tensor_scalar, K.gate[parity], K.gate[parity], K.inv, None, ALU.mult)


def add_group(m, K, C, t, p):
    x = K.x_tok[:, t, :]
    C.v_used[p][-1].wait(m.dve)
    C.added.wait(m.dve)
    for half in range(2):
        at = slice(half * 512, half * 512 + 512)
        ins = m.nc.vector.tensor_tensor(x[:, at], x[:, at], m.bank[2 * p + half][:, :], ALU.add)
    C.added.by(ins)


def run_group(m, K, io, C, t, parity, p):
    nc = m.nc
    G = K.GROUP
    first = p * G
    for table, rows, arrived, used in ((io["peer_u_2"][0], K.u, C.u_in, C.u_used),
                                       (io["peer_v_2"][0], K.v[p], C.v_in[p], C.v_used[p])):
        for s in range(G):
            used[s].wait(m.pool)
            nc.gpsimd.sem_inc(C.slot_free.sem, 1)
            arrived[s].by(nc.gpsimd.indirect_dma_start(
                out=rows[:, s, :], out_offset=None, in_=table,
                in_offset=bass.IndirectOffsetOnAxis(ap=K.index[parity][:, first + s:first + s + 1], axis=0)))
    for s in range(G):
        C.u_in[s].wait(m.dve)
        C.u_used[s].by(nc.vector.tensor_tensor_reduce(out=K.u[:, s, :], in0=K.u[:, s, :], in1=K.h_tok[:, t, :], scale=1.0,
                                                      scalar=0.0, op0=ALU.mult, op1=ALU.add, accum_out=K.dots[p][:, s:s + 1]))
    C.u_used[-1].wait(m.act)
    C.weighed.wait(m.act)
    C.gelu.by(nc.scalar.activation(K.acts[p], K.dots[p], ACT.Gelu))
    C.gelu.wait(m.dve)
    C.diag.wait(m.dve)
    C.step.wait(m.dve)
    C.weighed.by(nc.vector.tensor_tensor(K.weights[p], K.acts[p], K.gate[parity][:, first:first + G], ALU.mult))
    C.weighed.wait(m.act)
    C.v_used[p][-1].wait(m.act)
    for s in range(G):
        ins = nc.scalar.activation(K.diag[p][:, s, :], m.ident[:, :], ACT.Copy, scale=K.weights[p][:, s:s + 1])
    C.diag.by(ins)
    C.diag.wait(m.pe)
    C.added.wait(m.pe)
    for s in range(G):
        C.v_in[p][s].wait(m.pe)
        for half in range(2):
            ins = nc.tensor.matmul(m.bank[2 * p + half][:, :], K.diag[p][:, s, :], K.v[p][:, s, half * 512:half * 512 + 512],
                                   start=(s == 0), stop=(s == G - 1))
        C.v_used[p][s].by(ins)
    add_group(m, K, C, t, 1 - p)


def run_experts(m, K, io, t, C):
    for half in range(2):
        ins = m.nc.vector.memset(m.bank[2 + half][:, :], 0.0)
    C.added.by(ins)
    with rounds(m.nc, K.HEADS // 2, C.per_round) as j:
        for parity in range(2):
            C.chosen.wait(m.pool)
            run_group(m, K, io, C, t, parity, 0)
            choose_experts(m, K, C, j * 2 + (t * K.HEADS + parity + 1), 1 - parity)
            run_group(m, K, io, C, t, parity, 1)
    add_group(m, K, C, t, 1)
    C.added.wait(m.dve)


def peer(m, L, io, C, x_done, h2):
    nc = m.nc
    K = Peer(m, L)
    q_in = m.project(L.operand, lambda b: columns(io["peer_w_q_2"], 0, b * 256), 8, L.proj, 0, after=h2, ahead=False)
    view = lambda s: m.slot[s][:, :, :].rearrange("p k c -> p (k c)").rearrange("p (j e) -> p j e", e=P)
    sk = m.load_block(io["peer_sub_keys_2"][0].rearrange("h s n c -> n (h s) c"), view)
    m.loaded[sk].wait(m.pe)
    four = lambda b: m.bank[b][:, :].rearrange("p (j n) -> p j n", j=4)
    keys = []
    for i in range(4):
        m.pe.wait(*m.read[i])
        for j in range(4):
            tr = m.pe(nc.tensor.transpose, m.bank[i][:, j * P:(j + 1) * P], view(sk)[:, 4 * i + j, :], m.ident[:, :])
        c = m.act(nc.scalar.copy, K.keys[:, 4 * i:4 * i + 4, :], four(i), after=(tr,))
        m.read[i] = [c]
        keys.append(c)
    scored = [m.dve(nc.vector.memset, K.scores[:, 32:34, :], 0.0, after=keys)]
    for t in range(2):
        for i in range(4):
            b = 4 * t + i
            s = m.matmuls([(m.bank[b][:, j * P:(j + 1) * P], L.proj[:, 4 * i + j, t * P:(t + 1) * P], K.keys[:, 4 * i + j, :], True, True)
                           for j in range(4)], after=(*q_in, *keys), bank=b)
            c = m.act(nc.scalar.copy, K.scores[:, 16 * t + 4 * i:16 * t + 4 * i + 4, :], four(b), after=(s,))
            m.read[b] = [c]
            scored.append(c)
    i = m.pool(nc.gpsimd.iota, K.counting_i, pattern=[[1, 16]], base=0, channel_multiplier=0, after=q_in)
    i = m.dve(nc.vector.tensor_copy, K.counting, K.counting_i, after=(i,))
    C.prime(m)
    m.dve.wait(*scored[:2], i)
    choose_experts(m, K, C, 0, 0)
    ht = turn_out(m, K.h_tok, L.y, 4, after=(*h2, s))
    xt = turn_out(m, K.x_tok, L.x, 4, after=[x_done])
    m.sp.wait(s)
    m.misc_in.by(nc.sync.dma_start(K.gain, io["final_norm_g_2"].unsqueeze(0).to_broadcast([P, KT * P])))
    gain = m.misc_in.done()
    m.pool.wait(s, *keys)
    m.dve.wait(*scored, *xt, *ht)
    for t in range(2):
        run_experts(m, K, io, t, C)
    a = C.added.done()
    for t in range(2):
        x = K.x_tok[:, t, :]
        ss, r = K.ss[:, 2 * t:2 * t + 1], K.ss[:, 2 * t + 1:2 * t + 2]
        q = m.act(nc.scalar.activation, K.h_tok[:, t, :], x, ACT.Square, accum_out=ss, after=(a,))
        q = m.dve(nc.vector.tensor_scalar, r, ss, 1.0 / (KT * P), RMS_EPS, ALU.mult, ALU.add, after=(q,))
        q = m.dve(nc.vector.reciprocal, r, r, after=(q,))
        q = m.act(nc.scalar.activation, r, r, ACT.Sqrt, after=(q,))
        q = m.dve(nc.vector.scalar_tensor_tensor, out=x, in0=x, scalar=r, in1=K.gain, op0=ALU.mult, op1=ALU.mult, after=(q, gain))
        m.sp.wait(q)
        m.misc_in.by(nc.sync.dma_start(io["out"][0, t * P:(t + 1) * P, :], x))
    m.sp.wait(m.misc_in.done())


def last_block(m, L, B, io, C):
    nc = m.nc
    load_block_params(m, L, B, io)
    n = norm_to_pair(m, L.x, L.dw_w[:, 0:8], L.operand, L.y, L.stat[:, :], 3, after=[()] * 4, gain_in=lambda: turn_block_params(m, L))
    w = io["w_in_2"]
    M, m_row = mlstm_gates(m, L, B, n)
    xl_in = m.project(L.operand, lambda b: columns(w, 0, b * 256 + 2064), 4, L.proj, B.XL, after=n)
    for lru_w, name in zip(B.lru_w, ("lru_w_r_2", "lru_w_i_2")):
        m.misc_in.by(nc.sync.dma_start(lru_w, io[name][0].rearrange("d n c e -> c (d n) e")))
    gates = gates_by_token(m, B, M, m_row)
    decay = lru_decay(m, L, B)
    taps, taps_m, y_l = {}, {}, []
    finish(depthwise(m, taps, lambda c: L.proj[:, B.XL + c, :], lambda c: L.proj[:, B.LRU_X + c, :],
                     lambda k, c: L.dw_w[:, 56 + 8 * k + c:57 + 8 * k + c], 4, 2, range(KT),
                     bias=lambda c: L.dw_w[:, 88 + c:89 + c], after=xl_in))
    gate_in = []
    side = rg_lru(m, L, B, taps, decay, m.misc_in.done(), gate_in, y_l)
    gate_in += m.project(L.operand, lambda b: columns(w, 0, b * 256 + 3088), 4, L.proj, B.LRU_GATE, side=side)
    first = m.project(L.operand, lambda b: columns(w, 0, b * 256), 8, L.proj, B.XM, side=side)
    rest = m.project(L.operand, lambda b: columns(w, 0, b * 256 + 4112), 8, L.proj, B.MERGE, ahead=False, side=side)
    finish(side)
    finish(depthwise(m, taps_m, lambda c: L.proj[:, B.XM + c, :], lambda c: L.conv[:, c, :],
                     lambda k, c: L.dw_w[:, 8 + 8 * k + c:9 + 8 * k + c], 4, 2, range(KT),
                     bias=lambda c: L.dw_w[:, 40 + c:41 + c], after=(*first, *y_l)))
    y_m = mlstm(m, L, B, io, (*first, *rest), taps_m, gates)
    x = merge(m, L, B, io, y_m, y_l, rest)
    h2 = norm_to_pair(m, L.x, L.dw_w[:, 96:104], L.operand, L.y, L.stat[:, :], 3, after=x)
    peer(m, L, io, C, x, h2)


def program(nc, io):
    m = Machine(nc)
    L = Layer(m)
    B = Block(m, L)
    C = PeerCounts(m)
    m.start_phase()
    made = make_constants(m)
    rows = L.proj[:, 0:8, :].rearrange("p a b -> p (a b)").rearrange("p (t c) -> p t c", t=2)
    m.misc_in.by(nc.sync.dma_start(rows, io["x"][0].rearrange("(t p) c -> p t c", p=P)))
    turn_in(m, L.x, rows, after=(m.misc_in.done(), *made))
    m.end_phase()
    with nc.Fori(0, io["ffn1_w_in"].shape[0]) as l:
        m.start_phase()
        layer(m, L, io, l)
        m.end_phase()
    m.start_phase()
    last_block(m, L, B, io, C)


def kernel(**inputs):
    import concourse.bacc as bacc
    from concourse.bass_utils import run_bass_kernel_spmd

    nc = bacc.Bacc("TRN2", target_bir_lowering=False, num_devices=1)
    arrays, io = {}, {}
    for name, value in inputs.items():
        a = np.ascontiguousarray(value)
        arrays[f"in_{name}"] = a
        io[name] = nc.dram_tensor(f"in_{name}", a.shape, mybir.dt.from_np(a.dtype), kind="ExternalInput").ap()
    io["out"] = nc.dram_tensor("out_x", inputs["x"].shape, F32, kind="ExternalOutput").ap()
    program(nc, io)
    return run_bass_kernel_spmd(nc, [arrays], core_ids=[0]).results[0]["out_x"]
```
